# Optimizing a Trainium2 kernel written in Bass

```python
import math
import jax, jax.numpy as jnp
from jax import lax
import numpy as np

D_MODEL = 1024
BATCH = 1
SEQ = 1024
DEPTH = 1

D_CONV = 512
CONV_K = 3
N_HEADS = 8
HEAD_DIM = 64
D_ATTN = N_HEADS * HEAD_DIM
N_IDX_HEADS = 8
IDX_DIM = 64
TOPK_MAX = 256
Q_BLOCK = 128
N_BUCKETS = 32
MAX_EXACT = 16
MAX_DISTANCE = 128
D_FF = -(-8 * D_MODEL // (3 * 256)) * 256
EPS = 1e-6

PROJ_SIZES = (
    D_CONV, D_CONV, D_CONV,
    D_ATTN, HEAD_DIM, HEAD_DIM,
    N_IDX_HEADS * IDX_DIM, IDX_DIM,
    N_IDX_HEADS,
    D_MODEL, D_MODEL,
)
N_PROJ = int(sum(PROJ_SIZES))
PROJ_SPLITS = [int(v) for v in np.cumsum(PROJ_SIZES)[:-1]]


def rms_norm(x, g):
    xf = x.astype(jnp.float32)
    y = xf * lax.rsqrt(jnp.mean(xf * xf, axis=-1, keepdims=True) + EPS)
    return (y * g.astype(jnp.float32)).astype(x.dtype)

def rel_bucket(dist):
    n = jnp.maximum(dist, 0)
    large = MAX_EXACT + (jnp.log(jnp.maximum(n, 1).astype(jnp.float32) / MAX_EXACT)
                         / math.log(MAX_DISTANCE / MAX_EXACT)
                         * (N_BUCKETS - MAX_EXACT)).astype(jnp.int32)
    large = jnp.minimum(large, N_BUCKETS - 1)
    return jnp.where(n < MAX_EXACT, n, large)

def short_conv_mixer(gate_b, gate_c, x_a, conv_w):
    u = gate_c * x_a
    rhs = conv_w[:, None, :].astype(u.dtype)
    y = lax.conv_general_dilated(u, rhs, window_strides=(1,), padding=[(CONV_K - 1, 0)],
                                 dimension_numbers=("NWC", "WIO", "NWC"),
                                 feature_group_count=D_CONV)
    return gate_b * y

def dsa_attention(q, k, v, iq, ik, iw, rel_bias):
    bsz, seq_len = q.shape[0], q.shape[1]
    k_top = min(TOPK_MAX, seq_len // 4)
    n_blk = seq_len // Q_BLOCK
    iw = iw * (N_IDX_HEADS ** -0.5 * IDX_DIM ** -0.5)
    s_pos = jnp.arange(seq_len, dtype=jnp.int32)
    t_blocks = s_pos.reshape(n_blk, Q_BLOCK)

    def to_blocks(a):
        return jnp.moveaxis(a.reshape(bsz, n_blk, Q_BLOCK, *a.shape[2:]), 1, 0)

    gather = jax.vmap(lambda arr, ind: arr[ind])

    def block_fn(args):
        q_b, iq_b, iw_b, t_b = args
        dots = jnp.einsum("bthd,bsd->bths", iq_b, ik)
        score = jnp.einsum("bth,bths->bts", iw_b, jax.nn.relu(dots)).astype(jnp.float32)
        causal = s_pos[None, :] <= t_b[:, None]
        score = jnp.where(causal[None], score, -jnp.inf)
        _, idx = lax.top_k(score, k_top)
        valid = idx <= t_b[None, :, None]
        k_sel = gather(k, idx)
        v_sel = gather(v, idx)
        logits = jnp.einsum("bthd,btkd->bhtk", q_b, k_sel).astype(jnp.float32) * (HEAD_DIM ** -0.5)
        bias = rel_bias[rel_bucket(t_b[None, :, None] - idx)]
        logits = logits + jnp.moveaxis(bias, -1, 1).astype(jnp.float32)
        logits = jnp.where(valid[:, None], logits, -jnp.inf)
        p = jax.nn.softmax(logits, axis=-1).astype(v.dtype)
        o = jnp.einsum("bhtk,btkd->bthd", p, v_sel)
        return o.reshape(bsz, Q_BLOCK, D_ATTN)

    out = lax.map(block_fn, (to_blocks(q), to_blocks(iq), to_blocks(iw), t_blocks))
    return jnp.moveaxis(out, 0, 1).reshape(bsz, seq_len, D_ATTN)

def first_inputs(seed: int = 0) -> dict:
    key = jax.random.key(seed)
    ks = jax.random.split(key, 16)
    f32 = jnp.float32
    nrm = lambda k, shape, scale: jax.random.normal(k, shape, f32) * scale
    return {
        "x": nrm(ks[0], (BATCH, SEQ, D_MODEL), 1.0),
        "g_mix": 1.0 + nrm(ks[1], (DEPTH, D_MODEL), 0.02),
        "w_in": nrm(ks[2], (DEPTH, D_MODEL, N_PROJ), D_MODEL ** -0.5),
        "b_gate": nrm(ks[3], (DEPTH, 2 * D_MODEL), 0.02),
        "conv_w": nrm(ks[4], (DEPTH, CONV_K, D_CONV), CONV_K ** -0.5),
        "w_branch_a": nrm(ks[5], (DEPTH, D_CONV, D_MODEL), D_CONV ** -0.5),
        "w_branch_b": nrm(ks[6], (DEPTH, D_ATTN, D_MODEL), D_ATTN ** -0.5),
        "w_out": nrm(ks[7], (DEPTH, D_MODEL, D_MODEL), D_MODEL ** -0.5),
        "rel_bias": nrm(ks[8], (N_BUCKETS, N_HEADS), 0.5),
        "g_ffn": 1.0 + nrm(ks[9], (DEPTH, D_MODEL), 0.02),
        "w_ffn_gate": nrm(ks[10], (DEPTH, D_MODEL, D_FF), D_MODEL ** -0.5),
        "w_ffn_up": nrm(ks[11], (DEPTH, D_MODEL, D_FF), D_MODEL ** -0.5),
        "w_ffn_down": nrm(ks[12], (DEPTH, D_FF, D_MODEL), D_FF ** -0.5),
        "g_final": 1.0 + nrm(ks[13], (D_MODEL,), 0.02),
    }

def first_block(x, g_mix, w_in, b_gate, conv_w, w_branch_a, w_branch_b, w_out, rel_bias,
              g_ffn, w_ffn_gate, w_ffn_up, w_ffn_down, g_final):
    bsz, seq_len, _ = x.shape
    for layer in range(DEPTH):
        h = rms_norm(x, g_mix[layer])
        proj = h @ w_in[layer]
        (c_b, c_c, c_x, q, k, v, iq, ik, iw, g_a, g_b) = jnp.split(proj, PROJ_SPLITS, axis=-1)
        y_a = short_conv_mixer(c_b, c_c, c_x, conv_w[layer]) @ w_branch_a[layer]
        attn = dsa_attention(q.reshape(bsz, seq_len, N_HEADS, HEAD_DIM), k, v,
                             iq.reshape(bsz, seq_len, N_IDX_HEADS, IDX_DIM), ik, iw, rel_bias)
        y_b = attn @ w_branch_b[layer]
        gates = jax.nn.sigmoid(jnp.concatenate([g_a, g_b], axis=-1) + b_gate[layer])
        merged = gates[..., :D_MODEL] * y_a + gates[..., D_MODEL:] * y_b
        x = x + merged @ w_out[layer]
        h2 = rms_norm(x, g_ffn[layer])
        x = x + (jax.nn.silu(h2 @ w_ffn_gate[layer]) * (h2 @ w_ffn_up[layer])) @ w_ffn_down[layer]
    return rms_norm(x, g_final)


DEPTH_2 = 2

N_A = DEPTH_2 // 2
N_B = DEPTH_2 - N_A
EXPAND = 2
A_WIDTH = EXPAND * D_MODEL
POOL_WINDOWS = (2, 4, 8, 16)
N_POOL_GROUPS = len(POOL_WINDOWS)
GROUP_WIDTH = A_WIDTH // N_POOL_GROUPS
N_HEADS_2 = D_MODEL // HEAD_DIM
N_KV_HEADS = max(1, N_HEADS_2 // 8)
GQA_GROUPS = N_HEADS_2 // N_KV_HEADS
B_WIDTH = N_HEADS_2 * HEAD_DIM
WINDOW = 128
BLOCK = 128
NEG_INF = -1e30


def rmsnorm(x, g):
    xf = x.astype(jnp.float32)
    y = xf * lax.rsqrt(jnp.mean(xf * xf, axis=-1, keepdims=True) + EPS)
    return y.astype(x.dtype) * g

def modulate(h, shift, scale):
    return h * (1 + scale[:, None, :]) + shift[:, None, :]

def t5_causal_buckets():
    i = np.arange(BLOCK)[:, None]
    j = np.arange(2 * BLOCK)[None, :]
    n = np.maximum(i + BLOCK - j, 0)
    max_exact = N_BUCKETS // 2
    large = max_exact + (np.log(np.maximum(n, 1) / max_exact) / math.log(MAX_DISTANCE / max_exact)
                         * (N_BUCKETS - max_exact)).astype(np.int32)
    large = np.minimum(large, N_BUCKETS - 1)
    return np.where(n < max_exact, n, large).astype(np.int32)

def band_mask(n_blocks):
    i = jnp.arange(BLOCK)[:, None]
    j = jnp.arange(2 * BLOCK)[None, :]
    rel = i + BLOCK - j
    band = (rel >= 0) & (rel < WINDOW)
    blk = jnp.arange(n_blocks)[:, None, None]
    return band[None] & ((blk > 0) | (j[None] >= BLOCK))

def causal_multiscale_pool(u):
    S = u.shape[1]
    uf = u.astype(jnp.float32)
    csp = jnp.pad(jnp.cumsum(uf, axis=1), ((0, 0), (1, 0), (0, 0)))
    t = jnp.arange(S)
    outs = []
    for g, w in enumerate(POOL_WINDOWS):
        c_g = csp[..., g * GROUP_WIDTH:(g + 1) * GROUP_WIDTH]
        upper = c_g[:, 1:]
        lower = jnp.pad(c_g, ((0, 0), (w, 0), (0, 0)))[:, 1:S + 1]
        count = jnp.minimum(t + 1, w).astype(jnp.float32)[None, :, None]
        outs.append((upper - lower) / count)
    return (jnp.concatenate(outs, axis=-1) - uf).astype(u.dtype)

def pool_mixer(h, w_in, w_group, scale, w_out):
    B, S, _ = h.shape
    u, z = jnp.split(h @ w_in, 2, axis=-1)
    p = causal_multiscale_pool(u).reshape(B, S, N_POOL_GROUPS, GROUP_WIDTH)
    y = jnp.einsum('bsgc,gcd->bsgd', p, w_group).reshape(B, S, A_WIDTH) * scale
    return (y * jax.nn.silu(z)) @ w_out

def shared_kv_blocks(x, c_act, kv_norm_g, kv_ada_w, kv_ada_b, w_kv):
    B, S, _ = x.shape
    nb = S // BLOCK
    shift, scale = jnp.split(c_act @ kv_ada_w + kv_ada_b, 2, axis=-1)
    hk = modulate(rmsnorm(x, kv_norm_g), shift, scale)
    kv = (hk @ w_kv).reshape(B, S, 2, N_KV_HEADS, HEAD_DIM)
    k, v = kv[:, :, 0], kv[:, :, 1]

    def to_band(t):
        prev = jnp.pad(t, ((0, 0), (BLOCK, 0), (0, 0), (0, 0)))[:, :S]
        prev = prev.reshape(B, nb, BLOCK, N_KV_HEADS, HEAD_DIM)
        cur = t.reshape(B, nb, BLOCK, N_KV_HEADS, HEAD_DIM)
        return jnp.concatenate([prev, cur], axis=2).transpose(1, 0, 2, 3, 4)

    return to_band(k), to_band(v)

def swa_sink_mixer(h, kb, vb, pos_bias, mask, w_in, sinks, w_out):
    B, S, _ = h.shape
    nb = S // BLOCK
    q, z = jnp.split(h @ w_in, 2, axis=-1)
    q = q * (HEAD_DIM ** -0.5)
    qb = q.reshape(B, nb, BLOCK, N_KV_HEADS, GQA_GROUPS, HEAD_DIM).transpose(1, 0, 2, 3, 4, 5)
    sink = sinks.astype(jnp.float32).reshape(N_KV_HEADS, GQA_GROUPS)[None, :, :, None, None]

    def block_fn(args):
        qn, kn, vn, mn = args
        s = jnp.einsum('bqhgd,bkhd->bhgqk', qn, kn).astype(jnp.float32) + pos_bias
        s = jnp.where(mn[None, None, None], s, NEG_INF)
        m = jnp.maximum(jnp.max(s, axis=-1, keepdims=True), sink)
        p = jnp.exp(s - m)
        p = p / (jnp.sum(p, axis=-1, keepdims=True) + jnp.exp(sink - m))
        return jnp.einsum('bhgqk,bkhd->bqhgd', p.astype(vn.dtype), vn)

    o = lax.map(block_fn, (qb, kb, vb, mask))
    o = o.transpose(1, 0, 2, 3, 4, 5).reshape(B, S, B_WIDTH)
    return (o * jax.nn.silu(z)) @ w_out

def second_inputs(seed: int = 0) -> dict:
    key = jax.random.key(seed)
    ks = jax.random.split(key, 18)
    D, E, GW = D_MODEL, A_WIDTH, GROUP_WIDTH
    nrm = jax.random.normal
    f32 = jnp.float32
    return {
        "x": nrm(ks[0], (BATCH, SEQ, D), f32),
        "c": nrm(ks[1], (BATCH, D), f32),
        "norm_g": 1.0 + 0.05 * nrm(ks[2], (DEPTH_2, D), f32),
        "ada_w": 0.5 * D ** -0.5 * nrm(ks[3], (DEPTH_2, D, 3 * D), f32),
        "ada_b": 0.02 * nrm(ks[4], (DEPTH_2, 3 * D), f32),
        "a_w_in": D ** -0.5 * nrm(ks[5], (N_A, D, 2 * E), f32),
        "a_w_group": GW ** -0.5 * nrm(ks[6], (N_A, N_POOL_GROUPS, GW, GW), f32),
        "a_scale": 1.0 + 0.1 * nrm(ks[7], (N_A, E), f32),
        "a_w_out": E ** -0.5 * nrm(ks[8], (N_A, E, D), f32),
        "kv_norm_g": 1.0 + 0.05 * nrm(ks[9], (D,), f32),
        "kv_ada_w": 0.5 * D ** -0.5 * nrm(ks[10], (D, 2 * D), f32),
        "kv_ada_b": 0.02 * nrm(ks[11], (2 * D,), f32),
        "w_kv": D ** -0.5 * nrm(ks[12], (D, 2 * N_KV_HEADS * HEAD_DIM), f32),
        "b_w_in": D ** -0.5 * nrm(ks[13], (N_B, D, 2 * B_WIDTH), f32),
        "b_sinks": 0.5 * nrm(ks[14], (N_B, N_HEADS_2), f32),
        "b_w_out": B_WIDTH ** -0.5 * nrm(ks[15], (N_B, B_WIDTH, D), f32),
        "rel_bias": 0.5 * nrm(ks[16], (N_BUCKETS, N_HEADS_2), f32),
        "final_g": 1.0 + 0.05 * nrm(ks[17], (D,), f32),
    }

def second_block(x, c, norm_g, ada_w, ada_b, a_w_in, a_w_group, a_scale, a_w_out,
              kv_norm_g, kv_ada_w, kv_ada_b, w_kv, b_w_in, b_sinks, b_w_out,
              rel_bias, final_g):
    S = x.shape[1]
    nb = S // BLOCK
    c_act = jax.nn.silu(c)
    buckets = t5_causal_buckets()
    pos_bias = rel_bias[buckets].astype(jnp.float32).transpose(2, 0, 1)
    pos_bias = pos_bias.reshape(N_KV_HEADS, GQA_GROUPS, BLOCK, 2 * BLOCK)[None]
    mask = band_mask(nb)

    kb = vb = None
    for l in range(DEPTH_2):
        shift, scale, gate = jnp.split(c_act @ ada_w[l] + ada_b[l], 3, axis=-1)
        if l < N_A:
            h = modulate(rmsnorm(x, norm_g[l]), shift, scale)
            y = pool_mixer(h, a_w_in[l], a_w_group[l], a_scale[l], a_w_out[l])
        else:
            if l == N_A:
                kb, vb = shared_kv_blocks(x, c_act, kv_norm_g, kv_ada_w, kv_ada_b, w_kv)
            j = l - N_A
            h = modulate(rmsnorm(x, norm_g[l]), shift, scale)
            y = swa_sink_mixer(h, kb, vb, pos_bias, mask, b_w_in[j], b_sinks[j], b_w_out[j])
        x = x + gate[:, None, :] * y
    return rmsnorm(x, final_g)


def setup_inputs(seed=0):
    out = dict(first_inputs(seed))
    for name, value in second_inputs(seed + 1).items():
        if name != "x":
            out[name + "_2"] = value
    return out


def reference(
    x, g_mix, w_in, b_gate, conv_w, w_branch_a, w_branch_b, w_out, rel_bias, g_ffn, w_ffn_gate,
    w_ffn_up, w_ffn_down, g_final, c_2, norm_g_2, ada_w_2, ada_b_2, a_w_in_2, a_w_group_2,
    a_scale_2, a_w_out_2, kv_norm_g_2, kv_ada_w_2, kv_ada_b_2, w_kv_2, b_w_in_2, b_sinks_2,
    b_w_out_2, rel_bias_2, final_g_2,
):
    x = first_block(
        x, g_mix, w_in, b_gate, conv_w, w_branch_a, w_branch_b, w_out, rel_bias, g_ffn,
        w_ffn_gate, w_ffn_up, w_ffn_down, g_final,
    )
    return second_block(
        x, c_2, norm_g_2, ada_w_2, ada_b_2, a_w_in_2, a_w_group_2, a_scale_2, a_w_out_2,
        kv_norm_g_2, kv_ada_w_2, kv_ada_b_2, w_kv_2, b_w_in_2, b_sinks_2, b_w_out_2, rel_bias_2,
        final_g_2,
    )


_drawn_inputs = setup_inputs


def setup_inputs(seed=0):
    import zlib

    import numpy as np

    out = dict(_drawn_inputs(seed))
    spreads = {}
    factors = {'b_gate': 8.0,
     'g_ffn': 4.18,
     'g_final': 2.687,
     'norm_g_2': 4.14,
     'ada_b_2': 3.817,
     'a_scale_2': 3.036,
     'kv_norm_g_2': 8.0,
     'kv_ada_b_2': 8.0,
     'b_sinks_2': 37.023,
     'rel_bias_2': 3.197}
    for name, (base, spread) in spreads.items():
        noise = np.random.default_rng([zlib.crc32(name.encode()), seed]).standard_normal(out[name].shape)
        drawn = base * np.exp(spread * noise) if base else spread * noise
        out[name] = __import__('jax').numpy.asarray(drawn.astype(out[name].dtype))
    for name, factor in factors.items():
        out[name] = (out[name] * factor).astype(out[name].dtype)
    return out
```

```python
from contextlib import ExitStack

import numpy as np

import concourse.bass as bass
from concourse import mybir

F32 = mybir.dt.float32
FR = mybir.dt.float32r
ALU = mybir.AluOpType
ACT = mybir.ActivationFunctionType
AXX = mybir.AxisListType.X

S = 1024
NT = 8
DFF = 2816
T = 4096
BASE = 16640
MAIN = 15
NEG = -1.0e30
FUT = -3.0e38
GONE = -3.3e38

C_B, C_C, C_X, C_Q, C_KV, C_IQ, C_IK, C_GA, C_GB = 0, 512, 1024, 1536, 2048, 2176, 2688, 2760, 3784

V_GMIX, V_GFFN, V_GFIN, V_NORM, V_ADAB, V_KVG, V_KVB, V_SCALE, V_GATE, V_CONV, V_C, V_FIN2 = (
    0, 8, 16, 24, 40, 88, 96, 112, 128, 144, 156, 164)
V_ALL = 172


class Tok:

    __slots__ = ("eng", "idx", "sem", "val", "needed")

    def __init__(self, eng=None, idx=None, sem=None, val=None):
        self.eng, self.idx, self.sem, self.val, self.needed = eng, idx, sem, val, False


class Later:

    def matmul(self, *a, **k):
        return lambda e: e.matmul(*a, **k)

    def transpose(self, *a, **k):
        return lambda e: e.transpose(*a, **k)

    def activation(self, *a, **k):
        return lambda e: e.activation(*a, **k)

    def tensor_tensor(self, *a, **k):
        return lambda e: e.tensor_tensor(*a, **k)

    def scalar_tensor_tensor(self, *a, **k):
        return lambda e: e.scalar_tensor_tensor(*a, **k)

    def tensor_scalar(self, *a, **k):
        return lambda e: e.tensor_scalar(*a, **k)

    def tensor_copy(self, *a, **k):
        return lambda e: e.tensor_copy(*a, **k)

    def reciprocal(self, *a, **k):
        return lambda e: e.reciprocal(*a, **k)

    def memset(self, *a, **k):
        return lambda e: e.memset(*a, **k)

    def affine_select(self, *a, **k):
        return lambda e: e.affine_select(*a, **k)

    def max(self, *a, **k):
        return lambda e: e.max(*a, **k)

    def match_replace(self, *a, **k):
        return lambda e: e.match_replace(*a, **k)

    def tensor_tensor_reduce(self, *a, **k):
        return lambda e: e.tensor_tensor_reduce(*a, **k)

    def tensor_reduce(self, *a, **k):
        return lambda e: e.tensor_reduce(*a, **k)


LATER = Later()


class Queues:

    def __init__(self):
        self.q = {e: [] for e in ("pe", "act", "dve", "pool", "sp")}
        self.dma = {}

    def op(self, eng, fn, *after):
        fn = fn(LATER)
        t = Tok(eng, len(self.q[eng]))
        self.q[eng].append((fn, flat(after), t, None))
        return t

    def load(self, out, in_, sem, *after, eng="sp"):
        self.dma[sem] = self.dma.get(sem, 0) + 16
        t = Tok(sem=sem, val=self.dma[sem])
        self.q[eng].append((lambda e: e.dma_start(out, in_), flat(after), t, sem))
        return t

    def last(self, *engs):
        return [self.q[e][-1][2] for e in engs if self.q[e]]

    def emit(self, nc, ctx):
        for q in self.q.values():
            for _, after, _, _ in q:
                for t in after:
                    t.needed = True
        sems = {e: ctx.enter_context(nc.semaphore("s_" + e)) for e in self.q}
        sems.update({d: ctx.enter_context(nc.semaphore("d_" + d)) for d in self.dma})
        for e, q in self.q.items():
            n = 0
            for _, _, t, sem in q:
                if sem is None and t.needed:
                    n += 1
                    t.sem, t.val = e, n
        block = ctx.enter_context(nc.Block())
        ends = dict(self.dma)

        def run(e, name):
            seen = {}
            for fn, after, t, sem in self.q[name]:
                for a in after:
                    if seen.get(a.sem, 0) < a.val:
                        e.wait_ge(sems[a.sem], a.val)
                        seen[a.sem] = a.val
                ins = fn(e)
                if sem is not None:
                    ins.then_inc(sems[sem], 16)
                elif t.needed:
                    ins.then_inc(sems[name], 1)
            if name == "sp":
                for d, v in ends.items():
                    e.wait_ge(sems[d], v)

        @block.sync
        def _(e):
            run(e, "sp")

        @block.tensor
        def _(e):
            run(e, "pe")

        @block.scalar
        def _(e):
            run(e, "act")

        @block.vector
        def _(e):
            run(e, "dve")

        @block.gpsimd
        def _(e):
            run(e, "pool")


def flat(x):
    out = []
    for a in x:
        if a is None:
            continue
        if isinstance(a, (list, tuple)):
            out += flat(a)
        else:
            out.append(a)
    return out


class Slot:

    def __init__(self, t, name):
        self.t, self.name, self.free = t, name, []


class Ring:
    def __init__(self, slots):
        self.slots, self.n = slots, 0

    def take(self):
        s = self.slots[self.n % len(self.slots)]
        self.n += 1
        return s


class Net:
    def __init__(self, nc, A, out, consts, plan, mem):
        self.nc, self.A, self.out, self.C, self.plan, self.mem = nc, A, out, consts, plan, mem
        self.Q = Queues()
        self.units = []
        self.n_dma = self.n_split = 0
        self.split_no = 0
        self.lo_eng = "pool"
        self.ahead = 3

    def at(self, name, tile, cols=S, dt=F32, off=0, parts=128):
        key = (name, tile, dt)
        if key not in self.mem:
            self.mem[key] = self.nc.alloc_sbuf_tensor_at(
                name, [parts, cols], dt, offset=BASE + tile * T + off)
        return self.mem[key]

    def main(self, name, i, dt=F32, cols=S, off=0):
        return self.at(name, MAIN + i, cols, dt, off)

    def dram(self, name, shape):
        if name not in self.mem:
            self.mem[name] = self.nc.dram_tensor(name, shape, F32)
        return self.mem[name].ap()

    def setup(self):
        self.raw = [Slot(self.at(f"raw{i}", i), f"raw{i}") for i in range(3)]
        self.wh = [Slot(self.at(f"wh{i}", 3 + i, dt=FR), f"wh{i}") for i in range(3)]
        self.wl = [Slot(self.at(f"wl{i}", 6 + i, dt=FR), f"wl{i}") for i in range(3)]
        self.tmp = Ring([Slot(self.at(f"tmp{i}", 10 + i), f"tmp{i}") for i in range(5)])
        if "ps" not in self.mem:
            self.mem["ps"] = [self.nc.alloc_psum_tensor(f"ps{i}", [128, S], F32) for i in range(4)]
        self.ps = Ring([Slot(t, f"ps{i}") for i, t in enumerate(self.mem["ps"])])
        o = [0]

        def small(name, cols):
            t = self.at(name, 9, cols, off=o[0])
            o[0] += -(-4 * cols // 32) * 32
            return t

        self.ident = small("ident", 128)
        self.ones = small("ones", 128)
        self.flip = small("flip", 128)
        self.vec = small("vec", V_ALL)
        self.mod = small("mod", 64)
        self.gs = small("gs", 24)
        self.iw = small("iw", 64)
        self.cact = small("cact", 8)
        self.r8 = small("r8", 16)
        self.eps = small("eps", 1)
        self.st = small("st", 128)
        self.m8 = small("m8", 16)
        self.sk = small("sk", 16)
        self.invc = small("invc", 16 * 4)
        assert o[0] <= T, o[0]
        self.oneh = self.at("oneh", 51, 384, parts=32)
        self.rel = self.at("rel", 51, 24, off=1536, parts=32)
        self.gb = self.at("gbias", 51, 384, off=2048, parts=32)

    def issue_dma(self, j):
        parts, kind, _ = self.plan[j]
        slot = self.raw[j % 3]
        for view, src in parts:
            t = self.Q.load(view(slot.t), src, f"raw{j % 3}", slot.free)
        slot.free = []
        self.loaded[j] = t

    def issue_split(self, j):
        parts, kind, cols = self.plan[j]
        if kind == "raw":
            return
        raw = self.raw[j % 3]
        wh, wl = self.wh[self.n_w % 3], self.wl[self.n_w % 3]
        self.n_w += 1
        v, h, lo = raw.t[:, 0:cols], wh.t[:, 0:cols], wl.t[:, 0:cols]
        a = self.Q.op("act", lambda e: e.activation(h, v, ACT.Copy), self.loaded[j], wh.free)
        eng = self.lo_eng
        b = self.Q.op(eng, lambda e: e.tensor_tensor(lo, v, h.bitcast(F32), ALU.subtract), a, wl.free)
        wh.free, wl.free, raw.free = [], [], [a, b]
        self.ready[j] = (wh, wl, [a, b])

    def unit(self, parts, kind="split", cols=S):
        self.units.append((parts, kind, cols))
        i = len(self.units) - 1
        if self.plan is None:
            return (self.wh[0], self.wl[0], []) if kind == "split" else (self.raw[0], [])
        while self.n_split < min(i + self.ahead, len(self.plan)) or self.n_dma < min(i + 4, len(self.plan)):
            if self.n_dma < len(self.plan) and self.n_dma < self.n_split + 3:
                if not (self.plan[self.n_dma - 3][1] == "raw" and self.n_dma - 3 >= i) or self.n_dma < 3:
                    self.issue_dma(self.n_dma)
                    self.n_dma += 1
                    continue
            if self.n_split < min(i + self.ahead, self.n_dma):
                self.issue_split(self.n_split)
                self.n_split += 1
                continue
            break
        if kind == "raw":
            return self.raw[i % 3], [self.loaded[i]]
        return self.ready[i]

    def w8(self, w, c0, n=128, k0=0, nk=8):
        src = w[k0:k0 + nk * 128, c0:c0 + n].rearrange("(k p) n -> p k n", p=128)
        return [(lambda t: t[:, 0:nk * n].rearrange("p (k n) -> p k n", k=nk), src)]

    def gemm(self, unit, nk, n, acts, col0=0, m=128):
        wh, wl, toks = unit
        ps = self.ps.take()
        WH = wh.t[:, 0:nk * n].rearrange("p (k n) -> p k n", k=nk)
        WL = wl.t[:, 0:nk * n].rearrange("p (k n) -> p k n", k=nk)
        first = list(toks) + list(ps.free)
        ps.free = []
        for k in range(nk):
            hi, lo, atok = acts[k]
            wk, lk = WH[:, k, col0:col0 + m], WL[:, k, col0:col0 + m]
            seq = [(wk, hi, 0), (wk, hi, 1), (wk, lo, 0), (wk, lo, 1), (lk, hi, 0), (lk, hi, 1)]
            for i, (w, a, h) in enumerate(seq):
                o, r = ps.t[0:m, h * 512:h * 512 + 512], a[:, h * 512:h * 512 + 512]
                t = self.Q.op("pe", lambda e, o=o, w=w, r=r, s=(k == 0 and i < 2), z=(k == nk - 1 and i >= 4):
                              e.matmul(o, w, r, start=s, stop=z), first, atok if i == 0 else None)
                first = []
        wh.free = wl.free = [t]
        return ps, t

    def split(self, src, hi, lo, *after, free=(), eng=None):
        a = self.Q.op("act", lambda e: e.activation(hi, src, ACT.Copy), after, free)
        b = self.Q.op(eng or self.lo_eng, lambda e: e.tensor_tensor(lo, src, hi.bitcast(F32), ALU.subtract),
                      a, after, free)
        return [a, b]

    def split_ps(self, src, hi, lo, *after, scale=1.0, free=()):
        a = self.Q.op("act", lambda e: e.activation(hi, src, ACT.Copy, scale=scale), after, free)
        b = self.Q.op("dve", lambda e: e.scalar_tensor_tensor(
            out=lo, in0=src, scalar=scale, in1=hi.bitcast(F32), op0=ALU.mult, op1=ALU.subtract), a, free)
        return [a, b]

    def prods(self, o, L, R, first, last, after):
        seq = [(L[0], R[0]), (L[0], R[1]), (L[1], R[0])]
        for i, (a, b) in enumerate(seq):
            t = self.Q.op("pe", lambda e, a=a, b=b, s=(first and i == 0), z=(last and i == 2):
                          e.matmul(o, a, b, start=s, stop=z), after if i == 0 else None)
        return t

    def rstd(self, X, xtok):
        Q = self.Q
        acc = self.tmp.take()
        at = None
        for j in range(NT):
            if j == 0:
                at = Q.op("act", lambda e, x=X[0]: e.activation(acc.t[:, :], x[:, :], ACT.Square),
                          xtok[0], acc.free)
            else:
                s = self.tmp.take()
                if s is acc:
                    s = self.tmp.take()
                a = Q.op("act", lambda e, x=X[j], s=s: e.activation(s.t[:, :], x[:, :], ACT.Square),
                         xtok[j], s.free)
                at = Q.op("dve", lambda e, s=s: e.tensor_tensor(acc.t[:, :], acc.t[:, :], s.t[:, :], ALU.add),
                          a, at)
                s.free = [at]
        ps = self.ps.take()
        for t in range(NT):
            m = Q.op("pe", lambda e, t=t: e.matmul(ps.t[:, t:t + 1], acc.t[:, t * 128:t * 128 + 128],
                                                   self.ones[:, 0:1], start=True, stop=True),
                     at, ps.free, self.ctok)
        ps.free = []
        a = Q.op("act", lambda e: e.activation(self.r8[:, 0:8], ps.t[:, 0:8], ACT.Sqrt,
                                               bias=self.eps[:, 0:1], scale=1.0 / S), m, Q.last("dve"))
        r = Q.op("dve", lambda e: e.reciprocal(self.r8[:, 8:16], self.r8[:, 0:8]), a)
        ps.free = [a]
        dg = self.tmp.take()
        if dg is acc:
            dg = self.tmp.take()
        d = Q.op("dve", lambda e: e.tensor_tensor(
            dg.t[:, :].rearrange("p (t c) -> p t c", t=8),
            self.ident[:, :].unsqueeze(1).to_broadcast([128, 8, 128]),
            self.r8[:, 8:16].unsqueeze(2).to_broadcast([128, 8, 128]), ALU.mult), r, dg.free)
        rb = self.ps.take()
        for h in range(2):
            m2 = Q.op("pe", lambda e, h=h: e.matmul(rb.t[:, h * 512:h * 512 + 512], self.ones[:, :],
                                                    dg.t[:, h * 512:h * 512 + 512], start=True, stop=True),
                      d, rb.free)
        rb.free = []
        acc.free, dg.free = [m], [m2]
        return rb, m2

    def scaled(self, X, xtok, rb, rtok, g, hi, lo, free, shift=None):
        Q, toks = self.Q, []
        for j in range(NT):
            s = self.tmp.take()
            a = Q.op("dve", lambda e, j=j, s=s: e.scalar_tensor_tensor(
                out=s.t[:, :], in0=X[j][:, :], scalar=g(j), in1=rb.t[:, :], op0=ALU.mult, op1=ALU.mult),
                xtok[j], rtok, s.free)
            if shift is not None:
                a2 = Q.op("act", lambda e, j=j, s=s: e.activation(s.t[:, :], s.t[:, :], ACT.Identity,
                                                                  bias=shift(j)), a)
            else:
                a2 = a
            t = self.split(s.t[:, :], hi[j][:, :], lo[j][:, :], a2, free=free)
            s.free = t
            toks.append(t)
        rb.free = [a]
        return toks

    def acts(self, hi, lo, toks):
        return [(h, l, t) for h, l, t in zip(hi, lo, toks)]

    def build(self):
        Q, A = self.Q, self.A
        self.loaded, self.ready, self.n_w = {}, {}, 0
        self.setup()
        C = self.C
        c0 = [Q.load(self.ident[:, :], C["ident"], "c"), Q.load(self.flip[:, :], C["flip"], "c"), Q.load(self.oneh[:, :], C["oneh"], "c"),
              Q.load(self.rel[:, 0:8], A["rel_bias"], "c"), Q.load(self.rel[:, 8:24], A["rel_bias_2"], "c"),
              Q.load(self.invc[:, :], C["invc"].to_broadcast([128, 64]), "c"),
              Q.load(self.sk[:, :], A["b_sinks_2"].to_broadcast([128, 16]), "c")]
        va, vb = self.tmp.take(), self.tmp.take()
        rows = [("g_mix", V_GMIX), ("g_ffn", V_GFFN), ("g_final", V_GFIN), ("norm_g_2", V_NORM),
                ("ada_b_2", V_ADAB), ("kv_norm_g_2", V_KVG), ("kv_ada_b_2", V_KVB), ("a_scale_2", V_SCALE),
                ("b_gate", V_GATE), ("conv_w", V_CONV), ("c_2", V_C), ("final_g_2", V_FIN2)]
        for name, r in rows:
            ap = A[name]
            if len(ap.shape) == 1:
                flatv = ap
            elif len(ap.shape) == 2:
                flatv = ap.rearrange("a b -> (a b)")
            else:
                flatv = ap.rearrange("a b c -> (a b c)")
            n = flatv.shape[0] // 128
            src = flatv.rearrange("(r p) -> r p", p=128)
            n1 = max(0, min(n, 128 - r))
            if n1:
                cc = Q.load(va.t[r:r + n1, 0:128], src[0:n1, :], "c")
            if n > n1:
                cc = Q.load(vb.t[r + n1 - 128:r + n - 128, 0:128], src[n1:n, :], "c")
        z1 = Q.op("pool", lambda e: e.memset(self.ones[:, :], 1.0))
        z2 = Q.op("pool", lambda e: e.memset(self.eps[:, :], 1e-6))
        self.ctok = [cc, z1, z2]

        xn = [self.main(f"xn{i}", i) for i in range(NT)]
        X = [self.main(f"xt{j}", 16 + j) for j in range(NT)]
        for i in range(NT):
            xl = Q.load(xn[i][:, :], A["x"][0, i * 128:(i + 1) * 128, :], f"xn{i}")
            xn[i] = (xn[i], xl)
        ps = self.ps.take()
        Q.op("pe", lambda e: e.transpose(ps.t[:, 0:128], va.t[:, 0:128], self.ident[:, :]), cc)
        tv = Q.op("pe", lambda e: e.transpose(ps.t[:, 128:V_ALL], vb.t[0:V_ALL - 128, 0:128],
                                              self.ident[0:V_ALL - 128, 0:V_ALL - 128]))
        vv = Q.op("dve", lambda e: e.tensor_copy(self.vec[:, :], ps.t[:, 0:V_ALL]), tv)
        ps.free = [vv]
        va.free = vb.free = [tv]
        vec = lambda base: (lambda j: self.vec[:, base + j:base + j + 1])
        ca = Q.op("act", lambda e: e.activation(self.cact[:, :], self.vec[:, V_C:V_C + 8], ACT.Silu), vv)

        ps = self.ps.take()
        t = Q.op("pe", lambda e: e.matmul(ps.t[0:24, 0:384], self.rel[:, :], self.oneh[:, :],
                                          start=True, stop=True), cc, ps.free)
        t = Q.op("dve", lambda e: e.tensor_copy(self.gb[0:24, :], ps.t[0:24, 0:384]), t)
        ps.free = [t]
        gd = self.dram("gdist", [24, 384])
        gst = Q.load(gd, self.gb[0:24, :], "gst", t)

        xtok = self.transposed(xn, X, None)
        rb, rtok = self.rstd(X, xtok)
        hi = [self.main(f"ah{j}", j, FR) for j in range(NT)]
        lo = [self.main(f"al{j}", 8 + j, FR) for j in range(NT)]
        htok = self.scaled(X, xtok, rb, rtok, vec(V_GMIX), hi, lo, Q.last("pe"))
        h = self.acts(hi, lo, htok)
        W = A["w_in"][0]

        qh = [self.main(f"qh{j}", 16 + j, FR) for j in range(4)]
        ql = [self.main(f"ql{j}", 20 + j, FR) for j in range(4)]
        KE, KO, LE, LO = (self.main(f"kp{i}", 24 + i, FR) for i in range(4))
        kt, kt2 = self.main("kt", 33), self.main("kt2", 34)
        dead = [htok, Q.last("dve")]
        zz = self.zero_pads([(KE, 64), (LE, 64), (KO, 0), (LO, 0)], dead)
        u = self.unit(self.w8(W, C_IK, 72), cols=576)
        ps, t = self.gemm(u, 8, 72, h, m=72)
        t = Q.op("act", lambda e, ps=ps: e.activation(kt[0:72, :], ps.t[0:72, :], ACT.Copy), t, dead)
        ps.free = [t]
        ktt = self.k_pads(kt, kt2, (KE, LE, KO, LO), [t, zz], "swap0", [])
        ps = self.ps.take()
        for i in range(NT):
            t = Q.op("pe", lambda e, i=i, ps=ps: e.transpose(ps.t[:, i * 72:i * 72 + 72] if i < 7 else ps.t[:, 512:584],
                                                      kt[0:72, i * 128:i * 128 + 128], self.ident[0:72, 0:72]),
                     t if i == 0 else None, ps.free)
        for i in range(NT):
            c = i * 72 if i < 7 else 512
            t = Q.op("dve", lambda e, i=i, c=c, ps=ps: e.tensor_scalar(
                self.iw[:, i * 8:i * 8 + 8], ps.t[:, c + 64:c + 72], 512.0 ** -0.5, None, ALU.mult), t)
        ps.free = [t]
        iwt = t
        qt = []
        for j in range(4):
            u = self.unit(self.w8(W, C_IQ + 128 * j))
            ps, t = self.gemm(u, 8, 128, h)
            t = self.split_ps(ps.t[:, :], qh[j][:, :], ql[j][:, :], t, free=dead)
            ps.free = t[1:]
            qt.append(t)
        smt = {}
        off = [0]
        for b in range(NT):
            off.append(off[-1] + (b + 1) * 128)
        SMt = self.main("sm", 28, cols=off[-1])
        SM = [SMt[:, off[b]:off[b + 1]] for b in range(NT)]
        for b in range(2):
            t = Q.op("pool", lambda e, b=b: e.memset(SM[b], 0.0), dead)
            smt[b] = [Q.op("pool", lambda e, b=b: e.affine_select(
                out=SM[b][:, b * 128:b * 128 + 128], in_=SM[b][:, b * 128:b * 128 + 128],
                compare_op=ALU.is_ge, fill=NEG, base=0, pattern=[[-1, 128]], channel_multiplier=1), t)]
        for b in range(2, NT):
            Wd = (b + 1) * 128
            st = dead
            for hd in range(8):
                j, odd = hd // 2, hd % 2
                K = (KO, LO) if odd else (KE, LE)
                ps, t = self.logits((qh[j], ql[j]), K, b, Wd, [qt[j], ktt])
                r = self.tmp.take()
                a = Q.op("act", lambda e, ps=ps, r=r, Wd=Wd: e.activation(
                    r.t[:, 0:Wd], ps.t[:, 0:Wd], ACT.Relu), t, r.free)
                ps.free = [a]
                iwc = self.iw[:, b * 8 + hd:b * 8 + hd + 1]
                if hd == 0:
                    st = Q.op("dve", lambda e, b=b, r=r, Wd=Wd, iwc=iwc: e.tensor_scalar(
                        SM[b], r.t[:, 0:Wd], iwc, None, ALU.mult), a, st, iwt)
                else:
                    st = Q.op("dve", lambda e, b=b, r=r, Wd=Wd, iwc=iwc: e.scalar_tensor_tensor(
                        out=SM[b], in0=r.t[:, 0:Wd], scalar=iwc, in1=SM[b], op0=ALU.mult, op1=ALU.add), a, st)
                r.free = [st]
            smt[b] = Q.op("pool", lambda e, b=b: e.affine_select(
                out=SM[b][:, b * 128:b * 128 + 128], in_=SM[b][:, b * 128:b * 128 + 128],
                compare_op=ALU.is_ge, fill=FUT, base=0, pattern=[[-1, 128]], channel_multiplier=1), st)
        index_done = Q.last("pe")
        for b in range(2, NT):
            t = smt[b]
            for r in range(32):
                m8 = self.m8[:, (r % 2) * 8:(r % 2) * 8 + 8]
                t = Q.op("dve", lambda e, b=b, m8=m8: e.max(m8, SM[b]), t)
                t = Q.op("dve", lambda e, b=b, m8=m8: e.match_replace(SM[b], m8, SM[b], GONE), t)
            smt[b] = Q.op("dve", lambda e, b=b: e.tensor_scalar(SM[b], SM[b], -3.2e38, NEG, ALU.is_ge, ALU.mult), t)

        cv = self.dram("cv", [512, S])
        cvt = []
        for j in range(4):
            u = self.unit(self.w8(W, C_C + 128 * j))
            ps, t = self.gemm(u, 8, 128, h)
            x1 = self.tmp.take()
            t1 = Q.op("act", lambda e, ps=ps, x1=x1: e.activation(x1.t[:, :], ps.t[:, :], ACT.Copy), t, x1.free)
            ps.free = [t1]
            u = self.unit(self.w8(W, C_X + 128 * j))
            ps, t = self.gemm(u, 8, 128, h)
            x2 = self.tmp.take()
            t2 = Q.op("act", lambda e, ps=ps, x2=x2: e.activation(x2.t[:, :], ps.t[:, :], ACT.Copy), t, x2.free)
            ps.free = [t2]
            t1 = Q.op("pool", lambda e, x1=x1, x2=x2: e.tensor_tensor(x1.t[:, :], x1.t[:, :], x2.t[:, :], ALU.mult), t1, t2)
            y = self.tmp.take()
            w = [self.vec[:, V_CONV + 4 * k + j:V_CONV + 4 * k + j + 1] for k in range(3)]
            t3 = Q.op("pool", lambda e, x1=x1, y=y, w=w: e.tensor_scalar(y.t[:, :], x1.t[:, :], w[2], None, ALU.mult), t1, y.free, vv)
            for sh in (1, 2):
                t4 = Q.op("pool", lambda e, x1=x1, x2=x2, w=w, sh=sh: e.tensor_scalar(
                    x2.t[:, 0:S - sh], x1.t[:, 0:S - sh], w[2 - sh], None, ALU.mult), t3)
                t3 = Q.op("pool", lambda e, x2=x2, y=y, sh=sh: e.tensor_tensor(
                    y.t[:, sh:S], y.t[:, sh:S], x2.t[:, 0:S - sh], ALU.add), t4)
            x1.free = x2.free = [t3]
            u = self.unit(self.w8(W, C_B + 128 * j))
            ps, t = self.gemm(u, 8, 128, h)
            x3 = self.tmp.take()
            t2 = Q.op("act", lambda e, ps=ps, x3=x3: e.activation(x3.t[:, :], ps.t[:, :], ACT.Copy), t, x3.free)
            ps.free = [t2]
            t3 = Q.op("pool", lambda e, x3=x3, y=y: e.tensor_tensor(y.t[:, :], y.t[:, :], x3.t[:, :], ALU.mult), t2, t3)
            x3.free = [t3]
            cvt.append(Q.load(cv[j * 128:j * 128 + 128, :], y.t[:, :], "st_" + y.name, t3))
            y.free = [cvt[-1]]

        gd_ = self.dram("gates", [2048, S])
        gt = []
        for j in range(16):
            u = self.unit(self.w8(W, C_GA + 128 * j))
            ps, t = self.gemm(u, 8, 128, h)
            g = self.tmp.take()
            t = Q.op("act", lambda e, ps=ps, g=g, j=j: e.activation(g.t[:, :], ps.t[:, :], ACT.Sigmoid,
                                                                   bias=vec(V_GATE)(j)), t, g.free, vv)
            ps.free = [t]
            gt.append(Q.load(gd_[j * 128:j * 128 + 128, :], g.t[:, :], "st_" + g.name, t))
            g.free = [gt[-1]]

        u = self.unit(self.w8(W, C_KV))
        ps, t = self.gemm(u, 8, 128, h)
        t = Q.op("act", lambda e, ps=ps: e.activation(kt[:, :], ps.t[:, :], ACT.Copy), t, ktt)
        ps.free = [t]
        kvt = t
        ktt = self.k_pads(kt, kt2, (KE, LE, KO, LO), [t], "swap1", index_done)
        qt = []
        for j in range(4):
            u = self.unit(self.w8(W, C_Q + 128 * j))
            ps, t = self.gemm(u, 8, 128, h)
            s = self.tmp.take()
            t = Q.op("act", lambda e, ps=ps, s=s: e.activation(s.t[:, :], ps.t[:, :], ACT.Copy), t, s.free)
            ps.free = [t]
            t = self.split(s.t[:, :], qh[j][:, :], ql[j][:, :], t, free=index_done)
            s.free = t
            qt.append(t)
        projected = Q.last("pe")

        mp = self.ps.take()
        col = 0
        for w, n in ((A["ada_w_2"][0], 24), (A["ada_w_2"][1], 24), (A["kv_ada_w_2"], 16)):
            for c in range(n):
                r, rt = self.unit(self.w8(w, 128 * c), kind="raw")
                for k in range(8):
                    mt = Q.op("pe", lambda e, r=r, k=k, col=col: e.matmul(
                        mp.t[:, col:col + 1], r.t[:, k * 128:k * 128 + 128], self.cact[:, k:k + 1],
                        start=(k == 0), stop=(k == 7)), rt, mp.free, ca)
                mp.free = []
                r.free = [mt]
                col += 1

        VE, VO, VLE, VLO = (self.main(f"vp{i}", i, FR) for i in range(4))
        ptb = [(self.main(f"pth{i}", 4 + i, FR), self.main(f"ptl{i}", 6 + i, FR)) for i in range(2)]
        ptf = [projected, projected]
        oh = [self.main(f"oh{j}", 8 + j, FR) for j in range(4)]
        ol = [self.main(f"ol{j}", 12 + j, FR) for j in range(4)]
        zz = self.zero_v([(VE, 64), (VLE, 64), (VO, 0), (VLO, 0)], projected)
        vt = self.v_pads(kt, (VE, VLE, VO, VLO), 64, 64, [kvt, zz])
        T1 = self.main("t1", 34, cols=2048)
        t1t = self.table(T1, gd, 0, "t1", [gst, ktt, vt])
        mt2 = Q.op("dve", lambda e: e.tensor_tensor(self.mod[:, 0:48], mp.t[:, 0:48], self.vec[:, V_ADAB:V_ADAB + 48],
                                                    ALU.add), mt, vv)
        mt2 = Q.op("dve", lambda e: e.tensor_tensor(self.mod[:, 48:64], mp.t[:, 48:64], self.vec[:, V_KVB:V_KVB + 16], ALU.add), mt2)
        mp.free = [mt2]
        for i, (sc, gv) in enumerate(((8, V_NORM), (32, V_NORM + 8), (56, V_KVG))):
            gst_ = Q.op("dve", lambda e, i=i, sc=sc, gv=gv: e.scalar_tensor_tensor(
                out=self.gs[:, 8 * i:8 * i + 8], in0=self.mod[:, sc:sc + 8], scalar=1.0,
                in1=self.vec[:, gv:gv + 8], op0=ALU.add, op1=ALU.mult), mt2)
        self.modtok = [mt2, gst_]
        ott = [[] for _ in range(4)]
        n = 0
        for b in range(NT):
            Wd = (b + 1) * 128
            for j in range(4):
                pts = []
                for odd in range(2):
                    hd = 2 * j + odd
                    K = (KO, LO) if odd else (KE, LE)
                    ps, t = self.logits((qh[j], ql[j]), K, b, Wd, [qt[j], ktt])
                    L = self.tmp.take()
                    t1 = T1[:, hd * 256:hd * 256 + 256]
                    near = min(Wd, 256)
                    t = Q.op("dve", lambda e, ps=ps, L=L, Wd=Wd, near=near, t1=t1: e.scalar_tensor_tensor(
                        out=L.t[:, Wd - near:Wd], in0=ps.t[:, Wd - near:Wd], scalar=0.125, in1=t1[:, 256 - near:256],
                        op0=ALU.mult, op1=ALU.add), t, L.free, t1t)
                    if Wd > near:
                        t = Q.op("dve", lambda e, ps=ps, L=L, Wd=Wd, near=near, t1=t1: e.tensor_scalar(
                            L.t[:, 0:Wd - near], ps.t[:, 0:Wd - near], 0.125, t1[:, 0:1], ALU.mult, ALU.add))
                    ps.free = [t]
                    c = (n % 8) * 4
                    n += 1
                    mx, nm, sm, rs = (self.st[:, c + i:c + i + 1] for i in range(4))
                    t = Q.op("dve", lambda e, b=b, L=L, Wd=Wd, mx=mx: e.tensor_tensor_reduce(
                        L.t[:, 0:Wd], L.t[:, 0:Wd], SM[b], 1.0, -3.0e38, ALU.add, ALU.max, mx), t, smt[b])
                    t = Q.op("dve", lambda e, mx=mx, nm=nm: e.tensor_scalar(nm, mx, -1.0, None, ALU.mult), t)
                    t = Q.op("act", lambda e, L=L, Wd=Wd, nm=nm, sm=sm: e.activation(
                        L.t[:, 0:Wd], L.t[:, 0:Wd], ACT.Exp, bias=nm, accum_out=sm), t)
                    t = Q.op("dve", lambda e, rs=rs, sm=sm: e.reciprocal(rs, sm), t)
                    t = Q.op("dve", lambda e, rs=rs, L=L, Wd=Wd: e.tensor_scalar(
                        L.t[:, 0:Wd], L.t[:, 0:Wd], rs, None, ALU.mult), t)
                    ps = self.ps.take()
                    for i in range(b + 1):
                        t = Q.op("pe", lambda e, i=i, ps=ps, L=L: e.transpose(
                            ps.t[:, i * 128:i * 128 + 128], L.t[:, i * 128:i * 128 + 128], self.ident[:, :]), t, ps.free)
                    L.free = [t]
                    PH, PL = ptb[odd]
                    t = self.split_ps(ps.t[:, 0:Wd], PH[:, 0:Wd], PL[:, 0:Wd], t, free=ptf[odd])
                    ps.free = t[1:]
                    pts.append((PH, PL, t))
                po = self.ps.take()
                for odd in range(2):
                    V = (VO, VLO) if odd else (VE, VLE)
                    PH, PL, pt = pts[odd]
                    for i in range(b + 1):
                        c = slice(i * 128, i * 128 + 128)
                        t = self.prods(po.t[:, 0:128], (V[0][:, c], V[1][:, c]), (PH[:, c], PL[:, c]),
                                       odd == 0 and i == 0, odd == 1 and i == b, [pt, po.free, vt])
                    ptf[odd] = [t]
                c = slice(b * 128, b * 128 + 128)
                t = self.split_ps(po.t[:, 0:128], oh[j][:, c], ol[j][:, c], t, free=projected)
                po.free = t[1:]
                ott[j] += t
        attended = Q.last("pe", "dve", "act")

        ch = [self.main(f"ch{j}", 16 + j, FR) for j in range(4)]
        cl = [self.main(f"cl{j}", 20 + j, FR) for j in range(4)]
        ctk = []
        for j in range(4):
            s = self.tmp.take()
            t = Q.load(s.t[:, :], cv[j * 128:j * 128 + 128, :], "ld_" + s.name, s.free, cvt[j])
            t = self.split(s.t[:, :], ch[j][:, :], cl[j][:, :], t, free=attended)
            s.free = t
            ctk.append(t)
        mtile = [24 + j for j in range(12)] + [0, 1, 2, 3]
        mh = [self.main(f"mh{j}", mtile[j], FR) for j in range(8)]
        ml = [self.main(f"ml{j}", mtile[8 + j], FR) for j in range(8)]
        mtk = []
        self.ahead = 2
        for j in range(8):
            if j % 2 == 0:
                ua = self.unit(self.w8(A["w_branch_a"][0], 128 * j, 256, nk=4))
                ub = self.unit(self.w8(A["w_branch_b"][0], 128 * j, 256, nk=4))
            ya, ta = self.gemm(ua, 4, 256, self.acts(ch, cl, ctk), col0=128 * (j % 2))
            yb, tb = self.gemm(ub, 4, 256, self.acts(oh, ol, ott), col0=128 * (j % 2))
            s, s2 = self.tmp.take(), self.tmp.take()
            t = Q.load(s.t[:, :], gd_[j * 128:j * 128 + 128, :], "ld_" + s.name, s.free, gt[j])
            t2 = Q.load(s2.t[:, :], gd_[1024 + j * 128:1024 + j * 128 + 128, :], "ld_" + s2.name, s2.free, gt[8 + j])
            t = Q.op("dve", lambda e, s=s, ya=ya: e.tensor_tensor(s.t[:, :], ya.t[:, :], s.t[:, :], ALU.mult), t, ta)
            ya.free = [t]
            t2 = Q.op("dve", lambda e, s2=s2, yb=yb: e.tensor_tensor(s2.t[:, :], yb.t[:, :], s2.t[:, :], ALU.mult), t2, tb)
            yb.free = [t2]
            t = Q.op("dve", lambda e, s=s, s2=s2: e.tensor_tensor(s.t[:, :], s.t[:, :], s2.t[:, :], ALU.add), t, t2)
            s2.free = [t]
            t = self.split(s.t[:, :], mh[j][:, :], ml[j][:, :], t, free=attended)
            s.free = t
            mtk.append(t)
        self.ahead = 3
        branched = Q.last("pe")
        xn = [self.main(f"xm{i}", 16 + i) for i in range(NT)]
        X = [self.main(f"X{j}", 8 + j) for j in range(NT)]
        for i in range(NT):
            xl = Q.load(xn[i][:, :], A["x"][0, i * 128:(i + 1) * 128, :], f"xn{i}", branched)
            xn[i] = (xn[i], xl)
        xtok = self.transposed(xn, X, branched)
        for j in range(8):
            u = self.unit(self.w8(A["w_out"][0], 128 * j))
            ps, t = self.gemm(u, 8, 128, self.acts(mh, ml, mtk))
            t = Q.op("dve", lambda e, ps=ps, j=j: e.tensor_tensor(X[j][:, :], X[j][:, :], ps.t[:, :], ALU.add), t, xtok[j])
            ps.free = [t]
            xtok[j] = [t]

        hi = [self.main(f"bh{j}", 16 + j, FR) for j in range(NT)]
        lo = [self.main(f"bl{j}", 24 + j, FR) for j in range(NT)]
        gtile = [32, 33, 34, 35, 0, 1, 2, 3, 4, 5, 6, 7]
        self.G = Ring([Slot((self.main(f"gh{i}", gtile[i], FR), self.main(f"gl{i}", gtile[6 + i], FR)), f"g{i}")
                       for i in range(6)])
        rb, rtok = self.rstd(X, xtok)
        done = Q.last("pe")
        for s in self.G.slots:
            s.free = done
        htok = self.scaled(X, xtok, rb, rtok, vec(V_GFFN), hi, lo, done)
        h = self.acts(hi, lo, htok)
        groups = [4, 4, 4, 4, 4, 2]
        base = 0
        pend = None
        for gi, gn in enumerate(groups):
            tiles = []
            for i in range(gn):
                f = base + i
                u = self.unit(self.w8(A["w_ffn_gate"][0], 128 * f))
                pg, tg = self.gemm(u, 8, 128, h)
                u = self.unit(self.w8(A["w_ffn_up"][0], 128 * f))
                pu, tu = self.gemm(u, 8, 128, h)
                tiles.append(self.glu(pg, tg, pu, tu))
                if i == 0 and pend is not None:
                    self.down(pend, A["w_ffn_down"][0], X, xtok)
            pend = (base * 128, tiles)
            base += gn
        self.down(pend, A["w_ffn_down"][0], X, xtok)

        rb, rtok = self.rstd(X, xtok)
        for j in range(8):
            xtok[j] = [Q.op("dve", lambda e, j=j, rb=rb: e.scalar_tensor_tensor(
                out=X[j][:, :], in0=X[j][:, :], scalar=vec(V_GFIN)(j), in1=rb.t[:, :], op0=ALU.mult, op1=ALU.mult),
                xtok[j], rtok)]
        rb.free = xtok[7]

        rb, rtok = self.rstd(X, xtok)
        gs = lambda i: (lambda j: self.gs[:, 8 * i + j:8 * i + j + 1])
        md = lambda c: (lambda j: self.mod[:, c + j:c + j + 1])
        htok = self.scaled(X, xtok, rb, rtok, gs(0), hi, lo, Q.last("pe"), shift=md(0))
        h = self.acts(hi, lo, htok)
        Wi = A["a_w_in_2"][0]
        pend = None
        for g in range(4):
            pt = []
            for i in range(4):
                u = self.unit(self.w8(Wi, 512 * g + 128 * i))
                ps, t = self.gemm(u, 8, 128, h)
                pt.append(self.pooled(ps, t, g))
                if i == 0 and pend is not None:
                    self.down(pend, A["a_w_out_2"][0], X, xtok, gate=md(16))
            pacts = [(s.t[0], s.t[1], t) for s, t in pt]
            tiles = []

            def gated(i, py, ty, pz, tz):
                s = self.tmp.take()
                a = Q.op("act", lambda e: e.activation(s.t[:, :], pz.t[:, :], ACT.Silu), tz, s.free)
                pz.free = [a]
                sc = vec(V_SCALE)(4 * g + i)
                a = Q.op("dve", lambda e: e.scalar_tensor_tensor(
                    out=s.t[:, :], in0=py.t[:, :], scalar=sc, in1=s.t[:, :], op0=ALU.mult, op1=ALU.mult), a, ty)
                py.free = [a]
                gslot = self.G.take()
                t = self.split(s.t[:, :], gslot.t[0][:, :], gslot.t[1][:, :], a, free=gslot.free)
                s.free = t
                tiles.append((gslot, t))

            self.ahead = 2
            held = None
            for i in range(4):
                if i % 2 == 0:
                    uy = self.unit(self.w8(A["a_w_group_2"][0, g], 128 * i, 256, nk=4))
                py, ty = self.gemm(uy, 4, 256, pacts, col0=128 * (i % 2))
                u = self.unit(self.w8(Wi, 2048 + 512 * g + 128 * i))
                if i == 3:
                    for s, _ in pt:
                        s.free = [ty]
                    gated(*held)
                pz, tz = self.gemm(u, 8, 128, h)
                if i == 2:
                    held = (i, py, ty, pz, tz)
                else:
                    gated(i, py, ty, pz, tz)
            self.ahead = 3
            pend = (512 * g, tiles)
        self.down(pend, A["a_w_out_2"][0], X, xtok, gate=md(16))

        rb, rtok = self.rstd(X, xtok)
        htok = self.scaled(X, xtok, rb, rtok, gs(2), hi, lo, Q.last("pe"), shift=md(48))
        h = self.acts(hi, lo, htok)
        kx0, kx1, vt_ = self.main("kx0", 4), self.main("kx1", 33), self.main("vt", 34)
        pooled_done = Q.last("pe")
        u = self.unit(self.w8(A["w_kv_2"], 0))
        ps, t = self.gemm(u, 8, 128, h)
        t1 = Q.op("act", lambda e, ps=ps: e.activation(kx0[0:64, :], ps.t[0:64, :], ACT.Copy), t, pooled_done)
        t1 = Q.op("act", lambda e, ps=ps: e.activation(kx1[64:128, :], ps.t[64:128, :], ACT.Copy), t, pooled_done)
        ps.free = [t1]
        k0t = Q.load(kx0[64:128, :], kx0[0:64, :], "kx0", t1)
        k1t = Q.load(kx1[0:64, :], kx1[64:128, :], "kx1", t1)
        u = self.unit(self.w8(A["w_kv_2"], 128))
        ps, t = self.gemm(u, 8, 128, h)
        vtt = Q.op("act", lambda e, ps=ps: e.activation(vt_[:, :], ps.t[:, :], ACT.Copy), t, pooled_done)
        ps.free = [vtt]
        kv_done = Q.last("pe")
        htok = self.scaled(X, xtok, rb, rtok, gs(1), hi, lo, kv_done, shift=md(24))
        h = self.acts(hi, lo, htok)
        xs = self.dram("xs", [S, S])
        xst = [Q.load(xs[j * 128:j * 128 + 128, :], X[j][:, :], f"xs{j}", xtok[j]) for j in range(8)]
        qd = self.dram("qd", [2048, S])
        qdt = []
        for j in range(16):
            u = self.unit(self.w8(A["b_w_in_2"][0], 128 * j))
            ps, t = self.gemm(u, 8, 128, h)
            s = self.tmp.take()
            if j < 8:
                t = Q.op("act", lambda e, ps=ps, s=s: e.activation(s.t[:, :], ps.t[:, :], ACT.Copy, scale=0.125), t, s.free)
            else:
                t = Q.op("act", lambda e, ps=ps, s=s: e.activation(s.t[:, :], ps.t[:, :], ACT.Silu), t, s.free)
            ps.free = [t]
            qdt.append(Q.load(qd[j * 128:j * 128 + 128, :], s.t[:, :], "st_" + s.name, t))
            s.free = [qdt[-1]]
        qz_done = [Q.last("pe", "dve", "act"), xst, htok]
        KP = [self.main(f"k2p{i}", 16 + i, FR) for i in range(4)]
        VP = [self.main(f"v2p{i}", 20 + i, FR) for i in range(4)]
        T2 = self.main("t2", 24, cols=2048)
        ptb = [(self.main(f"p2h{i}", 26 + i, FR), self.main(f"p2l{i}", 28 + i, FR)) for i in range(2)]
        ptf = [qz_done, qz_done]
        qtile = [30, 31, 35, 0]
        qb = [(self.main(f"q2h{i}", qtile[i], FR), self.main(f"q2l{i}", qtile[2 + i], FR)) for i in range(2)]
        qf = [qz_done, qz_done]
        otile = [5, 1, 2, 3, 6, 7, 8, 9, 10, 11, 12, 13, 14, 15, 32, 4]
        oh = [self.main(f"o2h{j}", otile[j], FR) for j in range(8)]
        ol = [self.main(f"o2l{j}", otile[8 + j], FR) for j in range(8)]
        ott = [[] for _ in range(8)]
        zz = self.zero_pads([(KP[0], 64), (KP[1], 64), (KP[2], 0), (KP[3], 0)], qz_done)
        zv = self.zero_v([(VP[0], 64), (VP[1], 64), (VP[2], 0), (VP[3], 0)], qz_done)
        n = 0
        prev = qz_done
        for j in range(8):
            kvh = j // 4
            if j % 4 == 0:
                kx, kxt = ((kx0, [k0t, t1]), (kx1, [k1t, t1]))[kvh]
                kpt = []
                for half, (H, Lw) in ((0, (KP[0], KP[1])), (64, (KP[2], KP[3]))):
                    sl = slice(half, half + 64)
                    kpt += self.split(kx[sl, :], H[sl, :], Lw[sl, :], kxt, zz, free=prev, eng="dve")
                vpt = self.v_pads(vt_, VP, 64 * kvh, 128, [vtt, zv, prev])
                t2t = self.table(T2, gd, 8 + 8 * kvh, f"t2{kvh}", [gst, prev])
                T2v = T2[:, :].rearrange("p (h c) -> p h c", h=8)
                t2t = Q.op("pool", lambda e, T2v=T2v: e.affine_select(
                    out=T2v, in_=T2v, compare_op=ALU.is_ge, fill=NEG, base=128,
                    pattern=[[0, 8], [-1, 256]], channel_multiplier=1), t2t)
                t2t = Q.op("pool", lambda e, T2v=T2v: e.affine_select(
                    out=T2v, in_=T2v, compare_op=ALU.is_gt, fill=NEG, base=0,
                    pattern=[[0, 8], [1, 256]], channel_multiplier=-1), t2t)
            s = self.tmp.take()
            t = Q.load(s.t[:, :], qd[j * 128:j * 128 + 128, :], "ld_" + s.name, s.free, qdt[j])
            QH, QL = qb[j % 2]
            qt = self.split(s.t[:, :], QH[:, :], QL[:, :], t, free=qf[j % 2])
            s.free = qt
            z = self.tmp.take()
            zt = Q.load(z.t[:, :], qd[1024 + j * 128:1024 + j * 128 + 128, :], "ld_" + z.name, z.free, qdt[8 + j])
            po = None
            for hb in range(2):
                pts = []
                for odd in range(2):
                    hl = (2 * j + odd) % 8
                    K = (KP[2], KP[3]) if odd else (KP[0], KP[1])
                    ps = self.ps.take()
                    for i in range(4):
                        blk = 4 * hb + i
                        c = slice(blk * 128, blk * 128 + 128)
                        if blk == 0:
                            for w in range(2):
                                t = self.prods(ps.t[:, w * 128:w * 128 + 128], (QH[:, c], QL[:, c]),
                                               (K[0][:, 0:128], K[1][:, 0:128]), True, True, [qt, kpt, ps.free])
                        else:
                            k_ = slice(blk * 128 - 128, blk * 128 + 128)
                            t = self.prods(ps.t[:, i * 256:i * 256 + 256], (QH[:, c], QL[:, c]),
                                           (K[0][:, k_], K[1][:, k_]), True, True, [qt, kpt, ps.free])
                    L = self.tmp.take()
                    if L is z:
                        L = self.tmp.take()
                    L3 = L.t[:, :].rearrange("p (b c) -> p b c", b=4)
                    t = Q.op("dve", lambda e, ps=ps, L3=L3, hl=hl: e.tensor_tensor(
                        L3, ps.t[:, :].rearrange("p (b c) -> p b c", b=4),
                        T2[:, hl * 256:hl * 256 + 256].unsqueeze(1).to_broadcast([128, 4, 256]), ALU.add), t, L.free, t2t)
                    ps.free = [t]
                    if hb == 0:
                        t = Q.op("dve", lambda e, L=L: e.memset(L.t[:, 0:128], NEG), t)
                    c = (n % 4) * 32
                    n += 1
                    mx, mm, sm, es, dn, rd = (self.st[:, c + 4 * i:c + 4 * i + 4] for i in range(6))
                    sk = self.sk[:, 2 * j + odd:2 * j + odd + 1]
                    t = Q.op("dve", lambda e, L3=L3, mx=mx: e.tensor_reduce(mx, L3, AXX, ALU.max), t)
                    t = Q.op("dve", lambda e, mx=mx, mm=mm, sk=sk: e.tensor_scalar(mm, mx, sk, None, ALU.max), t)
                    t2 = Q.op("dve", lambda e, mm=mm, es=es, sk=sk: e.tensor_scalar(es, mm, -1.0, sk, ALU.mult, ALU.add), t)
                    t2 = Q.op("act", lambda e, es=es: e.activation(es, es, ACT.Exp), t2)
                    t = Q.op("pool", lambda e, L3=L3, mm=mm: e.tensor_tensor(
                        L3, L3, mm.unsqueeze(2).to_broadcast([128, 4, 256]), ALU.subtract), t)
                    t = Q.op("act", lambda e, L=L: e.activation(L.t[:, :], L.t[:, :], ACT.Exp), t)
                    t = Q.op("dve", lambda e, L3=L3, sm=sm: e.tensor_reduce(sm, L3, AXX, ALU.add), t)
                    t = Q.op("dve", lambda e, sm=sm, es=es, dn=dn: e.tensor_tensor(dn, sm, es, ALU.add), t, t2)
                    t = Q.op("dve", lambda e, dn=dn, rd=rd: e.reciprocal(rd, dn), t)
                    t = Q.op("pool", lambda e, L3=L3, rd=rd: e.tensor_tensor(
                        L3, L3, rd.unsqueeze(2).to_broadcast([128, 4, 256]), ALU.mult), t)
                    ps = self.ps.take()
                    for i in range(8):
                        t = Q.op("pe", lambda e, i=i, ps=ps, L=L: e.transpose(
                            ps.t[:, i * 128:i * 128 + 128], L.t[:, i * 128:i * 128 + 128], self.ident[:, :]), t, ps.free)
                    L.free = [t]
                    PH, PL = ptb[odd]
                    t = self.split_ps(ps.t[:, :], PH[:, :], PL[:, :], t, free=ptf[odd])
                    ps.free = t[1:]
                    pts.append((PH, PL, t))
                po = self.ps.take()
                for i in range(4):
                    blk = 4 * hb + i
                    items = [(odd, w) for odd in range(2) for w in range(2) if not (blk == 0 and w == 0)]
                    for x, (odd, w) in enumerate(items):
                        V = (VP[2], VP[3]) if odd else (VP[0], VP[1])
                        PH, PL, pt = pts[odd]
                        sv = slice((blk - 1 + w) * 128, (blk + w) * 128)
                        pc = slice(i * 256 + w * 128, i * 256 + w * 128 + 128)
                        t = self.prods(po.t[:, i * 128:i * 128 + 128], (V[0][:, sv], V[1][:, sv]), (PH[:, pc], PL[:, pc]),
                                       x == 0, x == len(items) - 1, [pt, po.free, vpt])
                ptf = [[t], [t]]
                hs = slice(hb * 512, hb * 512 + 512)
                t = Q.op("dve", lambda e, z=z, po=po, hs=hs: e.tensor_tensor(z.t[:, hs], z.t[:, hs], po.t[:, 0:512], ALU.mult), t, zt)
                po.free = [t]
                t = self.split(z.t[:, hs], oh[j][:, hs], ol[j][:, hs], t, free=[qz_done, kpt if j == 7 else None])
                ott[j] += t
            z.free = t
            qf[j % 2] = Q.last("pe")
            prev = Q.last("pe", "dve")
        att_done = Q.last("pe", "dve", "act", "pool")
        X = [self.main(f"Y{j}", 16 + j) for j in range(NT)]
        xtok = []
        for j in range(8):
            u = self.unit(self.w8(A["b_w_out_2"][0], 128 * j))
            ps, t = self.gemm(u, 8, 128, self.acts(oh, ol, ott))
            xl = Q.load(X[j][:, :], xs[j * 128:j * 128 + 128, :], f"xs{j}", att_done, xst[j])
            t = Q.op("dve", lambda e, ps=ps, j=j: e.scalar_tensor_tensor(
                out=X[j][:, :], in0=ps.t[:, :], scalar=md(40)(j), in1=X[j][:, :], op0=ALU.mult, op1=ALU.add), t, xl)
            ps.free = [t]
            xtok.append([t])
        rb, rtok = self.rstd(X, xtok)
        for j in range(8):
            xtok[j] = [Q.op("dve", lambda e, j=j, rb=rb: e.scalar_tensor_tensor(
                out=X[j][:, :], in0=X[j][:, :], scalar=vec(V_FIN2)(j), in1=rb.t[:, :], op0=ALU.mult, op1=ALU.mult),
                xtok[j], rtok)]
        rb.free = xtok[7]
        for i in range(NT):
            ps = self.ps.take()
            for j in range(NT):
                t = Q.op("pe", lambda e, i=i, j=j, ps=ps: e.transpose(
                    ps.t[:, j * 128:j * 128 + 128], X[j][:, i * 128:i * 128 + 128], self.ident[:, :]), xtok[j], ps.free)
            ps.free = []
            s = self.tmp.take()
            t = Q.op("act" if i % 2 else "dve", (lambda e, s=s, ps=ps: e.activation(s.t[:, :], ps.t[:, :], ACT.Copy)) if i % 2 else
                     (lambda e, s=s, ps=ps: e.tensor_copy(s.t[:, :], ps.t[:, :])), t, s.free)
            ps.free = [t]
            s.free = [Q.load(self.out[0, i * 128:(i + 1) * 128, :], s.t[:, :], "st_" + s.name, t)]

    def transposed(self, xn, X, free):
        toks = []
        for j in range(NT):
            ps = self.ps.take()
            for i in range(NT):
                t = self.Q.op("pe", lambda e, i=i, j=j, ps=ps: e.transpose(
                    ps.t[:, i * 128:i * 128 + 128], xn[i][0][:, j * 128:j * 128 + 128], self.ident[:, :]),
                    xn[i][1], ps.free, self.ctok)
            a = self.Q.op("act", lambda e, j=j, ps=ps: e.activation(X[j][:, :], ps.t[:, :], ACT.Copy), t, free)
            ps.free = [a]
            toks.append([a])
        return toks

    def zero_pads(self, pads, after):
        return [self.Q.op("dve", lambda e, p=p, h=h: e.memset(p[h:h + 64, :].bitcast(F32), 0.0), after)
                for p, h in pads]

    def zero_v(self, pads, after):
        return [self.Q.op("pool", lambda e, p=p, h=h: e.memset(
            p[:, :].rearrange("p (i c) -> p i c", c=128)[:, :, h:h + 64].bitcast(F32), 0.0), after)
            for p, h in pads]

    def k_pads(self, kt, kt2, pads, after, sem, free):
        KE, LE, KO, LO = pads
        d = self.Q.load(kt2[64:128, :], kt[0:64, :], sem, after)
        a = self.split(kt[0:64, :], KE[0:64, :], LE[0:64, :], after, free=free, eng="dve")
        b = self.split(kt2[64:128, :], KO[64:128, :], LO[64:128, :], d, after, free=free, eng="dve")
        return [a, b]

    def v_pads(self, src, pads, row, n, after):
        VE, VLE, VO, VLO = pads
        ps = self.ps.take()
        for i in range(NT):
            t = self.Q.op("pe", lambda e, i=i, ps=ps: e.transpose(
                ps.t[:, i * 128:i * 128 + 128], src[:, i * 128:i * 128 + 128], self.ident[:, :]), after, ps.free)
        v = ps.t[:, :].rearrange("p (i c) -> p i c", c=128)[:, :, row:row + 64]
        out = []
        for H, L, c in ((VE, VLE, 0), (VO, VLO, 64)):
            h = H[:, :].rearrange("p (i c) -> p i c", c=128)[:, :, c:c + 64]
            l = L[:, :].rearrange("p (i c) -> p i c", c=128)[:, :, c:c + 64]
            t = self.Q.op("act", lambda e, h=h: e.activation(h, v, ACT.Copy), t, after)
            t = self.Q.op("dve", lambda e, h=h, l=l: e.tensor_tensor(l, v, h.bitcast(F32), ALU.subtract), t)
            out.append(t)
        ps.free = [t]
        return out

    def table(self, Tt, gd, h0, sem, after):
        Q = self.Q
        src = bass.AP(gd.tensor, gd.offset + h0 * 384, [[1, 128], [384, 8], [1, 256]])
        t = Q.load(Tt[:, :].rearrange("p (h c) -> p h c", h=8), src, sem, after)
        toks = []
        for i in range(2):
            ps = self.ps.take()
            for h in range(2):
                c = i * 1024 + h * 512
                m = Q.op("pe", lambda e, ps=ps, h=h, c=c: e.matmul(
                    ps.t[:, h * 512:h * 512 + 512], self.flip[:, :], Tt[:, c:c + 512], start=True, stop=True), t, ps.free)
            a = Q.op("act", lambda e, ps=ps, i=i: e.activation(
                Tt[:, i * 1024:i * 1024 + 1024], ps.t[:, :], ACT.Copy), m)
            ps.free = [a]
            toks.append(a)
        return toks

    def logits(self, q, K, b, Wd, after):
        ps = self.ps.take()
        c = slice(b * 128, b * 128 + 128)
        for s0 in range(0, Wd, 512):
            s1 = min(s0 + 512, Wd)
            t = self.prods(ps.t[:, s0:s1], (q[0][:, c], q[1][:, c]), (K[0][:, s0:s1], K[1][:, s0:s1]),
                           True, True, [after, ps.free])
        ps.free = []
        return ps, t

    def glu(self, pg, tg, pu, tu):
        Q = self.Q
        s = self.tmp.take()
        a = Q.op("act", lambda e: e.activation(s.t[:, :], pg.t[:, :], ACT.Silu), tg, s.free)
        pg.free = [a]
        a = Q.op("dve", lambda e: e.tensor_tensor(s.t[:, :], s.t[:, :], pu.t[:, :], ALU.mult), a, tu)
        pu.free = [a]
        g = self.G.take()
        t = self.split(s.t[:, :], g.t[0][:, :], g.t[1][:, :], a, free=g.free)
        s.free = t
        return g, t

    def pooled(self, ps, t, g):
        Q, w = self.Q, 2 << g
        u, a, b = self.tmp.take(), self.tmp.take(), self.tmp.take()
        tu = Q.op("act", lambda e: e.activation(u.t[:, :], ps.t[:, :], ACT.Copy), t, u.free)
        ps.free = [tu]
        src, t = u, tu
        k = 1
        while k < w:
            dst = a if src is not a else b
            t1 = Q.op("dve", lambda e, s=src, d=dst, k=k: e.tensor_tensor(
                d.t[:, k:S], s.t[:, k:S], s.t[:, 0:S - k], ALU.add), t, dst.free)
            t2 = Q.op("dve", lambda e, s=src, d=dst, k=k: e.tensor_copy(d.t[:, 0:k], s.t[:, 0:k]), t, dst.free)
            dst.free = []
            t, src, k = [t1, t2], dst, 2 * k
        inv = self.invc[:, 16 * g:16 * g + 16]
        t = Q.op("dve", lambda e, s=src: e.tensor_tensor(s.t[:, 0:16], s.t[:, 0:16], inv, ALU.mult), t)
        t = Q.op("dve", lambda e, s=src: e.scalar_tensor_tensor(
            out=u.t[:, :], in0=s.t[:, :], scalar=1.0 / w, in1=u.t[:, :], op0=ALU.mult, op1=ALU.subtract), t)
        gs = self.G.take()
        t2 = self.split(u.t[:, :], gs.t[0][:, :], gs.t[1][:, :], t, free=gs.free)
        u.free, a.free, b.free = t2, [t], [t]
        return gs, t2

    def down(self, pend, W, X, xtok, gate=None):
        r0, tiles = pend
        nk = len(tiles)
        n = 1024 // nk
        acts = [(g.t[0], g.t[1], t) for g, t in tiles]
        for j in range(8):
            if (128 * j) % n == 0:
                u = self.unit(self.w8(W, 128 * j, n, k0=r0, nk=nk))
            ps, t = self.gemm(u, nk, n, acts, col0=(128 * j) % n)
            if gate is None:
                a = self.Q.op("dve", lambda e, ps=ps, j=j: e.tensor_tensor(
                    X[j][:, :], X[j][:, :], ps.t[:, :], ALU.add), t, xtok[j])
            else:
                a = self.Q.op("dve", lambda e, ps=ps, j=j: e.scalar_tensor_tensor(
                    out=X[j][:, :], in0=ps.t[:, :], scalar=gate(j), in1=X[j][:, :], op0=ALU.mult, op1=ALU.add),
                    t, xtok[j], self.modtok)
            ps.free = [a]
            xtok[j] = [a]
        for g, _ in tiles:
            g.free = [t]


def program(nc, A, out, consts):
    mem = {}
    draft = Net(nc, A, out, consts, None, mem)
    draft.build()
    net = Net(nc, A, out, consts, draft.units, mem)
    net.build()
    with ExitStack() as ctx:
        net.Q.emit(nc, ctx)


def constants():
    dist = np.maximum(255 - np.arange(384), 0)
    large = 16 + (np.log(np.maximum(dist, 1).astype(np.float32) / np.float32(16)) / np.float32(np.log(8.0))
                  * np.float32(16)).astype(np.int32)
    bucket = np.where(dist < 16, dist, np.minimum(large, 31))
    oneh = (np.arange(32)[:, None] == bucket[None, :]).astype(np.float32)
    t = np.arange(16)
    invc = np.stack([w / np.minimum(t + 1, w) for w in (2, 4, 8, 16)]).astype(np.float32).reshape(1, 64)
    return {"ident": np.eye(128, dtype=np.float32), "flip": np.eye(128, dtype=np.float32)[::-1].copy(), "oneh": oneh, "invc": invc}


_INS = ["x", "g_mix", "w_in", "b_gate", "conv_w", "w_branch_a", "w_branch_b", "w_out", "rel_bias", "g_ffn",
        "w_ffn_gate", "w_ffn_up", "w_ffn_down", "g_final", "c_2", "norm_g_2", "ada_w_2", "ada_b_2", "a_w_in_2",
        "a_w_group_2", "a_scale_2", "a_w_out_2", "kv_norm_g_2", "kv_ada_w_2", "kv_ada_b_2", "w_kv_2", "b_w_in_2",
        "b_sinks_2", "b_w_out_2", "rel_bias_2", "final_g_2"]


def kernel(**inputs):
    import concourse.bacc as _bacc
    from concourse.bass_utils import run_bass_kernel_spmd as _run

    nc = _bacc.Bacc("TRN2", target_bir_lowering=False, num_devices=1)
    arrays, A, C = {}, {}, {}
    for name in _INS:
        a = np.ascontiguousarray(inputs[name])
        arrays[f"in_{name}"] = a
        A[name] = nc.dram_tensor(f"in_{name}", a.shape, F32, kind="ExternalInput").ap()
    for name, a in constants().items():
        arrays[f"c_{name}"] = a
        C[name] = nc.dram_tensor(f"c_{name}", a.shape, F32, kind="ExternalInput").ap()
    out = nc.dram_tensor("out_0", (1, S, 1024), F32, kind="ExternalOutput").ap()
    program(nc, A, out, C)
    r = _run(nc, [arrays], core_ids=[0])
    return r.results[0]["out_0"]
```

```python
from contextlib import ExitStack

import numpy as np

import concourse.bass as bass
from concourse import mybir

F32 = mybir.dt.float32
FR = mybir.dt.float32r
ALU = mybir.AluOpType
ACT = mybir.ActivationFunctionType
AXX = mybir.AxisListType.X

S = 1024
NT = 8
DFF = 2816
T = 4096
BASE = 16640
MAIN = 15
NEG = -1.0e30
FUT = -3.0e38
GONE = -3.3e38

C_B, C_C, C_X, C_Q, C_KV, C_IQ, C_IK, C_GA, C_GB = 0, 512, 1024, 1536, 2048, 2176, 2688, 2760, 3784

V_GMIX, V_GFFN, V_GFIN, V_NORM, V_ADAB, V_KVG, V_KVB, V_SCALE, V_GATE, V_CONV, V_C, V_FIN2 = (
    0, 8, 16, 24, 40, 88, 96, 112, 128, 144, 156, 164)
V_ALL = 172


class Tok:

    __slots__ = ("eng", "idx", "sem", "val", "needed")

    def __init__(self, eng=None, idx=None, sem=None, val=None):
        self.eng, self.idx, self.sem, self.val, self.needed = eng, idx, sem, val, False


class Later:

    def matmul(self, *a, **k):
        return lambda e: e.matmul(*a, **k)

    def transpose(self, *a, **k):
        return lambda e: e.transpose(*a, **k)

    def activation(self, *a, **k):
        return lambda e: e.activation(*a, **k)

    def tensor_tensor(self, *a, **k):
        return lambda e: e.tensor_tensor(*a, **k)

    def scalar_tensor_tensor(self, *a, **k):
        return lambda e: e.scalar_tensor_tensor(*a, **k)

    def tensor_scalar(self, *a, **k):
        return lambda e: e.tensor_scalar(*a, **k)

    def tensor_copy(self, *a, **k):
        return lambda e: e.tensor_copy(*a, **k)

    def reciprocal(self, *a, **k):
        return lambda e: e.reciprocal(*a, **k)

    def memset(self, *a, **k):
        return lambda e: e.memset(*a, **k)

    def affine_select(self, *a, **k):
        return lambda e: e.affine_select(*a, **k)

    def max(self, *a, **k):
        return lambda e: e.max(*a, **k)

    def match_replace(self, *a, **k):
        return lambda e: e.match_replace(*a, **k)

    def tensor_tensor_reduce(self, *a, **k):
        return lambda e: e.tensor_tensor_reduce(*a, **k)

    def tensor_reduce(self, *a, **k):
        return lambda e: e.tensor_reduce(*a, **k)


LATER = Later()


class Queues:

    def __init__(self):
        self.q = {e: [] for e in ("pe", "act", "dve", "pool", "sp")}
        self.dma = {}

    def op(self, eng, fn, *after):
        fn = fn(LATER)
        t = Tok(eng, len(self.q[eng]))
        self.q[eng].append((fn, flat(after), t, None))
        return t

    def load(self, out, in_, sem, *after, eng="sp"):
        self.dma[sem] = self.dma.get(sem, 0) + 16
        t = Tok(sem=sem, val=self.dma[sem])
        self.q[eng].append((lambda e: e.dma_start(out, in_), flat(after), t, sem))
        return t

    def last(self, *engs):
        return [self.q[e][-1][2] for e in engs if self.q[e]]

    def emit(self, nc, ctx):
        for q in self.q.values():
            for _, after, _, _ in q:
                for t in after:
                    t.needed = True
        sems = {e: ctx.enter_context(nc.semaphore("s_" + e)) for e in self.q}
        sems.update({d: ctx.enter_context(nc.semaphore("d_" + d)) for d in self.dma})
        for e, q in self.q.items():
            n = 0
            for _, _, t, sem in q:
                if sem is None and t.needed:
                    n += 1
                    t.sem, t.val = e, n
        block = ctx.enter_context(nc.Block())
        ends = dict(self.dma)

        def run(e, name):
            seen = {}
            for fn, after, t, sem in self.q[name]:
                for a in after:
                    if seen.get(a.sem, 0) < a.val:
                        e.wait_ge(sems[a.sem], a.val)
                        seen[a.sem] = a.val
                ins = fn(e)
                if sem is not None:
                    ins.then_inc(sems[sem], 16)
                elif t.needed:
                    ins.then_inc(sems[name], 1)
            if name == "sp":
                for d, v in ends.items():
                    e.wait_ge(sems[d], v)

        @block.sync
        def _(e):
            run(e, "sp")

        @block.tensor
        def _(e):
            run(e, "pe")

        @block.scalar
        def _(e):
            run(e, "act")

        @block.vector
        def _(e):
            run(e, "dve")

        @block.gpsimd
        def _(e):
            run(e, "pool")


def flat(x):
    out = []
    for a in x:
        if a is None:
            continue
        if isinstance(a, (list, tuple)):
            out += flat(a)
        else:
            out.append(a)
    return out


class Slot:

    def __init__(self, t, name):
        self.t, self.name, self.free = t, name, []


class Ring:
    def __init__(self, slots):
        self.slots, self.n = slots, 0

    def take(self):
        s = self.slots[self.n % len(self.slots)]
        self.n += 1
        return s


class Net:
    def __init__(self, nc, A, out, consts, plan, mem):
        self.nc, self.A, self.out, self.C, self.plan, self.mem = nc, A, out, consts, plan, mem
        self.Q = Queues()
        self.units = []
        self.n_dma = self.n_split = 0
        self.split_no = 0
        self.lo_eng = "pool"
        self.ahead = 3
        self.ada_n = None

    def at(self, name, tile, cols=S, dt=F32, off=0, parts=128):
        key = (name, tile, dt)
        if key not in self.mem:
            self.mem[key] = self.nc.alloc_sbuf_tensor_at(
                name, [parts, cols], dt, offset=BASE + tile * T + off)
        return self.mem[key]

    def main(self, name, i, dt=F32, cols=S, off=0):
        return self.at(name, MAIN + i, cols, dt, off)

    def dram(self, name, shape):
        if name not in self.mem:
            self.mem[name] = self.nc.dram_tensor(name, shape, F32)
        return self.mem[name].ap()

    def setup(self):
        self.raw = [Slot(self.at(f"raw{i}", i), f"raw{i}") for i in range(3)]
        self.wh = [Slot(self.at(f"wh{i}", 3 + i, dt=FR), f"wh{i}") for i in range(3)]
        self.wl = [Slot(self.at(f"wl{i}", 6 + i, dt=FR), f"wl{i}") for i in range(3)]
        self.tmp = Ring([Slot(self.at(f"tmp{i}", 10 + i), f"tmp{i}") for i in range(5)])
        if "ps" not in self.mem:
            self.mem["ps"] = [self.nc.alloc_psum_tensor(f"ps{i}", [128, S], F32) for i in range(4)]
        self.ps = Ring([Slot(t, f"ps{i}") for i, t in enumerate(self.mem["ps"])])
        o = [0]

        def small(name, cols):
            t = self.at(name, 9, cols, off=o[0])
            o[0] += -(-4 * cols // 32) * 32
            return t

        self.ident = small("ident", 128)
        self.ones = small("ones", 128)
        self.flip = small("flip", 128)
        self.vec = small("vec", V_ALL)
        self.mod = small("mod", 64)
        self.gs = small("gs", 24)
        self.iw = small("iw", 64)
        self.cact = small("cact", 8)
        self.r8 = small("r8", 16)
        self.eps = small("eps", 1)
        self.st = small("st", 128)
        self.m8 = small("m8", 16)
        self.sk = small("sk", 16)
        self.invc = small("invc", 16 * 4)
        assert o[0] <= T, o[0]
        self.oneh = self.at("oneh", 51, 384, parts=32)
        self.rel = self.at("rel", 51, 24, off=1536, parts=32)
        self.gb = self.at("gbias", 51, 384, off=2048, parts=32)

    def issue_dma(self, j):
        parts, _ = self.plan[j]
        slot = self.raw[j % 3]
        for view, src in parts:
            t = self.Q.load(view(slot.t), src, f"raw{j % 3}", slot.free)
        slot.free = []
        self.loaded[j] = t

    def issue_split(self, j):
        _, cols = self.plan[j]
        raw = self.raw[j % 3]
        wh, wl = self.wh[self.n_w % 3], self.wl[self.n_w % 3]
        self.n_w += 1
        v, h, lo = raw.t[:, 0:cols], wh.t[:, 0:cols], wl.t[:, 0:cols]
        a = self.Q.op("act", lambda e: e.activation(h, v, ACT.Copy), self.loaded[j], wh.free)
        eng = self.lo_eng
        b = self.Q.op(eng, lambda e: e.tensor_tensor(lo, v, h.bitcast(F32), ALU.subtract), a, wl.free)
        wh.free, wl.free, raw.free = [], [], [a, b]
        self.ready[j] = (wh, wl, [a, b])

    def unit(self, parts, cols=S):
        self.units.append((parts, cols))
        i = len(self.units) - 1
        if self.plan is None:
            return self.wh[0], self.wl[0], []
        while self.n_split < min(i + self.ahead, len(self.plan)) or self.n_dma < min(i + 4, len(self.plan)):
            if self.n_dma < len(self.plan) and self.n_dma < self.n_split + 3:
                self.issue_dma(self.n_dma)
                self.n_dma += 1
                continue
            if self.n_split < min(i + self.ahead, self.n_dma):
                self.issue_split(self.n_split)
                self.n_split += 1
                continue
            break
        return self.ready[i]

    def w8(self, w, c0, n=128, k0=0, nk=8):
        src = w[k0:k0 + nk * 128, c0:c0 + n].rearrange("(k p) n -> p k n", p=128)
        return [(lambda t: t[:, 0:nk * n].rearrange("p (k n) -> p k n", k=nk), src)]

    def gemm(self, unit, nk, n, acts, col0=0, m=128):
        wh, wl, toks = unit
        ps = self.ps.take()
        WH = wh.t[:, 0:nk * n].rearrange("p (k n) -> p k n", k=nk)
        WL = wl.t[:, 0:nk * n].rearrange("p (k n) -> p k n", k=nk)
        first = list(toks) + list(ps.free)
        ps.free = []
        for k in range(nk):
            hi, lo, atok = acts[k]
            wk, lk = WH[:, k, col0:col0 + m], WL[:, k, col0:col0 + m]
            seq = [(wk, hi, 0), (wk, hi, 1), (wk, lo, 0), (wk, lo, 1), (lk, hi, 0), (lk, hi, 1)]
            for i, (w, a, h) in enumerate(seq):
                o, r = ps.t[0:m, h * 512:h * 512 + 512], a[:, h * 512:h * 512 + 512]
                t = self.Q.op("pe", lambda e, o=o, w=w, r=r, s=(k == 0 and i < 2), z=(k == nk - 1 and i >= 4):
                              e.matmul(o, w, r, start=s, stop=z), first, atok if i == 0 else None)
                first = []
        wh.free = wl.free = [t]
        if self.ada_n is not None and self.ada_n < 64:
            self.ada_step()
        return ps, t

    def ada_start(self, bufs, free, ready):
        self.ada = [Slot(t, f"ada{i}") for i, t in enumerate(bufs)]
        for s in self.ada:
            s.free = free
        self.ada_n, self.ada_ready, self.adal = 0, ready, []
        self.acc4, self.acc4_free = self.at("acc4", 51, 512), free
        for c in range(len(bufs)):
            self.ada_load(c)

    def ada_load(self, c):
        A = self.A
        w, col = ((A["ada_w_2"][0], c), (A["ada_w_2"][1], c - 24), (A["kv_ada_w_2"], c - 48))[min(c // 24, 2)]
        s = self.ada[c % len(self.ada)]
        (view, src), = self.w8(w, 128 * col)
        self.adal.append(self.Q.load(view(s.t), src, s.name, s.free))

    def ada_step(self):
        Q, c = self.Q, self.ada_n
        self.ada_n += 1
        s = self.ada[c % len(self.ada)]
        v = s.t[:, :].rearrange("p (k n) -> p k n", k=8)
        t = Q.op("dve", lambda e: e.tensor_tensor(
            v, v, self.cact[:, :].unsqueeze(2).to_broadcast([128, 8, 128]), ALU.mult), self.adal[c], self.ada_ready)
        o = self.acc4[:, (c % 4) * 128:(c % 4) * 128 + 128]
        t = Q.op("dve", lambda e: e.tensor_reduce(o, s.t[:, :].rearrange("p (k n) -> p n k", k=8), AXX, ALU.add),
                 t, self.acc4_free)
        s.free = [t]
        if c + len(self.ada) < 64:
            self.ada_load(c + len(self.ada))
        if c % 4 == 3:
            ps = self.ps.take()
            for i in range(4):
                m = Q.op("pe", lambda e: e.matmul(ps.t[:, i:i + 1], self.acc4[:, i * 128:i * 128 + 128],
                                                  self.ones[:, 0:1], start=True, stop=True), t, ps.free)
            self.acc4_free = [m]
            b = (V_ADAB if c < 48 else V_KVB - 48) + c - 3
            self.adat = Q.op("dve", lambda e: e.tensor_tensor(
                self.mod[:, c - 3:c + 1], ps.t[:, 0:4], self.vec[:, b:b + 4], ALU.add), m)
            ps.free = [self.adat]

    def split(self, src, hi, lo, *after, free=(), eng=None):
        a = self.Q.op("act", lambda e: e.activation(hi, src, ACT.Copy), after, free)
        b = self.Q.op(eng or self.lo_eng, lambda e: e.tensor_tensor(lo, src, hi.bitcast(F32), ALU.subtract),
                      a, after, free)
        return [a, b]

    def split_ps(self, src, hi, lo, *after, scale=1.0, free=()):
        a = self.Q.op("act", lambda e: e.activation(hi, src, ACT.Copy, scale=scale), after, free)
        b = self.Q.op("dve", lambda e: e.scalar_tensor_tensor(
            out=lo, in0=src, scalar=scale, in1=hi.bitcast(F32), op0=ALU.mult, op1=ALU.subtract), a, free)
        return [a, b]

    def prods(self, o, L, R, first, last, after):
        seq = [(L[0], R[0]), (L[0], R[1]), (L[1], R[0])]
        for i, (a, b) in enumerate(seq):
            t = self.Q.op("pe", lambda e, a=a, b=b, s=(first and i == 0), z=(last and i == 2):
                          e.matmul(o, a, b, start=s, stop=z), after if i == 0 else None)
        return t

    def rstd(self, X, xtok):
        Q = self.Q
        acc = self.tmp.take()
        at = None
        for j in range(NT):
            if j == 0:
                at = Q.op("act", lambda e, x=X[0]: e.activation(acc.t[:, :], x[:, :], ACT.Square),
                          xtok[0], acc.free)
            else:
                s = self.tmp.take()
                if s is acc:
                    s = self.tmp.take()
                a = Q.op("act", lambda e, x=X[j], s=s: e.activation(s.t[:, :], x[:, :], ACT.Square),
                         xtok[j], s.free)
                at = Q.op("dve", lambda e, s=s: e.tensor_tensor(acc.t[:, :], acc.t[:, :], s.t[:, :], ALU.add),
                          a, at)
                s.free = [at]
        ps = self.ps.take()
        for t in range(NT):
            m = Q.op("pe", lambda e, t=t: e.matmul(ps.t[:, t:t + 1], acc.t[:, t * 128:t * 128 + 128],
                                                   self.ones[:, 0:1], start=True, stop=True),
                     at, ps.free, self.ctok)
        ps.free = []
        a = Q.op("act", lambda e: e.activation(self.r8[:, 0:8], ps.t[:, 0:8], ACT.Sqrt,
                                               bias=self.eps[:, 0:1], scale=1.0 / S), m, Q.last("dve"))
        r = Q.op("dve", lambda e: e.reciprocal(self.r8[:, 8:16], self.r8[:, 0:8]), a)
        ps.free = [a]
        dg = self.tmp.take()
        if dg is acc:
            dg = self.tmp.take()
        d = Q.op("dve", lambda e: e.tensor_tensor(
            dg.t[:, :].rearrange("p (t c) -> p t c", t=8),
            self.ident[:, :].unsqueeze(1).to_broadcast([128, 8, 128]),
            self.r8[:, 8:16].unsqueeze(2).to_broadcast([128, 8, 128]), ALU.mult), r, dg.free)
        rb = self.ps.take()
        for h in range(2):
            m2 = Q.op("pe", lambda e, h=h: e.matmul(rb.t[:, h * 512:h * 512 + 512], self.ones[:, :],
                                                    dg.t[:, h * 512:h * 512 + 512], start=True, stop=True),
                      d, rb.free)
        rb.free = []
        acc.free, dg.free = [m], [m2]
        return rb, m2

    def scaled(self, X, xtok, rb, rtok, g, hi, lo, free, shift=None):
        Q, toks = self.Q, []
        for j in range(NT):
            s = self.tmp.take()
            a = Q.op("dve", lambda e, j=j, s=s: e.scalar_tensor_tensor(
                out=s.t[:, :], in0=X[j][:, :], scalar=g(j), in1=rb.t[:, :], op0=ALU.mult, op1=ALU.mult),
                xtok[j], rtok, s.free)
            if shift is not None:
                a2 = Q.op("act", lambda e, j=j, s=s: e.activation(s.t[:, :], s.t[:, :], ACT.Identity,
                                                                  bias=shift(j)), a)
            else:
                a2 = a
            t = self.split(s.t[:, :], hi[j][:, :], lo[j][:, :], a2, free=free, eng="pool" if j % 2 else "dve")
            s.free = t
            toks.append(t)
        rb.free = [a]
        return toks

    def acts(self, hi, lo, toks):
        return [(h, l, t) for h, l, t in zip(hi, lo, toks)]

    def build(self):
        Q, A = self.Q, self.A
        self.loaded, self.ready, self.n_w = {}, {}, 0
        self.setup()
        C = self.C
        c0 = [Q.load(self.ident[:, :], C["ident"], "c"), Q.load(self.flip[:, :], C["flip"], "c"), Q.load(self.oneh[:, :], C["oneh"], "c"),
              Q.load(self.rel[:, 0:8], A["rel_bias"], "c"), Q.load(self.rel[:, 8:24], A["rel_bias_2"], "c"),
              Q.load(self.invc[:, :], C["invc"].to_broadcast([128, 64]), "c"),
              Q.load(self.sk[:, :], A["b_sinks_2"].to_broadcast([128, 16]), "c")]
        va, vb = self.tmp.take(), self.tmp.take()
        rows = [("g_mix", V_GMIX), ("g_ffn", V_GFFN), ("g_final", V_GFIN), ("norm_g_2", V_NORM),
                ("ada_b_2", V_ADAB), ("kv_norm_g_2", V_KVG), ("kv_ada_b_2", V_KVB), ("a_scale_2", V_SCALE),
                ("b_gate", V_GATE), ("conv_w", V_CONV), ("c_2", V_C), ("final_g_2", V_FIN2)]
        for name, r in rows:
            ap = A[name]
            if len(ap.shape) == 1:
                flatv = ap
            elif len(ap.shape) == 2:
                flatv = ap.rearrange("a b -> (a b)")
            else:
                flatv = ap.rearrange("a b c -> (a b c)")
            n = flatv.shape[0] // 128
            src = flatv.rearrange("(r p) -> r p", p=128)
            n1 = max(0, min(n, 128 - r))
            if n1:
                cc = Q.load(va.t[r:r + n1, 0:128], src[0:n1, :], "c")
            if n > n1:
                cc = Q.load(vb.t[r + n1 - 128:r + n - 128, 0:128], src[n1:n, :], "c")
        z1 = Q.op("pool", lambda e: e.memset(self.ones[:, :], 1.0))
        z2 = Q.op("pool", lambda e: e.memset(self.eps[:, :], 1e-6))
        self.ctok = [cc, z1, z2]

        xn = [self.main(f"xn{i}", i) for i in range(NT)]
        X = [self.main(f"xt{j}", 16 + j) for j in range(NT)]
        for i in range(NT):
            xl = Q.load(xn[i][:, :], A["x"][0, i * 128:(i + 1) * 128, :], f"xn{i}")
            xn[i] = (xn[i], xl)
        ps = self.ps.take()
        Q.op("pe", lambda e: e.transpose(ps.t[:, 0:128], va.t[:, 0:128], self.ident[:, :]), cc)
        tv = Q.op("pe", lambda e: e.transpose(ps.t[:, 128:V_ALL], vb.t[0:V_ALL - 128, 0:128],
                                              self.ident[0:V_ALL - 128, 0:V_ALL - 128]))
        vv = Q.op("dve", lambda e: e.tensor_copy(self.vec[:, :], ps.t[:, 0:V_ALL]), tv)
        ps.free = [vv]
        va.free = vb.free = [tv]
        vec = lambda base: (lambda j: self.vec[:, base + j:base + j + 1])
        ca = Q.op("act", lambda e: e.activation(self.cact[:, :], self.vec[:, V_C:V_C + 8], ACT.Silu), vv)

        ps = self.ps.take()
        t = Q.op("pe", lambda e: e.matmul(ps.t[0:24, 0:384], self.rel[:, :], self.oneh[:, :],
                                          start=True, stop=True), cc, ps.free)
        t = Q.op("dve", lambda e: e.tensor_copy(self.gb[0:24, :], ps.t[0:24, 0:384]), t)
        ps.free = [t]
        gd = self.dram("gdist", [24, 384])
        gst = Q.load(gd, self.gb[0:24, :], "gst", t)

        xtok = self.transposed(xn, X, None)
        rb, rtok = self.rstd(X, xtok)
        hi = [self.main(f"ah{j}", j, FR) for j in range(NT)]
        lo = [self.main(f"al{j}", 8 + j, FR) for j in range(NT)]
        htok = self.scaled(X, xtok, rb, rtok, vec(V_GMIX), hi, lo, Q.last("pe"))
        h = self.acts(hi, lo, htok)
        W = A["w_in"][0]

        qh = [self.main(f"qh{j}", 16 + j, FR) for j in range(4)]
        ql = [self.main(f"ql{j}", 20 + j, FR) for j in range(4)]
        KE, KO, LE, LO = (self.main(f"kp{i}", 24 + i, FR) for i in range(4))
        kt, kt2 = self.main("kt", 33), self.main("kt2", 34)
        dead = [htok, Q.last("dve")]
        zz = self.zero_pads([(KE, 64), (LE, 64), (KO, 0), (LO, 0)], dead)
        u = self.unit(self.w8(W, C_IK, 72), cols=576)
        ps, t = self.gemm(u, 8, 72, h, m=72)
        t = Q.op("act", lambda e, ps=ps: e.activation(kt[0:72, :], ps.t[0:72, :], ACT.Copy), t, dead)
        ps.free = [t]
        ktt = self.k_pads(kt, kt2, (KE, LE, KO, LO), [t, zz], "swap0", [])
        ps = self.ps.take()
        for i in range(NT):
            t = Q.op("pe", lambda e, i=i, ps=ps: e.transpose(ps.t[:, i * 72:i * 72 + 72] if i < 7 else ps.t[:, 512:584],
                                                      kt[0:72, i * 128:i * 128 + 128], self.ident[0:72, 0:72]),
                     t if i == 0 else None, ps.free)
        for i in range(NT):
            c = i * 72 if i < 7 else 512
            t = Q.op("dve", lambda e, i=i, c=c, ps=ps: e.tensor_scalar(
                self.iw[:, i * 8:i * 8 + 8], ps.t[:, c + 64:c + 72], 512.0 ** -0.5, None, ALU.mult), t)
        ps.free = [t]
        iwt = t
        qt = []
        for j in range(4):
            u = self.unit(self.w8(W, C_IQ + 128 * j))
            ps, t = self.gemm(u, 8, 128, h)
            t = self.split_ps(ps.t[:, :], qh[j][:, :], ql[j][:, :], t, free=dead)
            ps.free = t[1:]
            qt.append(t)
        smt = {}
        off = [0]
        for b in range(NT):
            off.append(off[-1] + (b + 1) * 128)
        SMt = self.main("sm", 28, cols=off[-1])
        SM = [SMt[:, off[b]:off[b + 1]] for b in range(NT)]
        for b in range(2):
            t = Q.op("pool", lambda e, b=b: e.memset(SM[b], 0.0), dead)
            smt[b] = [Q.op("pool", lambda e, b=b: e.affine_select(
                out=SM[b][:, b * 128:b * 128 + 128], in_=SM[b][:, b * 128:b * 128 + 128],
                compare_op=ALU.is_ge, fill=NEG, base=0, pattern=[[-1, 128]], channel_multiplier=1), t)]
        for b in range(2, NT):
            Wd = (b + 1) * 128
            st = dead
            for hd in range(8):
                j, odd = hd // 2, hd % 2
                K = (KO, LO) if odd else (KE, LE)
                ps, t = self.logits((qh[j], ql[j]), K, b, Wd, [qt[j], ktt])
                r = self.tmp.take()
                a = Q.op("act", lambda e, ps=ps, r=r, Wd=Wd: e.activation(
                    r.t[:, 0:Wd], ps.t[:, 0:Wd], ACT.Relu), t, r.free)
                ps.free = [a]
                iwc = self.iw[:, b * 8 + hd:b * 8 + hd + 1]
                if hd == 0:
                    st = Q.op("dve", lambda e, b=b, r=r, Wd=Wd, iwc=iwc: e.tensor_scalar(
                        SM[b], r.t[:, 0:Wd], iwc, None, ALU.mult), a, st, iwt)
                else:
                    st = Q.op("dve", lambda e, b=b, r=r, Wd=Wd, iwc=iwc: e.scalar_tensor_tensor(
                        out=SM[b], in0=r.t[:, 0:Wd], scalar=iwc, in1=SM[b], op0=ALU.mult, op1=ALU.add), a, st)
                r.free = [st]
            smt[b] = Q.op("pool", lambda e, b=b: e.affine_select(
                out=SM[b][:, b * 128:b * 128 + 128], in_=SM[b][:, b * 128:b * 128 + 128],
                compare_op=ALU.is_ge, fill=FUT, base=0, pattern=[[-1, 128]], channel_multiplier=1), st)
        index_done = Q.last("pe")
        for b in range(2, NT):
            t = smt[b]
            for r in range(32):
                m8 = self.m8[:, (r % 2) * 8:(r % 2) * 8 + 8]
                t = Q.op("dve", lambda e, b=b, m8=m8: e.max(m8, SM[b]), t)
                t = Q.op("dve", lambda e, b=b, m8=m8: e.match_replace(SM[b], m8, SM[b], GONE), t)
            smt[b] = Q.op("dve", lambda e, b=b: e.tensor_scalar(SM[b], SM[b], -3.2e38, NEG, ALU.is_ge, ALU.mult), t)

        cv = self.dram("cv", [512, S])
        cvt = []
        for j in range(4):
            u = self.unit(self.w8(W, C_C + 128 * j))
            ps, t = self.gemm(u, 8, 128, h)
            x1 = self.tmp.take()
            t1 = Q.op("act", lambda e, ps=ps, x1=x1: e.activation(x1.t[:, :], ps.t[:, :], ACT.Copy), t, x1.free)
            ps.free = [t1]
            u = self.unit(self.w8(W, C_X + 128 * j))
            ps, t = self.gemm(u, 8, 128, h)
            x2 = self.tmp.take()
            t2 = Q.op("act", lambda e, ps=ps, x2=x2: e.activation(x2.t[:, :], ps.t[:, :], ACT.Copy), t, x2.free)
            ps.free = [t2]
            t1 = Q.op("pool", lambda e, x1=x1, x2=x2: e.tensor_tensor(x1.t[:, :], x1.t[:, :], x2.t[:, :], ALU.mult), t1, t2)
            y = self.tmp.take()
            w = [self.vec[:, V_CONV + 4 * k + j:V_CONV + 4 * k + j + 1] for k in range(3)]
            t3 = Q.op("pool", lambda e, x1=x1, y=y, w=w: e.tensor_scalar(y.t[:, :], x1.t[:, :], w[2], None, ALU.mult), t1, y.free, vv)
            for sh in (1, 2):
                t4 = Q.op("pool", lambda e, x1=x1, x2=x2, w=w, sh=sh: e.tensor_scalar(
                    x2.t[:, 0:S - sh], x1.t[:, 0:S - sh], w[2 - sh], None, ALU.mult), t3)
                t3 = Q.op("pool", lambda e, x2=x2, y=y, sh=sh: e.tensor_tensor(
                    y.t[:, sh:S], y.t[:, sh:S], x2.t[:, 0:S - sh], ALU.add), t4)
            x1.free = x2.free = [t3]
            u = self.unit(self.w8(W, C_B + 128 * j))
            ps, t = self.gemm(u, 8, 128, h)
            x3 = self.tmp.take()
            t2 = Q.op("act", lambda e, ps=ps, x3=x3: e.activation(x3.t[:, :], ps.t[:, :], ACT.Copy), t, x3.free)
            ps.free = [t2]
            t3 = Q.op("pool", lambda e, x3=x3, y=y: e.tensor_tensor(y.t[:, :], y.t[:, :], x3.t[:, :], ALU.mult), t2, t3)
            x3.free = [t3]
            cvt.append(Q.load(cv[j * 128:j * 128 + 128, :], y.t[:, :], "st_" + y.name, t3))
            y.free = [cvt[-1]]

        gd_ = self.dram("gates", [2048, S])
        gt = []
        for j in range(16):
            u = self.unit(self.w8(W, C_GA + 128 * j))
            ps, t = self.gemm(u, 8, 128, h)
            g = self.tmp.take()
            t = Q.op("act", lambda e, ps=ps, g=g, j=j: e.activation(g.t[:, :], ps.t[:, :], ACT.Sigmoid,
                                                                   bias=vec(V_GATE)(j)), t, g.free, vv)
            ps.free = [t]
            gt.append(Q.load(gd_[j * 128:j * 128 + 128, :], g.t[:, :], "st_" + g.name, t))
            g.free = [gt[-1]]

        u = self.unit(self.w8(W, C_KV))
        ps, t = self.gemm(u, 8, 128, h)
        t = Q.op("act", lambda e, ps=ps: e.activation(kt[:, :], ps.t[:, :], ACT.Copy), t, ktt)
        ps.free = [t]
        kvt = t
        ktt = self.k_pads(kt, kt2, (KE, LE, KO, LO), [t], "swap1", index_done)
        qt = []
        for j in range(4):
            u = self.unit(self.w8(W, C_Q + 128 * j))
            ps, t = self.gemm(u, 8, 128, h)
            s = self.tmp.take()
            t = Q.op("act", lambda e, ps=ps, s=s: e.activation(s.t[:, :], ps.t[:, :], ACT.Copy), t, s.free)
            ps.free = [t]
            t = self.split(s.t[:, :], qh[j][:, :], ql[j][:, :], t, free=index_done)
            s.free = t
            qt.append(t)
        projected = Q.last("pe")

        VE, VO, VLE, VLO = (self.main(f"vp{i}", i, FR) for i in range(4))
        ptb = [(self.main(f"pth{i}", 4 + i, FR), self.main(f"ptl{i}", 6 + i, FR)) for i in range(2)]
        ptf = [projected, projected]
        oh = [self.main(f"oh{j}", 8 + j, FR) for j in range(4)]
        ol = [self.main(f"ol{j}", 12 + j, FR) for j in range(4)]
        zz = self.zero_v([(VE, 64), (VLE, 64), (VO, 0), (VLO, 0)], projected)
        vt = self.v_pads(kt, (VE, VLE, VO, VLO), 64, 64, [kvt, zz])
        T1 = self.main("t1", 34, cols=2048)
        t1t = self.table(T1, gd, 0, "t1", [gst, ktt, vt])
        ott = [[] for _ in range(4)]
        t1s = []
        for hd in range(8):
            t1s.append(Q.op("dve", lambda e: e.tensor_scalar(
                T1[:, hd * 256:hd * 256 + 256], T1[:, hd * 256:hd * 256 + 256], T1[:, hd * 256:hd * 256 + 1],
                None, ALU.subtract), t1t))
        items = [(b, hd) for b in range(NT) for hd in range(8)]
        st = {}

        def score(n):
            b, hd = items[n]
            Wd = (b + 1) * 128
            K = (KO, LO) if hd % 2 else (KE, LE)
            j = hd // 2
            st[n] = self.logits((qh[j], ql[j]), K, b, Wd, [qt[j], ktt])

        def top(n):
            b, hd = items[n]
            Wd = (b + 1) * 128
            ps, t = st[n]
            L = self.tmp.take()
            near = min(Wd, 256)
            far = Wd - near
            mf, mx, nm, sm, rs = (self.st[:, (n % 8) * 8 + i:(n % 8) * 8 + i + 1] for i in range(5))
            if far:
                f = Q.op("dve", lambda e: e.tensor_tensor_reduce(
                    L.t[:, 0:far], ps.t[:, 0:far], SM[b][:, 0:far], 0.125, -3.0e38, ALU.add, ALU.max, mf),
                    t, L.free, smt[b])
            t = Q.op("dve", lambda e: e.scalar_tensor_tensor(
                out=L.t[:, far:Wd], in0=ps.t[:, far:Wd], scalar=0.125,
                in1=T1[:, hd * 256 + 256 - near:hd * 256 + 256], op0=ALU.mult, op1=ALU.add), t, L.free, t1s[hd])
            ps.free = [t]
            t = Q.op("dve", lambda e: e.tensor_tensor_reduce(
                L.t[:, far:Wd], L.t[:, far:Wd], SM[b][:, far:Wd], 1.0, mf if far else -3.0e38,
                ALU.add, ALU.max, mx), t, smt[b], [f] if far else None)
            t = Q.op("dve", lambda e: e.tensor_scalar(nm, mx, -1.0, None, ALU.mult), t)
            t = Q.op("act", lambda e: e.activation(L.t[:, 0:Wd], L.t[:, 0:Wd], ACT.Exp, bias=nm, accum_out=sm), t)
            st[n] = (L, t, sm, rs)

        def norm(n):
            b, hd = items[n]
            Wd = (b + 1) * 128
            L, t, sm, rs = st[n]
            t = Q.op("dve", lambda e: e.reciprocal(rs, sm), t)
            t = Q.op("act", lambda e: e.activation(L.t[:, 0:Wd], L.t[:, 0:Wd], ACT.Copy, scale=rs), t)
            st[n] = (L, t)

        def turn(n):
            b, hd = items[n]
            L, t = st[n]
            ps = self.ps.take()
            for i in range(b + 1):
                m = Q.op("pe", lambda e: e.transpose(
                    ps.t[:, i * 128:i * 128 + 128], L.t[:, i * 128:i * 128 + 128], self.ident[:, :]), t, ps.free)
            L.free = [m]
            st[n] = (ps, m)

        def turned(n):
            b, hd = items[n]
            Wd = (b + 1) * 128
            ps, t = st[n]
            PH, PL = ptb[hd % 2]
            t = self.split_ps(ps.t[:, 0:Wd], PH[:, 0:Wd], PL[:, 0:Wd], t, free=ptf[hd % 2])
            ps.free = t[1:]
            st[n] = (PH, PL, t)

        def values(n):
            b, hd = items[n]
            if hd % 2 == 0:
                return
            po = self.ps.take()
            for odd in range(2):
                V = (VO, VLO) if odd else (VE, VLE)
                PH, PL, pt = st[n - 1 + odd]
                for i in range(b + 1):
                    c = slice(i * 128, i * 128 + 128)
                    t = self.prods(po.t[:, 0:128], (V[0][:, c], V[1][:, c]), (PH[:, c], PL[:, c]),
                                   odd == 0 and i == 0, odd == 1 and i == b, [pt, po.free, vt])
                ptf[odd] = [t]
            c, j = slice(b * 128, b * 128 + 128), hd // 2
            t = self.split_ps(po.t[:, 0:128], oh[j][:, c], ol[j][:, c], t, free=projected)
            po.free = t[1:]
            ott[j] += t

        self.pipeline(len(items), [(0, score), (3, values), (2, turn), (2, turned), (1, norm), (0, top)])
        attended = Q.last("pe", "dve", "act")

        ch = [self.main(f"ch{j}", 16 + j, FR) for j in range(4)]
        cl = [self.main(f"cl{j}", 20 + j, FR) for j in range(4)]
        ctk = []
        for j in range(4):
            s = self.tmp.take()
            t = Q.load(s.t[:, :], cv[j * 128:j * 128 + 128, :], "ld_" + s.name, s.free, cvt[j])
            t = self.split(s.t[:, :], ch[j][:, :], cl[j][:, :], t, free=attended)
            s.free = t
            ctk.append(t)
        mtile = [24 + j for j in range(12)] + [0, 1, 2, 3]
        mh = [self.main(f"mh{j}", mtile[j], FR) for j in range(8)]
        ml = [self.main(f"ml{j}", mtile[8 + j], FR) for j in range(8)]
        mtk = []
        self.ahead = 2
        for j in range(8):
            if j % 2 == 0:
                ua = self.unit(self.w8(A["w_branch_a"][0], 128 * j, 256, nk=4))
                ub = self.unit(self.w8(A["w_branch_b"][0], 128 * j, 256, nk=4))
            ya, ta = self.gemm(ua, 4, 256, self.acts(ch, cl, ctk), col0=128 * (j % 2))
            yb, tb = self.gemm(ub, 4, 256, self.acts(oh, ol, ott), col0=128 * (j % 2))
            s, s2 = self.tmp.take(), self.tmp.take()
            t = Q.load(s.t[:, :], gd_[j * 128:j * 128 + 128, :], "ld_" + s.name, s.free, gt[j])
            t2 = Q.load(s2.t[:, :], gd_[1024 + j * 128:1024 + j * 128 + 128, :], "ld_" + s2.name, s2.free, gt[8 + j])
            t = Q.op("dve", lambda e, s=s, ya=ya: e.tensor_tensor(s.t[:, :], ya.t[:, :], s.t[:, :], ALU.mult), t, ta)
            ya.free = [t]
            t2 = Q.op("dve", lambda e, s2=s2, yb=yb: e.tensor_tensor(s2.t[:, :], yb.t[:, :], s2.t[:, :], ALU.mult), t2, tb)
            yb.free = [t2]
            t = Q.op("dve", lambda e, s=s, s2=s2: e.tensor_tensor(s.t[:, :], s.t[:, :], s2.t[:, :], ALU.add), t, t2)
            s2.free = [t]
            t = self.split(s.t[:, :], mh[j][:, :], ml[j][:, :], t, free=attended)
            s.free = t
            mtk.append(t)
        self.ahead = 3
        branched = Q.last("pe")
        xn = [self.main(f"xm{i}", 16 + i) for i in range(NT)]
        X = [self.main(f"X{j}", 8 + j) for j in range(NT)]
        for i in range(NT):
            xl = Q.load(xn[i][:, :], A["x"][0, i * 128:(i + 1) * 128, :], f"xn{i}", branched)
            xn[i] = (xn[i], xl)
        xtok = self.transposed(xn, X, branched)
        for j in range(8):
            u = self.unit(self.w8(A["w_out"][0], 128 * j))
            ps, t = self.gemm(u, 8, 128, self.acts(mh, ml, mtk))
            t = Q.op("dve", lambda e, ps=ps, j=j: e.tensor_tensor(X[j][:, :], X[j][:, :], ps.t[:, :], ALU.add), t, xtok[j])
            ps.free = [t]
            xtok[j] = [t]

        hi = [self.main(f"bh{j}", 16 + j, FR) for j in range(NT)]
        lo = [self.main(f"bl{j}", 24 + j, FR) for j in range(NT)]
        gtile = [32, 33, 34, 35, 0, 1, 2, 3, 4, 5, 6, 7]
        self.G = Ring([Slot((self.main(f"gh{i}", gtile[i], FR), self.main(f"gl{i}", gtile[6 + i], FR)), f"g{i}")
                       for i in range(6)])
        rb, rtok = self.rstd(X, xtok)
        done = Q.last("pe")
        for s in self.G.slots:
            s.free = done
        htok = self.scaled(X, xtok, rb, rtok, vec(V_GFFN), hi, lo, done)
        h = self.acts(hi, lo, htok)
        self.G.slots = self.G.slots[0:5]
        self.ada_start([self.main("ada0", 1), self.main("ada1", 7)], done, [ca, vv])
        groups = [4, 4, 4, 4, 4, 2]
        base = 0
        pend = None
        for gi, gn in enumerate(groups):
            tiles = []
            for i in range(gn):
                f = base + i
                u = self.unit(self.w8(A["w_ffn_gate"][0], 128 * f))
                pg, tg = self.gemm(u, 8, 128, h)
                u = self.unit(self.w8(A["w_ffn_up"][0], 128 * f))
                pu, tu = self.gemm(u, 8, 128, h)
                tiles.append(self.glu(pg, tg, pu, tu))
                if i == 0 and pend is not None:
                    self.down(pend, A["w_ffn_down"][0], X, xtok)
            pend = (base * 128, tiles)
            base += gn
        self.down(pend, A["w_ffn_down"][0], X, xtok)
        while self.ada_n < 64:
            self.ada_step()
        self.ada_n = None
        for i, (sc, gv) in enumerate(((8, V_NORM), (32, V_NORM + 8), (56, V_KVG))):
            gst_ = Q.op("dve", lambda e, i=i, sc=sc, gv=gv: e.scalar_tensor_tensor(
                out=self.gs[:, 8 * i:8 * i + 8], in0=self.mod[:, sc:sc + 8], scalar=1.0,
                in1=self.vec[:, gv:gv + 8], op0=ALU.add, op1=ALU.mult), self.adat)
        self.modtok = [self.adat, gst_]
        last = Q.last("pe")
        self.G = Ring([Slot((self.main(f"gh{i}", gtile[i], FR), self.main(f"gl{i}", gtile[6 + i], FR)), f"g{i}")
                       for i in range(6)])
        for s in self.G.slots:
            s.free = last

        rb, rtok = self.rstd(X, xtok)
        for j in range(8):
            xtok[j] = [Q.op("dve", lambda e, j=j, rb=rb: e.scalar_tensor_tensor(
                out=X[j][:, :], in0=X[j][:, :], scalar=vec(V_GFIN)(j), in1=rb.t[:, :], op0=ALU.mult, op1=ALU.mult),
                xtok[j], rtok)]
        rb.free = xtok[7]

        rb, rtok = self.rstd(X, xtok)
        gs = lambda i: (lambda j: self.gs[:, 8 * i + j:8 * i + j + 1])
        md = lambda c: (lambda j: self.mod[:, c + j:c + j + 1])
        htok = self.scaled(X, xtok, rb, rtok, gs(0), hi, lo, Q.last("pe"), shift=md(0))
        h = self.acts(hi, lo, htok)
        Wi = A["a_w_in_2"][0]
        pend = None
        for g in range(4):
            pt = []
            for i in range(4):
                u = self.unit(self.w8(Wi, 512 * g + 128 * i))
                ps, t = self.gemm(u, 8, 128, h)
                pt.append(self.pooled(ps, t, g))
                if i == 0 and pend is not None:
                    self.down(pend, A["a_w_out_2"][0], X, xtok, gate=md(16))
            pacts = [(s.t[0], s.t[1], t) for s, t in pt]
            tiles = []

            def gated(i, py, ty, pz, tz):
                s = self.tmp.take()
                a = Q.op("act", lambda e: e.activation(s.t[:, :], pz.t[:, :], ACT.Silu), tz, s.free)
                pz.free = [a]
                sc = vec(V_SCALE)(4 * g + i)
                a = Q.op("dve", lambda e: e.scalar_tensor_tensor(
                    out=s.t[:, :], in0=py.t[:, :], scalar=sc, in1=s.t[:, :], op0=ALU.mult, op1=ALU.mult), a, ty)
                py.free = [a]
                gslot = self.G.take()
                t = self.split(s.t[:, :], gslot.t[0][:, :], gslot.t[1][:, :], a, free=gslot.free)
                s.free = t
                tiles.append((gslot, t))

            self.ahead = 2
            held = None
            for i in range(4):
                if i % 2 == 0:
                    uy = self.unit(self.w8(A["a_w_group_2"][0, g], 128 * i, 256, nk=4))
                py, ty = self.gemm(uy, 4, 256, pacts, col0=128 * (i % 2))
                u = self.unit(self.w8(Wi, 2048 + 512 * g + 128 * i))
                if i == 3:
                    for s, _ in pt:
                        s.free = [ty]
                    gated(*held)
                pz, tz = self.gemm(u, 8, 128, h)
                if i == 2:
                    held = (i, py, ty, pz, tz)
                else:
                    gated(i, py, ty, pz, tz)
            self.ahead = 3
            pend = (512 * g, tiles)
        self.down(pend, A["a_w_out_2"][0], X, xtok, gate=md(16))

        rb, rtok = self.rstd(X, xtok)
        htok = self.scaled(X, xtok, rb, rtok, gs(2), hi, lo, Q.last("pe"), shift=md(48))
        h = self.acts(hi, lo, htok)
        kx0, kx1, vt_ = self.main("kx0", 4), self.main("kx1", 33), self.main("vt", 34)
        pooled_done = Q.last("pe")
        u = self.unit(self.w8(A["w_kv_2"], 0))
        ps, t = self.gemm(u, 8, 128, h)
        t1 = Q.op("act", lambda e, ps=ps: e.activation(kx0[0:64, :], ps.t[0:64, :], ACT.Copy), t, pooled_done)
        t1 = Q.op("act", lambda e, ps=ps: e.activation(kx1[64:128, :], ps.t[64:128, :], ACT.Copy), t, pooled_done)
        ps.free = [t1]
        k0t = Q.load(kx0[64:128, :], kx0[0:64, :], "kx0", t1)
        k1t = Q.load(kx1[0:64, :], kx1[64:128, :], "kx1", t1)
        u = self.unit(self.w8(A["w_kv_2"], 128))
        ps, t = self.gemm(u, 8, 128, h)
        vtt = Q.op("act", lambda e, ps=ps: e.activation(vt_[:, :], ps.t[:, :], ACT.Copy), t, pooled_done)
        ps.free = [vtt]
        kv_done = Q.last("pe")
        htok = self.scaled(X, xtok, rb, rtok, gs(1), hi, lo, kv_done, shift=md(24))
        h = self.acts(hi, lo, htok)
        xs = self.dram("xs", [S, S])
        xst = [Q.load(xs[j * 128:j * 128 + 128, :], X[j][:, :], f"xs{j}", xtok[j]) for j in range(8)]
        qd = self.dram("qd", [2048, S])
        qdt = []
        for j in range(16):
            u = self.unit(self.w8(A["b_w_in_2"][0], 128 * j))
            ps, t = self.gemm(u, 8, 128, h)
            s = self.tmp.take()
            if j < 8:
                t = Q.op("act", lambda e, ps=ps, s=s: e.activation(s.t[:, :], ps.t[:, :], ACT.Copy, scale=0.125), t, s.free)
            else:
                t = Q.op("act", lambda e, ps=ps, s=s: e.activation(s.t[:, :], ps.t[:, :], ACT.Silu), t, s.free)
            ps.free = [t]
            qdt.append(Q.load(qd[j * 128:j * 128 + 128, :], s.t[:, :], "st_" + s.name, t))
            s.free = [qdt[-1]]
        qz_done = [Q.last("pe", "dve", "act"), xst, htok]
        KP = [self.main(f"k2p{i}", 16 + i, FR) for i in range(4)]
        VP = [self.main(f"v2p{i}", 20 + i, FR) for i in range(4)]
        T2 = self.main("t2", 24, cols=2048)
        ptb = [(self.main(f"p2h{i}", 26 + i, FR), self.main(f"p2l{i}", 28 + i, FR)) for i in range(2)]
        ptf = [qz_done, qz_done]
        qtile = [30, 31, 35, 0]
        qb = [(self.main(f"q2h{i}", qtile[i], FR), self.main(f"q2l{i}", qtile[2 + i], FR)) for i in range(2)]
        qf = [qz_done, qz_done]
        otile = [5, 1, 2, 3, 6, 7, 8, 9, 10, 11, 12, 13, 14, 15, 32, 4]
        oh = [self.main(f"o2h{j}", otile[j], FR) for j in range(8)]
        ol = [self.main(f"o2l{j}", otile[8 + j], FR) for j in range(8)]
        ott = [[] for _ in range(8)]
        zz = self.zero_pads([(KP[0], 64), (KP[1], 64), (KP[2], 0), (KP[3], 0)], qz_done)
        zv = self.zero_v([(VP[0], 64), (VP[1], 64), (VP[2], 0), (VP[3], 0)], qz_done)
        prev = qz_done
        items = [(j, hb, odd) for j in range(8) for hb in range(2) for odd in range(2)]
        st, heads, pads = {}, {}, {}

        def begin(n):
            j, hb, odd = items[n]
            if hb or odd:
                return
            kvh = j // 4
            if j % 4 == 0:
                prev = qz_done + Q.last("pe", "dve")
                kx, kxt = ((kx0, [k0t, t1]), (kx1, [k1t, t1]))[kvh]
                kpt = []
                for half, (H, Lw) in ((0, (KP[0], KP[1])), (64, (KP[2], KP[3]))):
                    sl = slice(half, half + 64)
                    kpt += self.split(kx[sl, :], H[sl, :], Lw[sl, :], kxt, zz, free=prev, eng="dve")
                vpt = self.v_pads(vt_, VP, 64 * kvh, 128, [vtt, zv, prev])
                t2t = self.table(T2, gd, 8 + 8 * kvh, f"t2{kvh}", [gst, prev])
                T2v = T2[:, :].rearrange("p (h c) -> p h c", h=8)
                t2t = Q.op("pool", lambda e: e.affine_select(
                    out=T2v, in_=T2v, compare_op=ALU.is_ge, fill=NEG, base=128,
                    pattern=[[0, 8], [-1, 256]], channel_multiplier=1), t2t)
                t2t = Q.op("pool", lambda e: e.affine_select(
                    out=T2v, in_=T2v, compare_op=ALU.is_gt, fill=NEG, base=0,
                    pattern=[[0, 8], [1, 256]], channel_multiplier=-1), t2t)
                pads[kvh] = (kpt, vpt, t2t)
            s = self.tmp.take()
            t = Q.load(s.t[:, :], qd[j * 128:j * 128 + 128, :], "ld_" + s.name, s.free, qdt[j])
            QH, QL = qb[j % 2]
            qt = self.split(s.t[:, :], QH[:, :], QL[:, :], t, free=qf[j % 2])
            s.free = qt
            heads[j] = (QH, QL, qt)

        def score(n):
            j, hb, odd = items[n]
            QH, QL, qt = heads[j]
            kpt = pads[j // 4][0]
            K = (KP[2], KP[3]) if odd else (KP[0], KP[1])
            ps = self.ps.take()
            for i in range(4):
                blk = 4 * hb + i
                c = slice(blk * 128, blk * 128 + 128)
                lo_ = max(blk - 1, 0)
                k_ = slice(lo_ * 128, blk * 128 + 128)
                o = i * 256 + (128 if blk == 0 else 0)
                t = self.prods(ps.t[:, o:i * 256 + 256], (QH[:, c], QL[:, c]),
                               (K[0][:, k_], K[1][:, k_]), True, True, [qt, kpt, ps.free])
            st[n] = (ps, t)
            if hb and odd:
                qf[j % 2] = [t]

        def top(n):
            j, hb, odd = items[n]
            ps, t = st[n]
            hl = (2 * j + odd) % 8
            L = self.att.take()
            c = (n % 4) * 32
            mm, nm, sm, es, rd = (self.st[:, c + 4 * i:c + 4 * i + 4] for i in range(5))
            sk = self.sk[:, 2 * j + odd:2 * j + odd + 1]
            zt = Q.op("pool", lambda e: e.memset(L.t[:, 0:128], 0.0), L.free) if hb == 0 else None
            for i in range(4):
                o = i * 256 + (128 if hb == 0 and i == 0 else 0)
                e_ = i * 256 + 256
                tt = Q.op("dve", lambda e: e.tensor_tensor_reduce(
                    L.t[:, o:e_], ps.t[:, o:e_], T2[:, hl * 256 + o - i * 256:hl * 256 + 256], 1.0, sk,
                    ALU.add, ALU.max, mm[:, i:i + 1]), t, L.free, pads[j // 4][2])
            ps.free = [tt]
            t = Q.op("dve", lambda e: e.tensor_scalar(nm, mm, -1.0, None, ALU.mult), tt)
            for i in range(4):
                o = i * 256 + (128 if hb == 0 and i == 0 else 0)
                e_ = i * 256 + 256
                t2 = Q.op("act", lambda e: e.activation(L.t[:, o:e_], L.t[:, o:e_], ACT.Exp,
                                                        bias=nm[:, i:i + 1], accum_out=sm[:, i:i + 1]), t)
            t = Q.op("act", lambda e: e.activation(es, nm, ACT.Exp, bias=sk), t)
            st[n] = (L, [t2, t, zt], sm, es, rd)

        def norm(n):
            L, t, sm, es, rd = st[n]
            t = Q.op("dve", lambda e: e.tensor_tensor(sm, sm, es, ALU.add), t)
            t = Q.op("dve", lambda e: e.reciprocal(rd, sm), t)
            L3 = L.t[:, :].rearrange("p (b c) -> p b c", b=4)
            t = Q.op("pool", lambda e: e.tensor_tensor(
                L3, L3, rd.unsqueeze(2).to_broadcast([128, 4, 256]), ALU.mult), t)
            st[n] = (L, t)

        def turn(n):
            L, t = st[n]
            ps = self.ps.take()
            for i in range(8):
                m = Q.op("pe", lambda e: e.transpose(
                    ps.t[:, i * 128:i * 128 + 128], L.t[:, i * 128:i * 128 + 128], self.ident[:, :]), t, ps.free)
            L.free = [m]
            st[n] = (ps, m)

        def turned(n):
            odd = items[n][2]
            ps, t = st[n]
            PH, PL = ptb[odd]
            t = self.split_ps(ps.t[:, :], PH[:, :], PL[:, :], t, free=ptf[odd])
            ps.free = t[1:]
            st[n] = (PH, PL, t)

        def values(n):
            j, hb, odd = items[n]
            if not odd:
                return
            po = self.ps.take()
            vpt = pads[j // 4][1]
            for i in range(4):
                blk = 4 * hb + i
                terms = [(odd, w) for odd in range(2) for w in range(2) if not (blk == 0 and w == 0)]
                for x, (odd, w) in enumerate(terms):
                    V = (VP[2], VP[3]) if odd else (VP[0], VP[1])
                    PH, PL, pt = st[n - 1 + odd]
                    sv = slice((blk - 1 + w) * 128, (blk + w) * 128)
                    pc = slice(i * 256 + w * 128, i * 256 + w * 128 + 128)
                    t = self.prods(po.t[:, i * 128:i * 128 + 128], (V[0][:, sv], V[1][:, sv]), (PH[:, pc], PL[:, pc]),
                                   x == 0, x == len(terms) - 1, [pt, po.free, vpt])
            ptf[0] = ptf[1] = [t]
            hs = slice(hb * 512, hb * 512 + 512)
            if hb == 0:
                z = self.tmp.take()
                zt = Q.load(z.t[:, :], qd[1024 + j * 128:1024 + j * 128 + 128, :], "ld_" + z.name, z.free, qdt[8 + j])
                heads["z"] = (z, zt)
            z, zt = heads["z"]
            t = Q.op("dve", lambda e: e.tensor_tensor(z.t[:, hs], z.t[:, hs], po.t[:, 0:512], ALU.mult), t, zt)
            po.free = [t]
            t = self.split(z.t[:, hs], oh[j][:, hs], ol[j][:, hs], t, free=[qz_done, pads[1][0] if j == 7 else None])
            ott[j] += t
            z.free = (z.free if hb else []) + t

        self.att = Ring(self.tmp.slots[0:3])
        self.tmp = Ring(self.tmp.slots[3:5])
        for kv in (0, 4):
            n0 = 4 * kv
            self.pipeline(16, [(0, begin), (0, score), (3, values), (2, turn), (2, turned), (1, norm), (0, top)], n0)
        self.tmp = Ring(self.att.slots + self.tmp.slots)
        att_done = Q.last("pe", "dve", "act", "pool")
        X = [self.main(f"Y{j}", 16 + j) for j in range(NT)]
        xtok = []
        for j in range(8):
            u = self.unit(self.w8(A["b_w_out_2"][0], 128 * j))
            ps, t = self.gemm(u, 8, 128, self.acts(oh, ol, ott))
            xl = Q.load(X[j][:, :], xs[j * 128:j * 128 + 128, :], f"xs{j}", att_done, xst[j])
            t = Q.op("dve", lambda e, ps=ps, j=j: e.scalar_tensor_tensor(
                out=X[j][:, :], in0=ps.t[:, :], scalar=md(40)(j), in1=X[j][:, :], op0=ALU.mult, op1=ALU.add), t, xl)
            ps.free = [t]
            xtok.append([t])
        rb, rtok = self.rstd(X, xtok)
        for j in range(8):
            xtok[j] = [Q.op("dve", lambda e, j=j, rb=rb: e.scalar_tensor_tensor(
                out=X[j][:, :], in0=X[j][:, :], scalar=vec(V_FIN2)(j), in1=rb.t[:, :], op0=ALU.mult, op1=ALU.mult),
                xtok[j], rtok)]
        rb.free = xtok[7]
        for i in range(NT):
            ps = self.ps.take()
            for j in range(NT):
                t = Q.op("pe", lambda e, i=i, j=j, ps=ps: e.transpose(
                    ps.t[:, j * 128:j * 128 + 128], X[j][:, i * 128:i * 128 + 128], self.ident[:, :]), xtok[j], ps.free)
            ps.free = []
            s = self.tmp.take()
            t = Q.op("act" if i % 2 else "dve", (lambda e, s=s, ps=ps: e.activation(s.t[:, :], ps.t[:, :], ACT.Copy)) if i % 2 else
                     (lambda e, s=s, ps=ps: e.tensor_copy(s.t[:, :], ps.t[:, :])), t, s.free)
            ps.free = [t]
            s.free = [Q.load(self.out[0, i * 128:(i + 1) * 128, :], s.t[:, :], "st_" + s.name, t)]

    def pipeline(self, n, stages, n0=0):
        for s in range(n + max(lag for lag, _ in stages)):
            for lag, f in stages:
                if 0 <= s - lag < n:
                    f(n0 + s - lag)

    def transposed(self, xn, X, free):
        toks = []
        for j in range(NT):
            ps = self.ps.take()
            for i in range(NT):
                t = self.Q.op("pe", lambda e, i=i, j=j, ps=ps: e.transpose(
                    ps.t[:, i * 128:i * 128 + 128], xn[i][0][:, j * 128:j * 128 + 128], self.ident[:, :]),
                    xn[i][1], ps.free, self.ctok)
            a = self.Q.op("act", lambda e, j=j, ps=ps: e.activation(X[j][:, :], ps.t[:, :], ACT.Copy), t, free)
            ps.free = [a]
            toks.append([a])
        return toks

    def zero_pads(self, pads, after):
        return [self.Q.op("dve", lambda e, p=p, h=h: e.memset(p[h:h + 64, :].bitcast(F32), 0.0), after)
                for p, h in pads]

    def zero_v(self, pads, after):
        return [self.Q.op("pool", lambda e, p=p, h=h: e.memset(
            p[:, :].rearrange("p (i c) -> p i c", c=128)[:, :, h:h + 64].bitcast(F32), 0.0), after)
            for p, h in pads]

    def k_pads(self, kt, kt2, pads, after, sem, free):
        KE, LE, KO, LO = pads
        d = self.Q.load(kt2[64:128, :], kt[0:64, :], sem, after)
        a = self.split(kt[0:64, :], KE[0:64, :], LE[0:64, :], after, free=free, eng="dve")
        b = self.split(kt2[64:128, :], KO[64:128, :], LO[64:128, :], d, after, free=free, eng="dve")
        return [a, b]

    def v_pads(self, src, pads, row, n, after):
        VE, VLE, VO, VLO = pads
        ps = self.ps.take()
        for i in range(NT):
            t = self.Q.op("pe", lambda e, i=i, ps=ps: e.transpose(
                ps.t[:, i * 128:i * 128 + 128], src[:, i * 128:i * 128 + 128], self.ident[:, :]), after, ps.free)
        v = ps.t[:, :].rearrange("p (i c) -> p i c", c=128)[:, :, row:row + 64]
        out = []
        for H, L, c in ((VE, VLE, 0), (VO, VLO, 64)):
            h = H[:, :].rearrange("p (i c) -> p i c", c=128)[:, :, c:c + 64]
            l = L[:, :].rearrange("p (i c) -> p i c", c=128)[:, :, c:c + 64]
            t = self.Q.op("act", lambda e, h=h: e.activation(h, v, ACT.Copy), t, after)
            t = self.Q.op("dve", lambda e, h=h, l=l: e.tensor_tensor(l, v, h.bitcast(F32), ALU.subtract), t)
            out.append(t)
        ps.free = [t]
        return out

    def table(self, Tt, gd, h0, sem, after):
        Q = self.Q
        src = bass.AP(gd.tensor, gd.offset + h0 * 384, [[1, 128], [384, 8], [1, 256]])
        t = Q.load(Tt[:, :].rearrange("p (h c) -> p h c", h=8), src, sem, after)
        toks = []
        for i in range(2):
            ps = self.ps.take()
            for h in range(2):
                c = i * 1024 + h * 512
                m = Q.op("pe", lambda e, ps=ps, h=h, c=c: e.matmul(
                    ps.t[:, h * 512:h * 512 + 512], self.flip[:, :], Tt[:, c:c + 512], start=True, stop=True), t, ps.free)
            a = Q.op("act", lambda e, ps=ps, i=i: e.activation(
                Tt[:, i * 1024:i * 1024 + 1024], ps.t[:, :], ACT.Copy), m)
            ps.free = [a]
            toks.append(a)
        return toks

    def logits(self, q, K, b, Wd, after):
        ps = self.ps.take()
        c = slice(b * 128, b * 128 + 128)
        for s0 in range(0, Wd, 512):
            s1 = min(s0 + 512, Wd)
            t = self.prods(ps.t[:, s0:s1], (q[0][:, c], q[1][:, c]), (K[0][:, s0:s1], K[1][:, s0:s1]),
                           True, True, [after, ps.free])
        ps.free = []
        return ps, t

    def glu(self, pg, tg, pu, tu):
        Q = self.Q
        s = self.tmp.take()
        a = Q.op("act", lambda e: e.activation(s.t[:, :], pg.t[:, :], ACT.Silu), tg, s.free)
        pg.free = [a]
        a = Q.op("dve", lambda e: e.tensor_tensor(s.t[:, :], s.t[:, :], pu.t[:, :], ALU.mult), a, tu)
        pu.free = [a]
        g = self.G.take()
        t = self.split(s.t[:, :], g.t[0][:, :], g.t[1][:, :], a, free=g.free)
        s.free = t
        return g, t

    def pooled(self, ps, t, g):
        Q, w = self.Q, 2 << g
        u, a, b = self.tmp.take(), self.tmp.take(), self.tmp.take()
        tu = Q.op("act", lambda e: e.activation(u.t[:, :], ps.t[:, :], ACT.Copy), t, u.free)
        ps.free = [tu]
        src, t = u, tu
        k = 1
        while k < w:
            dst = a if src is not a else b
            t1 = Q.op("dve", lambda e, s=src, d=dst, k=k: e.tensor_tensor(
                d.t[:, k:S], s.t[:, k:S], s.t[:, 0:S - k], ALU.add), t, dst.free)
            t2 = Q.op("dve", lambda e, s=src, d=dst, k=k: e.tensor_copy(d.t[:, 0:k], s.t[:, 0:k]), t, dst.free)
            dst.free = []
            t, src, k = [t1, t2], dst, 2 * k
        inv = self.invc[:, 16 * g:16 * g + 16]
        t = Q.op("dve", lambda e, s=src: e.tensor_tensor(s.t[:, 0:16], s.t[:, 0:16], inv, ALU.mult), t)
        t = Q.op("dve", lambda e, s=src: e.scalar_tensor_tensor(
            out=u.t[:, :], in0=s.t[:, :], scalar=1.0 / w, in1=u.t[:, :], op0=ALU.mult, op1=ALU.subtract), t)
        gs = self.G.take()
        t2 = self.split(u.t[:, :], gs.t[0][:, :], gs.t[1][:, :], t, free=gs.free)
        u.free, a.free, b.free = t2, [t], [t]
        return gs, t2

    def down(self, pend, W, X, xtok, gate=None):
        r0, tiles = pend
        nk = len(tiles)
        n = 1024 // nk
        acts = [(g.t[0], g.t[1], t) for g, t in tiles]
        for j in range(8):
            if (128 * j) % n == 0:
                u = self.unit(self.w8(W, 128 * j, n, k0=r0, nk=nk))
            ps, t = self.gemm(u, nk, n, acts, col0=(128 * j) % n)
            if gate is None:
                a = self.Q.op("dve", lambda e, ps=ps, j=j: e.tensor_tensor(
                    X[j][:, :], X[j][:, :], ps.t[:, :], ALU.add), t, xtok[j])
            else:
                a = self.Q.op("dve", lambda e, ps=ps, j=j: e.scalar_tensor_tensor(
                    out=X[j][:, :], in0=ps.t[:, :], scalar=gate(j), in1=X[j][:, :], op0=ALU.mult, op1=ALU.add),
                    t, xtok[j], self.modtok)
            ps.free = [a]
            xtok[j] = [a]
        for g, _ in tiles:
            g.free = [t]


def program(nc, A, out, consts):
    mem = {}
    draft = Net(nc, A, out, consts, None, mem)
    draft.build()
    net = Net(nc, A, out, consts, draft.units, mem)
    net.build()
    with ExitStack() as ctx:
        net.Q.emit(nc, ctx)


def constants():
    dist = np.maximum(255 - np.arange(384), 0)
    large = 16 + (np.log(np.maximum(dist, 1).astype(np.float32) / np.float32(16)) / np.float32(np.log(8.0))
                  * np.float32(16)).astype(np.int32)
    bucket = np.where(dist < 16, dist, np.minimum(large, 31))
    oneh = (np.arange(32)[:, None] == bucket[None, :]).astype(np.float32)
    t = np.arange(16)
    invc = np.stack([w / np.minimum(t + 1, w) for w in (2, 4, 8, 16)]).astype(np.float32).reshape(1, 64)
    return {"ident": np.eye(128, dtype=np.float32), "flip": np.eye(128, dtype=np.float32)[::-1].copy(), "oneh": oneh, "invc": invc}


_INS = ["x", "g_mix", "w_in", "b_gate", "conv_w", "w_branch_a", "w_branch_b", "w_out", "rel_bias", "g_ffn",
        "w_ffn_gate", "w_ffn_up", "w_ffn_down", "g_final", "c_2", "norm_g_2", "ada_w_2", "ada_b_2", "a_w_in_2",
        "a_w_group_2", "a_scale_2", "a_w_out_2", "kv_norm_g_2", "kv_ada_w_2", "kv_ada_b_2", "w_kv_2", "b_w_in_2",
        "b_sinks_2", "b_w_out_2", "rel_bias_2", "final_g_2"]


def kernel(**inputs):
    import concourse.bacc as _bacc
    from concourse.bass_utils import run_bass_kernel_spmd as _run

    nc = _bacc.Bacc("TRN2", target_bir_lowering=False, num_devices=1)
    arrays, A, C = {}, {}, {}
    for name in _INS:
        a = np.ascontiguousarray(inputs[name])
        arrays[f"in_{name}"] = a
        A[name] = nc.dram_tensor(f"in_{name}", a.shape, F32, kind="ExternalInput").ap()
    for name, a in constants().items():
        arrays[f"c_{name}"] = a
        C[name] = nc.dram_tensor(f"c_{name}", a.shape, F32, kind="ExternalInput").ap()
    out = nc.dram_tensor("out_0", (1, S, 1024), F32, kind="ExternalOutput").ap()
    program(nc, A, out, C)
    r = _run(nc, [arrays], core_ids=[0])
    return r.results[0]["out_0"]
```

```python
from contextlib import ExitStack

import numpy as np

import concourse.bass as bass
from concourse import mybir

F32 = mybir.dt.float32
FR = mybir.dt.float32r
ALU = mybir.AluOpType
ACT = mybir.ActivationFunctionType
AXX = mybir.AxisListType.X

S = 1024
NT = 8
DFF = 2816
T = 4096
BASE = 16640
MAIN = 15
NEG = -1.0e30
FUT = -3.0e38
GONE = -3.3e38

C_B, C_C, C_X, C_Q, C_KV, C_IQ, C_IK, C_GA, C_GB = 0, 512, 1024, 1536, 2048, 2176, 2688, 2760, 3784

V_GMIX, V_GFFN, V_GFIN, V_NORM, V_ADAB, V_KVG, V_KVB, V_SCALE, V_GATE, V_CONV, V_C, V_FIN2 = (
    0, 8, 16, 24, 40, 88, 96, 112, 128, 144, 156, 164)
V_ALL = 172


class Tok:

    __slots__ = ("eng", "idx", "sem", "val", "needed")

    def __init__(self, eng=None, idx=None, sem=None, val=None):
        self.eng, self.idx, self.sem, self.val, self.needed = eng, idx, sem, val, False


class Later:

    def matmul(self, *a, **k):
        return lambda e: e.matmul(*a, **k)

    def transpose(self, *a, **k):
        return lambda e: e.transpose(*a, **k)

    def activation(self, *a, **k):
        return lambda e: e.activation(*a, **k)

    def tensor_tensor(self, *a, **k):
        return lambda e: e.tensor_tensor(*a, **k)

    def scalar_tensor_tensor(self, *a, **k):
        return lambda e: e.scalar_tensor_tensor(*a, **k)

    def tensor_scalar(self, *a, **k):
        return lambda e: e.tensor_scalar(*a, **k)

    def tensor_copy(self, *a, **k):
        return lambda e: e.tensor_copy(*a, **k)

    def reciprocal(self, *a, **k):
        return lambda e: e.reciprocal(*a, **k)

    def memset(self, *a, **k):
        return lambda e: e.memset(*a, **k)

    def affine_select(self, *a, **k):
        return lambda e: e.affine_select(*a, **k)

    def max(self, *a, **k):
        return lambda e: e.max(*a, **k)

    def match_replace(self, *a, **k):
        return lambda e: e.match_replace(*a, **k)

    def tensor_tensor_reduce(self, *a, **k):
        return lambda e: e.tensor_tensor_reduce(*a, **k)

    def tensor_reduce(self, *a, **k):
        return lambda e: e.tensor_reduce(*a, **k)


LATER = Later()


class Queues:

    def __init__(self):
        self.q = {e: [] for e in ("pe", "act", "dve", "pool", "sp")}
        self.dma = {}

    def op(self, eng, fn, *after):
        fn = fn(LATER)
        t = Tok(eng, len(self.q[eng]))
        self.q[eng].append((fn, flat(after), t, None))
        return t

    def load(self, out, in_, sem, *after, eng="sp"):
        self.dma[sem] = self.dma.get(sem, 0) + 16
        t = Tok(sem=sem, val=self.dma[sem])
        self.q[eng].append((lambda e: e.dma_start(out, in_), flat(after), t, sem))
        return t

    def last(self, *engs):
        return [self.q[e][-1][2] for e in engs if self.q[e]]

    def emit(self, nc, ctx):
        for q in self.q.values():
            for _, after, _, _ in q:
                for t in after:
                    t.needed = True
        sems = {e: ctx.enter_context(nc.semaphore("s_" + e)) for e in self.q}
        sems.update({d: ctx.enter_context(nc.semaphore("d_" + d)) for d in self.dma})
        for e, q in self.q.items():
            n = 0
            for _, _, t, sem in q:
                if sem is None and t.needed:
                    n += 1
                    t.sem, t.val = e, n
        block = ctx.enter_context(nc.Block())
        ends = dict(self.dma)

        def run(e, name):
            seen = {}
            for fn, after, t, sem in self.q[name]:
                for a in after:
                    if seen.get(a.sem, 0) < a.val:
                        e.wait_ge(sems[a.sem], a.val)
                        seen[a.sem] = a.val
                ins = fn(e)
                if sem is not None:
                    ins.then_inc(sems[sem], 16)
                elif t.needed:
                    ins.then_inc(sems[name], 1)
            if name == "sp":
                for d, v in ends.items():
                    e.wait_ge(sems[d], v)

        @block.sync
        def _(e):
            run(e, "sp")

        @block.tensor
        def _(e):
            run(e, "pe")

        @block.scalar
        def _(e):
            run(e, "act")

        @block.vector
        def _(e):
            run(e, "dve")

        @block.gpsimd
        def _(e):
            run(e, "pool")


def flat(x):
    out = []
    for a in x:
        if a is None:
            continue
        if isinstance(a, (list, tuple)):
            out += flat(a)
        else:
            out.append(a)
    return out


class Slot:

    def __init__(self, t, name):
        self.t, self.name, self.free = t, name, []


class Ring:
    def __init__(self, slots):
        self.slots, self.n = slots, 0

    def take(self):
        s = self.slots[self.n % len(self.slots)]
        self.n += 1
        return s


class Net:
    def __init__(self, nc, A, out, consts, plan, mem):
        self.nc, self.A, self.out, self.C, self.plan, self.mem = nc, A, out, consts, plan, mem
        self.Q = Queues()
        self.units = []
        self.n_dma = self.n_split = 0
        self.split_no = 0
        self.lo_eng = "pool"
        self.ahead = 3
        self.ada_n = None

    def at(self, name, tile, cols=S, dt=F32, off=0, parts=128):
        key = (name, tile, dt)
        if key not in self.mem:
            self.mem[key] = self.nc.alloc_sbuf_tensor_at(
                name, [parts, cols], dt, offset=BASE + tile * T + off)
        return self.mem[key]

    def main(self, name, i, dt=F32, cols=S, off=0):
        return self.at(name, MAIN + i, cols, dt, off)

    def dram(self, name, shape):
        if name not in self.mem:
            self.mem[name] = self.nc.dram_tensor(name, shape, F32)
        return self.mem[name].ap()

    def setup(self):
        self.raw = [Slot(self.at(f"raw{i}", i), f"raw{i}") for i in range(3)]
        self.wh = [Slot(self.at(f"wh{i}", 3 + i, dt=FR), f"wh{i}") for i in range(3)]
        self.wl = [Slot(self.at(f"wl{i}", 6 + i, dt=FR), f"wl{i}") for i in range(3)]
        self.tmp = Ring([Slot(self.at(f"tmp{i}", 10 + i), f"tmp{i}") for i in range(5)])
        if "ps" not in self.mem:
            self.mem["ps"] = [self.nc.alloc_psum_tensor(f"ps{i}", [128, S], F32) for i in range(4)]
        self.ps = Ring([Slot(t, f"ps{i}") for i, t in enumerate(self.mem["ps"])])
        o = [0]

        def small(name, cols):
            t = self.at(name, 9, cols, off=o[0])
            o[0] += -(-4 * cols // 32) * 32
            return t

        self.ident = small("ident", 128)
        self.ones = small("ones", 128)
        self.flip = small("flip", 128)
        self.vec = small("vec", V_ALL)
        self.mod = small("mod", 64)
        self.gs = small("gs", 24)
        self.iw = small("iw", 64)
        self.cact = small("cact", 8)
        self.r8 = small("r8", 32)
        self.eps = small("eps", 1)
        self.g12 = small("g12", 8)
        self.st = small("st", 128)
        self.m8 = small("m8", 32)
        self.sk = small("sk", 16)
        self.invc = small("invc", 16 * 4)
        assert o[0] <= T, o[0]
        self.oneh = self.at("oneh", 51, 384, parts=32)
        self.rel = self.at("rel", 51, 24, off=1536, parts=32)
        self.gb = self.at("gbias", 51, 384, off=2048, parts=32)

    def issue_dma(self, j):
        parts, _ = self.plan[j]
        slot = self.raw[j % 3]
        for view, src in parts:
            t = self.Q.load(view(slot.t), src, f"raw{j % 3}", slot.free)
        slot.free = []
        self.loaded[j] = t

    def issue_split(self, j):
        _, cols = self.plan[j]
        raw = self.raw[j % 3]
        wh, wl = self.wh[self.n_w % 3], self.wl[self.n_w % 3]
        self.n_w += 1
        v, h, lo = raw.t[:, 0:cols], wh.t[:, 0:cols], wl.t[:, 0:cols]
        a = self.Q.op("act", lambda e: e.activation(h, v, ACT.Copy), self.loaded[j], wh.free)
        eng = self.lo_eng
        b = self.Q.op(eng, lambda e: e.tensor_tensor(lo, v, h.bitcast(F32), ALU.subtract), a, wl.free)
        wh.free, wl.free, raw.free = [], [], [a, b]
        self.ready[j] = (wh, wl, [a, b])

    def advance(self, i):
        if self.plan is None:
            return
        while self.n_split < min(i + self.ahead, len(self.plan)) or self.n_dma < min(i + 4, len(self.plan)):
            if self.n_dma < len(self.plan) and self.n_dma < self.n_split + 3:
                self.issue_dma(self.n_dma)
                self.n_dma += 1
                continue
            if self.n_split < min(i + self.ahead, self.n_dma):
                self.issue_split(self.n_split)
                self.n_split += 1
                continue
            break

    def unit(self, parts, cols=S):
        self.units.append((parts, cols))
        i = len(self.units) - 1
        if self.plan is None:
            return self.wh[0], self.wl[0], []
        self.advance(i)
        return self.ready[i]

    def w8(self, w, c0, n=128, k0=0, nk=8):
        src = w[k0:k0 + nk * 128, c0:c0 + n].rearrange("(k p) n -> p k n", p=128)
        return [(lambda t: t[:, 0:nk * n].rearrange("p (k n) -> p k n", k=nk), src)]

    def gemm(self, unit, nk, n, acts, col0=0, m=128, half=None, ps=None, hooks={}):
        wh, wl, toks = unit
        first = list(toks)
        if ps is None:
            ps = self.ps.take()
            first += ps.free
            ps.free = []
        WH = wh.t[:, 0:nk * n].rearrange("p (k n) -> p k n", k=nk)
        WL = wl.t[:, 0:nk * n].rearrange("p (k n) -> p k n", k=nk)
        halves = (0, 1) if half is None else (half,)
        for k in range(nk):
            hi, lo = acts[k][0:2]
            wk, lk = WH[:, k, col0:col0 + m], WL[:, k, col0:col0 + m]
            seq = [(i, w, a, h) for i, (w, a) in enumerate([(wk, hi), (wk, lo), (lk, hi)]) for h in halves]
            for i, w, a, h in seq:
                o, r = ps.t[0:m, h * 512:h * 512 + 512], a[:, h * 512:h * 512 + 512]
                t = self.Q.op("pe", lambda e, o=o, w=w, r=r, s=(k == 0 and i == 0), z=(k == nk - 1 and i == 2):
                              e.matmul(o, w, r, start=s, stop=z), first, acts[k][2 + h] if i == 0 else None)
                first = []
            if k in hooks:
                hooks[k]()
        wh.free = wl.free = [t]
        if self.ada_n is not None and self.ada_n < 64 and nk > 2:
            self.ada_step()
        return ps, t

    def ada_start(self, bufs, free, ready):
        self.ada = [Slot(t, f"ada{i}") for i, t in enumerate(bufs)]
        for s in self.ada:
            s.free = free
        self.ada_n, self.ada_ready, self.adal = 0, ready, []
        self.acc4, self.acc4_free = self.at("acc4", 51, 512), free
        for c in range(len(bufs)):
            self.ada_load(c)

    def ada_load(self, c):
        A = self.A
        w, col = ((A["ada_w_2"][0], c), (A["ada_w_2"][1], c - 24), (A["kv_ada_w_2"], c - 48))[min(c // 24, 2)]
        s = self.ada[c % len(self.ada)]
        (view, src), = self.w8(w, 128 * col)
        self.adal.append(self.Q.load(view(s.t), src, s.name, s.free))

    def ada_step(self):
        Q, c = self.Q, self.ada_n
        self.ada_n += 1
        s = self.ada[c % len(self.ada)]
        v = s.t[:, :].rearrange("p (k n) -> p k n", k=8)
        t = Q.op("dve", lambda e: e.tensor_tensor(
            v, v, self.cact[:, :].unsqueeze(2).to_broadcast([128, 8, 128]), ALU.mult), self.adal[c], self.ada_ready)
        o = self.acc4[:, (c % 4) * 128:(c % 4) * 128 + 128]
        t = Q.op("dve", lambda e: e.tensor_reduce(o, s.t[:, :].rearrange("p (k n) -> p n k", k=8), AXX, ALU.add),
                 t, self.acc4_free)
        s.free = [t]
        if c + len(self.ada) < 64:
            self.ada_load(c + len(self.ada))
        if c % 4 == 3:
            ps = self.ps.take()
            for i in range(4):
                m = Q.op("pe", lambda e: e.matmul(ps.t[:, i:i + 1], self.acc4[:, i * 128:i * 128 + 128],
                                                  self.ones[:, 0:1], start=True, stop=True), t, ps.free)
            self.acc4_free = [m]
            b = (V_ADAB if c < 48 else V_KVB - 48) + c - 3
            self.adat = Q.op("dve", lambda e: e.tensor_tensor(
                self.mod[:, c - 3:c + 1], ps.t[:, 0:4], self.vec[:, b:b + 4], ALU.add), m)
            ps.free = [self.adat]

    def split(self, src, hi, lo, *after, free=(), eng=None):
        a = self.Q.op("act", lambda e: e.activation(hi, src, ACT.Copy), after, free)
        b = self.Q.op(eng or self.lo_eng, lambda e: e.tensor_tensor(lo, src, hi.bitcast(F32), ALU.subtract),
                      a, after, free)
        return [a, b]

    def split_ps(self, src, hi, lo, *after, scale=1.0, free=()):
        a = self.Q.op("act", lambda e: e.activation(hi, src, ACT.Copy, scale=scale), after, free)
        b = self.Q.op("dve", lambda e: e.scalar_tensor_tensor(
            out=lo, in0=src, scalar=scale, in1=hi.bitcast(F32), op0=ALU.mult, op1=ALU.subtract), a, free)
        return [a, b]

    def prods(self, o, L, R, first, last, after):
        seq = [(L[0], R[0]), (L[0], R[1]), (L[1], R[0])]
        for i, (a, b) in enumerate(seq):
            t = self.Q.op("pe", lambda e, a=a, b=b, s=(first and i == 0), z=(last and i == 2):
                          e.matmul(o, a, b, start=s, stop=z), after if i == 0 else None)
        return t

    def norm_open(self, X, g1=None):
        slots = [self.tmp.take() for _ in range(5)]
        self.X, self.g1 = X, g1
        keep = 3 if g1 is not None else 2
        self.acc, self.R = slots[0], slots[1]
        self.acc2 = slots[2] if keep == 3 else None
        self.parts = slots[keep:]
        self.hs = Ring([Slot(x.t[:, c:c + 512], x.name) for x in self.parts for c in (0, 512)])
        for i, x in enumerate(self.hs.slots):
            x.free = list(self.parts[i // 2].free)
        self.acct, self.rt, self.acct2, self.rt2 = [None, None], [None, None], [None, None], [None, None]
        self.htok = [[None] * NT, [None] * NT]
        self.used = []

    def norm_close(self):
        for i, x in enumerate(self.parts):
            x.free = self.hs.slots[2 * i].free + self.hs.slots[2 * i + 1].free
        for x in (self.acc, self.R, self.acc2):
            if x is not None:
                x.free = self.used
        return self.htok

    def square(self, j, h, tok):
        Q, c = self.Q, slice(h * 512, h * 512 + 512)
        x = self.X[j][:, c]
        todo = [(self.acc, self.acct, "dve", 1.0)]
        if self.g1 is not None:
            todo.append((self.acc2, self.acct2, "pool", self.g1(j)))
        for acc, at, eng, sc in todo:
            if eng == "pool" and (h == 0 or j % 2):
                eng = "dve"
            if j == 0:
                at[h] = Q.op("act", lambda e: e.activation(acc.t[:, c], x, ACT.Square, scale=sc), tok, acc.free)
            else:
                s = self.hs.take()
                a = Q.op("act", lambda e: e.activation(s.t, x, ACT.Square, scale=sc), tok, s.free)
                at[h] = Q.op(eng, lambda e: e.tensor_tensor(acc.t[:, c], acc.t[:, c], s.t, ALU.add), a, at[h])
                s.free = [at[h]]

    def sums(self, h, diagonal=True):
        Q = self.Q
        ps = self.ps.take()
        two = self.g1 is not None
        n = 8 if two else 4
        r = self.r8[:, h * 16:h * 16 + n]
        for i in range(4):
            c = slice(h * 512 + i * 128, h * 512 + i * 128 + 128)
            m = Q.op("pe", lambda e: e.matmul(ps.t[:, i:i + 1], self.acc.t[:, c], self.ones[:, 0:1],
                                              start=True, stop=True), self.acct[h], ps.free, self.ctok)
            if two:
                m2 = Q.op("pe", lambda e: e.matmul(ps.t[:, 512 + i:513 + i], self.acc2.t[:, c], self.ones[:, 0:1],
                                                   start=True, stop=True), self.acct2[h])
        self.used = self.used + [m]
        t = Q.op("dve", lambda e: e.tensor_scalar(r[:, 0:4], ps.t[:, 0:4], 1.0 / S, 1e-6, ALU.mult, ALU.add), m)
        if two:
            t = Q.op("dve", lambda e: e.tensor_scalar(r[:, 4:8], r[:, 0:4], 1e-6, None, ALU.mult), t)
            t = Q.op("dve", lambda e: e.scalar_tensor_tensor(
                out=r[:, 4:8], in0=ps.t[:, 512:516], scalar=1.0 / S, in1=r[:, 4:8], op0=ALU.mult, op1=ALU.add), t, m2)
        a = Q.op("act", lambda e: e.activation(r, r, ACT.Sqrt), t)
        t = Q.op("dve", lambda e: e.reciprocal(r, r), a)
        self.spread = []
        if not diagonal:
            ps.free = [t]
            return r, t
        for k in range(n // 4):
            dg = self.hs.take()
            d = Q.op("dve", lambda e: e.tensor_tensor(
                dg.t.rearrange("p (t c) -> p t c", t=4),
                self.ident[:, :].unsqueeze(1).to_broadcast([128, 4, 128]),
                r[:, 4 * k:4 * k + 4].unsqueeze(2).to_broadcast([128, 4, 128]), ALU.mult), t, dg.free)
            self.spread.append((ps, dg, d))

    def rstd(self, h):
        Q, c = self.Q, slice(h * 512, h * 512 + 512)
        for k, (ps, dg, d) in enumerate(self.spread):
            p = ps.t[:, k * 512:k * 512 + 512]
            m = Q.op("pe", lambda e: e.matmul(p, self.ones[:, :], dg.t, start=True, stop=True), d)
            dg.free = [m]
            R = (self.R, self.acc2)[k]
            a = Q.op("act", lambda e: e.activation(R.t[:, c], p, ACT.Copy), m, R.free if k == 0 else None)
            if k == 0:
                self.rt[h] = a
            else:
                self.rt2[h] = a
            ps.free = [a]

    def scaled(self, h, g, hi, lo, free, shift=None):
        Q, c = self.Q, slice(h * 512, h * 512 + 512)
        r, rt = (self.R.t, self.rt[h]) if self.g1 is None else (self.acc2.t, self.rt2[h])
        last = None
        for j in range(NT + 1):
            if j < NT:
                s = self.hs.take()
                H, L = hi[j][:, c], lo[j][:, c]
                a = Q.op("dve", lambda e: e.scalar_tensor_tensor(
                    out=s.t, in0=self.X[j][:, c], scalar=g(j), in1=r[:, c], op0=ALU.mult, op1=ALU.mult), rt, s.free)
                self.used = self.used + [a]
                plain = shift is None or j % 2 == 1
                if shift is not None and plain:
                    a = Q.op("act", lambda e: e.activation(s.t, s.t, ACT.Identity, bias=shift(j)), a)
                if plain:
                    b = Q.op("act", lambda e: e.activation(H, s.t, ACT.Copy), a, free)
                else:
                    b = Q.op("act", lambda e: e.activation(H, s.t, ACT.Identity, bias=shift(j)), a, free)
                this = (j, s, H, L, a, b, plain)
            else:
                this = None
            if last is not None:
                k, s0, H0, L0, a0, b0, plain0 = last
                if plain0:
                    d = Q.op("pool" if k % 2 else "dve", lambda e: e.tensor_tensor(
                        L0, s0.t, H0.bitcast(F32), ALU.subtract), b0, a0, free)
                else:
                    d = Q.op("dve", lambda e: e.scalar_tensor_tensor(
                        out=L0, in0=s0.t, scalar=shift(k), in1=H0.bitcast(F32), op0=ALU.add, op1=ALU.subtract), b0, free)
                s0.free = [b0, d]
                self.htok[h][k] = [b0, d]
            last = this

    def times_norm(self, h, g, js=range(NT)):
        c = slice(h * 512, h * 512 + 512)
        out = []
        for j in js:
            t = self.Q.op("dve", lambda e: e.scalar_tensor_tensor(
                out=self.X[j][:, c], in0=self.X[j][:, c], scalar=g(j), in1=self.R.t[:, c], op0=ALU.mult, op1=ALU.mult),
                self.rt[h])
            out.append(t)
        self.used = self.used + [t]
        return out

    def by_halves(self, product, update, xtok, middle):
        done = self.summed = [[None] * NT, [None] * NT]
        for h in range(2):
            c = slice(h * 512, h * 512 + 512)
            for j in range(NT):
                ps, t = product(j, h)
                t = update(j, c, ps.t[:, c], t, xtok[j])
                ps.free = [t]
                done[h][j] = t
                self.square(j, h, t)
                if h == 1 and j in middle:
                    middle[j]()
        for j in range(NT):
            xtok[j] = [done[0][j], done[1][j]]

    def first_two(self, make, second, hi, lo, rstd=True):
        old, self.ahead = self.ahead, 2
        us = [self.unit(parts, cols) for parts, _, _, cols in make]
        acts = [(hi[k], lo[k], self.htok[0][k], self.htok[1][k]) for k in range(NT)]
        out = []
        for i, (_, n, m, _) in enumerate(make):
            hooks = {} if not rstd else {1: lambda: self.rstd(1)} if i else {5: lambda: self.sums(1)}
            out.append(self.gemm(us[i], 8, n, acts, m=m, half=0, hooks=hooks)[0])
        second()
        acts = [(hi[k], lo[k], self.htok[0][k], self.htok[1][k]) for k in range(NT)]
        res = []
        for i, (_, n, m, _) in enumerate(make):
            res.append(self.gemm(us[i], 8, n, acts, m=m, half=1, ps=out[i]))
        self.ahead = old
        return res

    def both(self):
        return [[self.htok[0][k], self.htok[1][k]] for k in range(NT)]

    def acts(self, hi, lo, toks):
        return [(h, l, t, t) for h, l, t in zip(hi, lo, toks)]

    def build(self):
        Q, A = self.Q, self.A
        self.loaded, self.ready, self.n_w = {}, {}, 0
        self.setup()
        C = self.C
        idt = Q.load(self.ident[:, :], C["ident"], "id")
        xn = [self.main(f"xn{i}", 24 + i) for i in range(NT)]
        for i in range(NT):
            xn[i] = (xn[i], Q.load(xn[i][:, :], A["x"][0, i * 128:(i + 1) * 128, :], f"xn{i}"))
        c0 = [Q.load(self.flip[:, :], C["flip"], "c"), Q.load(self.oneh[:, :], C["oneh"], "c"),
              Q.load(self.rel[:, 0:8], A["rel_bias"], "c"), Q.load(self.rel[:, 8:24], A["rel_bias_2"], "c"),
              Q.load(self.invc[:, :], C["invc"].to_broadcast([128, 64]), "c"),
              Q.load(self.sk[:, :], A["b_sinks_2"].to_broadcast([128, 16]), "c")]
        va, vb = Slot(self.main("va", 32), "va"), Slot(self.main("vb", 33), "vb")
        rows = [("g_mix", V_GMIX), ("g_ffn", V_GFFN), ("g_final", V_GFIN), ("norm_g_2", V_NORM),
                ("ada_b_2", V_ADAB), ("kv_norm_g_2", V_KVG), ("kv_ada_b_2", V_KVB), ("a_scale_2", V_SCALE),
                ("b_gate", V_GATE), ("conv_w", V_CONV), ("c_2", V_C), ("final_g_2", V_FIN2)]
        for name, r in rows:
            ap = A[name]
            if len(ap.shape) == 1:
                flatv = ap
            elif len(ap.shape) == 2:
                flatv = ap.rearrange("a b -> (a b)")
            else:
                flatv = ap.rearrange("a b c -> (a b c)")
            n = flatv.shape[0] // 128
            src = flatv.rearrange("(r p) -> r p", p=128)
            n1 = max(0, min(n, 128 - r))
            if n1:
                cc = Q.load(va.t[r:r + n1, 0:128], src[0:n1, :], "c")
            if n > n1:
                cc = Q.load(vb.t[r + n1 - 128:r + n - 128, 0:128], src[n1:n, :], "c")
        z1 = Q.op("pool", lambda e: e.memset(self.ones[:, :], 1.0))
        z2 = Q.op("pool", lambda e: e.memset(self.eps[:, :], 1e-6))
        self.ctok = [idt, z1, z2]

        X = [self.main(f"xt{j}", 16 + j) for j in range(NT)]
        hi = [self.main(f"ah{j}", j, FR) for j in range(NT)]
        lo = [self.main(f"al{j}", 8 + j, FR) for j in range(NT)]
        self.norm_open(X)
        self.copied = [[] for _ in range(NT)]
        self.transposed(xn, X, 0)
        self.advance(-1)
        ps = self.ps.take()
        Q.op("pe", lambda e: e.transpose(ps.t[:, 0:128], va.t[:, 0:128], self.ident[:, :]), cc, ps.free)
        tv = Q.op("pe", lambda e: e.transpose(ps.t[:, 128:V_ALL], vb.t[0:V_ALL - 128, 0:128],
                                              self.ident[0:V_ALL - 128, 0:V_ALL - 128]))
        vv = Q.op("dve", lambda e: e.tensor_copy(self.vec[:, :], ps.t[:, 0:V_ALL]), tv)
        ps.free = [vv]
        vec = lambda base: (lambda j: self.vec[:, base + j:base + j + 1])
        ca = Q.op("act", lambda e: e.activation(self.cact[:, :], self.vec[:, V_C:V_C + 8], ACT.Silu), vv)

        def middle():
            self.rstd(0)
            self.scaled(0, vec(V_GMIX), hi, lo, None)

        self.transposed(xn, X, 1, {1: lambda: self.sums(0), 3: middle})
        W = A["w_in"][0]

        qh = [self.main(f"qh{j}", 16 + j, FR) for j in range(4)]
        ql = [self.main(f"ql{j}", 20 + j, FR) for j in range(4)]
        KE, KO, LE, LO = (self.main(f"kp{i}", 24 + i, FR) for i in range(4))
        kt, kt2 = self.main("kt", 33), self.main("kt2", 34)
        (ps, t), q0 = self.first_two(
            [(self.w8(W, C_IK, 72), 72, 72, 576), (self.w8(W, C_IQ), 128, 128, S)],
            lambda: self.scaled(1, vec(V_GMIX), hi, lo, None), hi, lo)
        xd = self.dram("xd", [S, S])
        xdt = [Q.load(xd[j * 128:j * 128 + 128, :], X[j][:, :], f"xs{j}", self.copied[j]) for j in range(NT)]

        psb = self.ps.take()
        tb = Q.op("pe", lambda e: e.matmul(psb.t[0:24, 0:384], self.rel[:, :], self.oneh[:, :],
                                           start=True, stop=True), cc, psb.free)
        tb = Q.op("dve", lambda e: e.tensor_copy(self.gb[0:24, :], psb.t[0:24, 0:384]), tb)
        psb.free = [tb]
        gd = self.dram("gdist", [24, 384])
        gst = Q.load(gd, self.gb[0:24, :], "gst", tb)
        self.norm_close()
        htok = self.both()
        h = self.acts(hi, lo, htok)
        dead = [htok, xdt, Q.last("dve")]
        zz = self.zero_pads([(KE, 64), (LE, 64), (KO, 0), (LO, 0)], dead)
        t = Q.op("act", lambda e, ps=ps: e.activation(kt[0:72, :], ps.t[0:72, :], ACT.Copy), t, dead)
        ps.free = [t]
        ktt = self.k_pads(kt, kt2, (KE, LE, KO, LO), [t, zz], "swap0", [])
        ps = self.ps.take()
        for i in range(NT):
            t = Q.op("pe", lambda e, i=i, ps=ps: e.transpose(ps.t[:, i * 72:i * 72 + 72] if i < 7 else ps.t[:, 512:584],
                                                      kt[0:72, i * 128:i * 128 + 128], self.ident[0:72, 0:72]),
                     t if i == 0 else None, ps.free)
        for i in range(NT):
            c = i * 72 if i < 7 else 512
            t = Q.op("dve", lambda e, i=i, c=c, ps=ps: e.tensor_scalar(
                self.iw[:, i * 8:i * 8 + 8], ps.t[:, c + 64:c + 72], 512.0 ** -0.5, None, ALU.mult), t)
        ps.free = [t]
        iwt = t
        qt = []
        for j in range(4):
            if j:
                u = self.unit(self.w8(W, C_IQ + 128 * j))
                ps, t = self.gemm(u, 8, 128, h)
            else:
                ps, t = q0
            t = self.split_ps(ps.t[:, :], qh[j][:, :], ql[j][:, :], t, free=dead)
            ps.free = t[1:]
            qt.append(t)
        smt = {}
        off = [0]
        for b in range(NT):
            off.append(off[-1] + (b + 1) * 128)
        SMt = self.main("sm", 28, cols=off[-1])
        SM = [SMt[:, off[b]:off[b + 1]] for b in range(NT)]
        for b in range(2):
            t = Q.op("pool", lambda e, b=b: e.memset(SM[b], 0.0), dead)
            smt[b] = [Q.op("pool", lambda e, b=b: e.affine_select(
                out=SM[b][:, b * 128:b * 128 + 128], in_=SM[b][:, b * 128:b * 128 + 128],
                compare_op=ALU.is_ge, fill=NEG, base=0, pattern=[[-1, 128]], channel_multiplier=1), t)]
        for b in range(2, NT):
            Wd = (b + 1) * 128
            st = dead
            for hd in range(8):
                j, odd = hd // 2, hd % 2
                K = (KO, LO) if odd else (KE, LE)
                ps, t = self.logits((qh[j], ql[j]), K, b, Wd, [qt[j], ktt])
                r = self.tmp.take()
                a = Q.op("act", lambda e, ps=ps, r=r, Wd=Wd: e.activation(
                    r.t[:, 0:Wd], ps.t[:, 0:Wd], ACT.Relu), t, r.free)
                ps.free = [a]
                iwc = self.iw[:, b * 8 + hd:b * 8 + hd + 1]
                if hd == 0:
                    st = Q.op("dve", lambda e, b=b, r=r, Wd=Wd, iwc=iwc: e.tensor_scalar(
                        SM[b], r.t[:, 0:Wd], iwc, None, ALU.mult), a, st, iwt)
                else:
                    st = Q.op("dve", lambda e, b=b, r=r, Wd=Wd, iwc=iwc: e.scalar_tensor_tensor(
                        out=SM[b], in0=r.t[:, 0:Wd], scalar=iwc, in1=SM[b], op0=ALU.mult, op1=ALU.add), a, st)
                r.free = [st]
            smt[b] = Q.op("pool", lambda e, b=b: e.affine_select(
                out=SM[b][:, b * 128:b * 128 + 128], in_=SM[b][:, b * 128:b * 128 + 128],
                compare_op=ALU.is_ge, fill=FUT, base=0, pattern=[[-1, 128]], channel_multiplier=1), st)
        index_done = Q.last("pe")
        for b0 in range(2, NT, 2):
            for r in range(32):
                for b in (b0, b0 + 1):
                    m8 = self.m8[:, (2 * (b % 2) + r % 2) * 8:(2 * (b % 2) + r % 2) * 8 + 8]
                    smt[b] = Q.op("dve", lambda e: e.max(m8, SM[b]), smt[b])
                for b in (b0, b0 + 1):
                    m8 = self.m8[:, (2 * (b % 2) + r % 2) * 8:(2 * (b % 2) + r % 2) * 8 + 8]
                    smt[b] = Q.op("dve", lambda e: e.match_replace(SM[b], m8, SM[b], GONE), smt[b])
            for b in (b0, b0 + 1):
                smt[b] = Q.op("dve", lambda e: e.tensor_scalar(SM[b], SM[b], -3.2e38, NEG, ALU.is_ge, ALU.mult), smt[b])

        cv = self.dram("cv", [512, S])
        cvt = []
        for j in range(4):
            u = self.unit(self.w8(W, C_C + 128 * j))
            ps, t = self.gemm(u, 8, 128, h)
            x1 = self.tmp.take()
            t1 = Q.op("act", lambda e, ps=ps, x1=x1: e.activation(x1.t[:, :], ps.t[:, :], ACT.Copy), t, x1.free)
            ps.free = [t1]
            u = self.unit(self.w8(W, C_X + 128 * j))
            ps, t = self.gemm(u, 8, 128, h)
            x2 = self.tmp.take()
            t2 = Q.op("act", lambda e, ps=ps, x2=x2: e.activation(x2.t[:, :], ps.t[:, :], ACT.Copy), t, x2.free)
            ps.free = [t2]
            t1 = Q.op("pool", lambda e, x1=x1, x2=x2: e.tensor_tensor(x1.t[:, :], x1.t[:, :], x2.t[:, :], ALU.mult), t1, t2)
            y = self.tmp.take()
            w = [self.vec[:, V_CONV + 4 * k + j:V_CONV + 4 * k + j + 1] for k in range(3)]
            t3 = Q.op("pool", lambda e, x1=x1, y=y, w=w: e.tensor_scalar(y.t[:, :], x1.t[:, :], w[2], None, ALU.mult), t1, y.free, vv)
            for sh in (1, 2):
                t4 = Q.op("pool", lambda e, x1=x1, x2=x2, w=w, sh=sh: e.tensor_scalar(
                    x2.t[:, 0:S - sh], x1.t[:, 0:S - sh], w[2 - sh], None, ALU.mult), t3)
                t3 = Q.op("pool", lambda e, x2=x2, y=y, sh=sh: e.tensor_tensor(
                    y.t[:, sh:S], y.t[:, sh:S], x2.t[:, 0:S - sh], ALU.add), t4)
            x1.free = x2.free = [t3]
            u = self.unit(self.w8(W, C_B + 128 * j))
            ps, t = self.gemm(u, 8, 128, h)
            x3 = self.tmp.take()
            t2 = Q.op("act", lambda e, ps=ps, x3=x3: e.activation(x3.t[:, :], ps.t[:, :], ACT.Copy), t, x3.free)
            ps.free = [t2]
            t3 = Q.op("pool", lambda e, x3=x3, y=y: e.tensor_tensor(y.t[:, :], y.t[:, :], x3.t[:, :], ALU.mult), t2, t3)
            x3.free = [t3]
            cvt.append(Q.load(cv[j * 128:j * 128 + 128, :], y.t[:, :], "st_" + y.name, t3))
            y.free = [cvt[-1]]

        gd_ = self.dram("gates", [2048, S])
        gt = []
        for j in range(16):
            u = self.unit(self.w8(W, C_GA + 128 * j))
            ps, t = self.gemm(u, 8, 128, h)
            g = self.tmp.take()
            t = Q.op("act", lambda e, ps=ps, g=g, j=j: e.activation(g.t[:, :], ps.t[:, :], ACT.Sigmoid,
                                                                   bias=vec(V_GATE)(j)), t, g.free, vv)
            ps.free = [t]
            gt.append(Q.load(gd_[j * 128:j * 128 + 128, :], g.t[:, :], "st_" + g.name, t))
            g.free = [gt[-1]]

        u = self.unit(self.w8(W, C_KV))
        ps, t = self.gemm(u, 8, 128, h)
        t = Q.op("act", lambda e, ps=ps: e.activation(kt[:, :], ps.t[:, :], ACT.Copy), t, ktt)
        ps.free = [t]
        kvt = t
        ktt = self.k_pads(kt, kt2, (KE, LE, KO, LO), [t], "swap1", index_done)
        qt = []
        for j in range(4):
            u = self.unit(self.w8(W, C_Q + 128 * j))
            ps, t = self.gemm(u, 8, 128, h)
            s = self.tmp.take()
            t = Q.op("act", lambda e, ps=ps, s=s: e.activation(s.t[:, :], ps.t[:, :], ACT.Copy), t, s.free)
            ps.free = [t]
            t = self.split(s.t[:, :], qh[j][:, :], ql[j][:, :], t, free=index_done, eng="dve" if j == 3 else "pool")
            s.free = t
            qt.append(t)
            if j == 1:
                T1 = self.main("t1", 34, cols=2048)
                t1t = self.table_flip(T1, self.table_load(T1, gd, 0, "t1", [gst, ktt]))
                t1s = []
                for hd in range(8):
                    t1s.append(Q.op("dve", lambda e: e.tensor_scalar(
                        T1[:, hd * 256:hd * 256 + 256], T1[:, hd * 256:hd * 256 + 256], T1[:, hd * 256:hd * 256 + 1],
                        None, ALU.subtract), t1t))
        projected = Q.last("pe")

        VE, VO, VLE, VLO = (self.main(f"vp{i}", i, FR) for i in range(4))
        ptb = [(self.main(f"pth{i}", (4, 12)[i], FR, cols=2048), self.main(f"ptl{i}", (6, 14)[i], FR, cols=2048))
               for i in range(2)]
        ptf = [projected, projected]
        OT = self.main("ot", 8, cols=4096)
        zz = self.zero_v([(VE, 64), (VLE, 64), (VO, 0), (VLO, 0)], projected)
        vt = self.v_pads(kt, (VE, VLE, VO, VLO), 64, 64, kvt, zz)
        items = [(b, hd) for b in range(NT) for hd in (0, 2, 1, 3, 4, 6, 5, 7)]
        st = {}

        def score(n):
            b, hd = items[n]
            Wd = (b + 1) * 128
            K = (KO, LO) if hd % 2 else (KE, LE)
            j = hd // 2
            st[n] = self.logits((qh[j], ql[j]), K, b, Wd, [qt[j], ktt])

        def top(n):
            b, hd = items[n]
            Wd = (b + 1) * 128
            ps, t = st[n]
            L = self.tmp.take()
            near = min(Wd, 256)
            far = Wd - near
            mf, mx, nm, sm, rs = (self.st[:, (n % 8) * 8 + i:(n % 8) * 8 + i + 1] for i in range(5))
            if far:
                f = Q.op("dve", lambda e: e.tensor_tensor_reduce(
                    L.t[:, 0:far], ps.t[:, 0:far], SM[b][:, 0:far], 0.125, -3.0e38, ALU.add, ALU.max, mf),
                    t, L.free, smt[b])
            t = Q.op("dve", lambda e: e.scalar_tensor_tensor(
                out=L.t[:, far:Wd], in0=ps.t[:, far:Wd], scalar=0.125,
                in1=T1[:, hd * 256 + 256 - near:hd * 256 + 256], op0=ALU.mult, op1=ALU.add), t, L.free, t1s[hd])
            ps.free = [t]
            t = Q.op("dve", lambda e: e.tensor_tensor_reduce(
                L.t[:, far:Wd], L.t[:, far:Wd], SM[b][:, far:Wd], 1.0, mf if far else -3.0e38,
                ALU.add, ALU.max, mx), t, smt[b], [f] if far else None)
            t = Q.op("dve", lambda e: e.tensor_scalar(nm, mx, -1.0, None, ALU.mult), t)
            st[n] = (L, t, nm, sm, rs)

        def exps(n):
            b, hd = items[n]
            Wd = (b + 1) * 128
            L, t, nm, sm, rs = st[n]
            t = Q.op("act", lambda e: e.activation(L.t[:, 0:Wd], L.t[:, 0:Wd], ACT.Exp, bias=nm, accum_out=sm), t)
            st[n] = (L, t, sm, rs)

        def norm(n):
            b, hd = items[n]
            Wd = (b + 1) * 128
            L, t, sm, rs = st[n]
            t = Q.op("dve", lambda e: e.reciprocal(rs, sm), t)
            if n % 2:
                t = Q.op("act", lambda e: e.activation(L.t[:, 0:Wd], L.t[:, 0:Wd], ACT.Copy, scale=rs), t)
            else:
                t = Q.op("dve", lambda e: e.tensor_scalar(L.t[:, 0:Wd], L.t[:, 0:Wd], rs, None, ALU.mult), t)
            st[n] = (L, t)

        def turn(n):
            b, hd = items[n]
            L, t = st[n]
            ps = self.ps.take()
            for i in range(b + 1):
                m = Q.op("pe", lambda e: e.transpose(
                    ps.t[:, i * 128:i * 128 + 128], L.t[:, i * 128:i * 128 + 128], self.ident[:, :]), t, ps.free)
            L.free = [m]
            st[n] = (ps, m)

        def turned(n):
            b, hd = items[n]
            Wd = (b + 1) * 128
            ps, t = st[n]
            g = n // 2 % 2
            PH, PL = (p[:, 0:2 * Wd].rearrange("p (i h c) -> p i h c", h=2, c=128)[:, :, n % 2, :] for p in ptb[g])
            src = ps.t[:, 0:Wd].rearrange("p (i c) -> p i c", c=128)
            t = self.split_ps(src, PH, PL, t, free=ptf[g])
            ps.free = t[1:]
            st[n] = t

        def values(n, part):
            b, hd = items[n]
            if n % 2 == 0:
                return
            odd, g = hd % 2, n // 2 % 2
            if not odd and part == 0:
                st["po"] = self.po.take()
            po = st["po"]
            V = (VO, VLO) if odd else (VE, VLE)
            PH, PL = ptb[g]
            mid = (b + 2) // 2
            for i in (range(mid, b + 1) if part else range(mid)):
                c, c2 = slice(i * 128, i * 128 + 128), slice(i * 256, i * 256 + 256)
                t = self.prods(po.t[:, 0:256], (V[0][:, c], V[1][:, c]), (PH[:, c2], PL[:, c2]),
                               odd == 0 and i == 0, odd == 1 and i == b, [st[n - 1], st[n], po.free, vt])
                st["t"] = t
            if part:
                ptf[g] = [st["t"]]
                st["po", n] = (po, st["t"])

        def stored(n):
            b, hd = items[n]
            if n % 4 != 3:
                return
            po, t = st["po", n]
            j0 = hd // 4 * 2
            o = OT[:, :].rearrange("p (j t) -> p j t", j=4)[:, j0:j0 + 2, b * 128:b * 128 + 128]
            t = Q.op("act", lambda e: e.activation(o, po.t[:, 0:256].rearrange("p (j t) -> p j t", j=2), ACT.Copy),
                     t, projected)
            po.free = [t]

        self.part_psum()
        self.pipeline(len(items), [
            (0, score), (3, turn), (5, lambda n: values(n, 1)), (4, lambda n: values(n, 0)), (2, norm), (0, top),
            (6, stored), (3, turned), (0, exps)])
        self.join_psum()
        attended = Q.last("pe", "dve", "act")

        ch = [self.main(f"ch{j}", 32 + j, FR) for j in range(4)]
        cl = [self.main(f"cl{j}", j, FR) for j in range(4)]
        ctk = []
        for j in range(4):
            s = self.tmp.take()
            t = Q.load(s.t[:, :], cv[j * 128:j * 128 + 128, :], "ld_" + s.name, s.free, cvt[j])
            t = self.split(s.t[:, :], ch[j][:, :], cl[j][:, :], t, free=attended)
            s.free = t
            ctk.append(t)
        oh = [self.main(f"oh{j}", 4 + j, FR) for j in range(4)]
        ol = [self.main(f"ol{j}", 12 + j, FR) for j in range(4)]
        ott = [self.split(OT[:, j * S:j * S + S], oh[j][:, :], ol[j][:, :], attended, eng="dve") for j in range(4)]
        X = [self.main(f"X{j}", 8 + j) for j in range(NT)]
        xtok = [[Q.load(X[j][:, :], xd[j * 128:j * 128 + 128, :], f"xl{j}", attended, ott, xdt[j])] for j in range(4)]
        mh = [self.main(f"mh{j}", 16 + j, FR) for j in range(8)]
        ml = [self.main(f"ml{j}", 24 + j, FR) for j in range(8)]
        mtk = []
        for j0 in range(0, 8, 2):
            held = []
            for w, acts, r0, gt0 in ((A["w_branch_a"][0], self.acts(ch, cl, ctk), 0, 0),
                                     (A["w_branch_b"][0], self.acts(oh, ol, ott), 1024, 8)):
                u = self.unit(self.w8(w, 128 * j0, 256, nk=4))
                for j in (j0, j0 + 1):
                    y, ty = self.gemm(u, 4, 256, acts, col0=128 * (j - j0))
                    s = self.tmp.take()
                    t = Q.load(s.t[:, :], gd_[r0 + j * 128:r0 + j * 128 + 128, :], "ld_" + s.name, s.free, gt[gt0 + j])
                    t = Q.op("dve", lambda e: e.tensor_tensor(s.t[:, :], y.t[:, :], s.t[:, :], ALU.mult), t, ty)
                    y.free = [t]
                    if r0 == 0:
                        held.append((s, t))
                        continue
                    s1, t1 = held[j - j0]
                    t = Q.op("dve", lambda e: e.tensor_tensor(s1.t[:, :], s1.t[:, :], s.t[:, :], ALU.add), t, t1)
                    s.free = [t]
                    s1.free = self.split(s1.t[:, :], mh[j][:, :], ml[j][:, :], t, free=attended)
                    mtk.append(s1.free)
        branched = Q.last("pe")
        xtok += [[Q.load(X[j][:, :], xd[j * 128:j * 128 + 128, :], f"xl{j}", branched, xdt[j])] for j in range(4, 8)]

        def add(j, c, p, t, xt):
            return Q.op("dve", lambda e: e.tensor_tensor(X[j][:, c], X[j][:, c], p, ALU.add), t, xt)

        self.norm_open(X)
        hi = [self.main(f"bh{j}", 16 + j, FR) for j in range(NT)]
        lo = [self.main(f"bl{j}", 24 + j, FR) for j in range(NT)]
        half_done = {}

        def product(j, hf):
            u = self.unit(self.w8(A["w_out"][0], 128 * j))
            r = self.gemm(u, 8, 128, self.acts(mh, ml, mtk), half=hf)
            half_done[hf] = [r[1]]
            return r

        def middle():
            self.sums(0)

        def middle2():
            self.rstd(0)
            self.scaled(0, vec(V_GFFN), hi, lo, half_done[0])

        self.by_halves(product, add, xtok, {1: middle, 2: middle2})

        gtile = [32, 33, 34, 35, 0, 1, 2, 3, 4, 5, 6, 7]
        self.G = Ring([Slot((self.main(f"gh{i}", gtile[i], FR), self.main(f"gl{i}", gtile[6 + i], FR)), f"g{i}")
                       for i in range(6)])
        done = Q.last("pe")
        for s in self.G.slots:
            s.free = done
        self.G.slots = self.G.slots[0:5]
        self.ada_start([self.main("ada0", 1), self.main("ada1", 7)], done, [ca, vv])
        first = self.first_two([(self.w8(A[n][0], 0), 128, 128, S) for n in ("w_ffn_gate", "w_ffn_up")],
                               lambda: self.scaled(1, vec(V_GFFN), hi, lo, done), hi, lo)
        self.norm_close()
        h = self.acts(hi, lo, self.both())
        groups = [2, 4, 4, 4, 4, 4]
        base = 0
        pend = None
        for gi, gn in enumerate(groups):
            tiles = []
            for i in range(gn):
                f = base + i
                if f == 0:
                    (pg, tg), (pu, tu) = first
                else:
                    u = self.unit(self.w8(A["w_ffn_gate"][0], 128 * f))
                    pg, tg = self.gemm(u, 8, 128, h)
                    u = self.unit(self.w8(A["w_ffn_up"][0], 128 * f))
                    pu, tu = self.gemm(u, 8, 128, h)
                tiles.append(self.glu(pg, tg, pu, tu))
                if i == 0 and pend is not None:
                    self.down(pend, A["w_ffn_down"][0], X, xtok)
            pend = (base * 128, tiles)
            base += gn
        while self.ada_n < 64:
            self.ada_step()
        self.ada_n = None
        for i, (sc, gv) in enumerate(((8, V_NORM), (32, V_NORM + 8), (56, V_KVG))):
            gst_ = Q.op("dve", lambda e, i=i, sc=sc, gv=gv: e.scalar_tensor_tensor(
                out=self.gs[:, 8 * i:8 * i + 8], in0=self.mod[:, sc:sc + 8], scalar=1.0,
                in1=self.vec[:, gv:gv + 8], op0=ALU.add, op1=ALU.mult), self.adat)
        self.modtok = [self.adat, gst_]
        last = Q.last("pe")
        gs = lambda i: (lambda j: self.gs[:, 8 * i + j:8 * i + j + 1])
        md = lambda c: (lambda j: self.mod[:, c + j:c + j + 1])
        t = Q.op("dve", lambda e: e.tensor_tensor(self.g12[:, :], self.gs[:, 0:8], self.vec[:, V_GFIN:V_GFIN + 8],
                                                  ALU.mult), gst_)
        g12 = lambda j: self.g12[:, j:j + 1]

        self.norm_open(X, vec(V_GFIN))
        normed = [None, None]

        def middle():
            self.rstd(0)
            self.scaled(0, g12, hi, lo, last, shift=md(0))

        def scale_first(j):
            normed[0] = (normed[0] or []) + self.times_norm(0, vec(V_GFIN), (j, j + 1))

        self.down(pend, A["w_ffn_down"][0], X, xtok, middle={1: lambda: self.sums(0), 2: middle,
                                                                 **{4 + i: (lambda i=i: scale_first(2 * i)) for i in range(4)}})
        done = Q.last("pe")
        Wi = A["a_w_in_2"][0]

        def second():
            self.scaled(1, g12, hi, lo, last, shift=md(0))
            normed[1] = self.times_norm(1, vec(V_GFIN))

        first = self.first_two([(self.w8(Wi, 128 * i), 128, 128, S) for i in range(2)], second, hi, lo)
        self.norm_close()
        h = self.acts(hi, lo, self.both())
        for j in range(8):
            xtok[j] = [normed[0][j], normed[1][j]]

        self.G = Ring([Slot((self.main(f"gh{i}", gtile[i], FR), self.main(f"gl{i}", gtile[6 + i], FR)), f"g{i}")
                       for i in range(6)])
        for s in self.G.slots:
            s.free = done
        pend = None
        for g in range(4):
            pt = []
            for i in range(4):
                if g == 0 and i < 2:
                    ps, t = first[i]
                else:
                    u = self.unit(self.w8(Wi, 512 * g + 128 * i))
                    ps, t = self.gemm(u, 8, 128, h)
                pt.append(self.pooled(ps, t, g))
                if i == 0 and pend is not None:
                    self.down(pend, A["a_w_out_2"][0], X, xtok, gate=md(16))
            pacts = [(s.t[0], s.t[1], t, t) for s, t in pt]
            tiles = []

            def gated(i, py, ty, pz, tz):
                s = self.tmp.take()
                a = Q.op("act", lambda e: e.activation(s.t[:, :], pz.t[:, :], ACT.Silu), tz, s.free)
                pz.free = [a]
                sc = vec(V_SCALE)(4 * g + i)
                a = Q.op("dve", lambda e: e.scalar_tensor_tensor(
                    out=s.t[:, :], in0=py.t[:, :], scalar=sc, in1=s.t[:, :], op0=ALU.mult, op1=ALU.mult), a, ty)
                py.free = [a]
                gslot = self.G.take()
                t = self.split(s.t[:, :], gslot.t[0][:, :], gslot.t[1][:, :], a, free=gslot.free)
                s.free = t
                tiles.append((gslot, t))

            ys, zs = {}, {}
            for i in ("z0", "y0", "z1", "y2", "z2", "z3"):
                k = int(i[1])
                if i[0] == "z":
                    u = self.unit(self.w8(Wi, 2048 + 512 * g + 128 * k))
                    zs[k] = self.gemm(u, 8, 128, h)
                else:
                    u = self.unit(self.w8(A["a_w_group_2"][0, g], 128 * k, 256, nk=4))
                    for m in (k, k + 1):
                        ys[m] = self.gemm(u, 4, 256, pacts, col0=128 * (m - k))
                    if k == 2:
                        for s, _ in pt:
                            s.free = [ys[3][1]]
                for m in sorted(ys):
                    if m in zs:
                        gated(m, *ys.pop(m), *zs.pop(m))
            pend = (512 * g, tiles)
        last = Q.last("pe")
        self.norm_open(X)

        def middle():
            self.rstd(0)
            self.scaled(0, gs(2), hi, lo, last, shift=md(48))

        def second():
            k0_done = Q.last("pe")
            self.scaled(1, gs(2), hi, lo, last, shift=md(48))
            self.keys_tok = [list(x) for x in self.htok]
            self.scaled(0, gs(1), hi, lo, k0_done, shift=md(24))

        self.down(pend, A["a_w_out_2"][0], X, xtok, gate=md(16), middle={1: lambda: self.sums(0), 2: middle})

        kx0, kx1, vt_ = self.main("kx0", 4), self.main("kx1", 33), self.main("vt", 34)
        pooled_done = Q.last("pe")
        (ps, t), (psv, tv2) = self.first_two(
            [(self.w8(A["w_kv_2"], 128 * i), 128, 128, S) for i in range(2)], second, hi, lo)
        t1 = Q.op("act", lambda e, ps=ps: e.activation(kx0[0:64, :], ps.t[0:64, :], ACT.Copy), t, pooled_done)
        t1 = Q.op("act", lambda e, ps=ps: e.activation(kx1[64:128, :], ps.t[64:128, :], ACT.Copy), t, pooled_done)
        ps.free = [t1]
        t1k = t1
        k0t = Q.load(kx0[64:128, :], kx0[0:64, :], "kx0", t1)
        k1t = Q.load(kx1[0:64, :], kx1[64:128, :], "kx1", t1)
        vtt = Q.op("act", lambda e: e.activation(vt_[:, :], psv.t[:, :], ACT.Copy), tv2, pooled_done)
        psv.free = [vtt]
        kv_done = Q.last("pe")
        q01 = self.first_two([(self.w8(A["b_w_in_2"][0], 128 * i), 128, 128, S) for i in range(2)],
                             lambda: self.scaled(1, gs(1), hi, lo, kv_done, shift=md(24)), hi, lo, False)
        self.norm_close()
        htok = self.both()
        h = self.acts(hi, lo, htok)
        xs = self.dram("xs", [S, S])
        xst = [Q.load(xs[j * 128:j * 128 + 128, :], X[j][:, :], f"xs{j}", xtok[j]) for j in range(8)]
        qd = self.dram("qd", [2048, S])
        qdt = []
        KP = [self.main(f"k2p{i}", 8 + i, FR) for i in range(4)]
        VP = [self.main(f"v2p{i}", 12 + i, FR) for i in range(4)]
        T2 = [self.main(f"t2{i}", 2 * i, cols=2048) for i in range(2)]
        pads = {}

        def key_pads(kv, after):
            kx, kxt = ((kx0, [k0t, t1k]), (kx1, [k1t, t1k]))[kv]
            out = []
            for half, (H, Lw) in ((0, (KP[0], KP[1])), (64, (KP[2], KP[3]))):
                sl = slice(half, half + 64)
                out += self.split(kx[sl, :], H[sl, :], Lw[sl, :], kxt, after, eng="dve")
            pads["k"] = out

        def tables(kv):
            t = self.table_flip(T2[kv], tl[kv])
            T2v = T2[kv][:, :].rearrange("p (h c) -> p h c", h=8)
            t = Q.op("pool", lambda e: e.affine_select(
                out=T2v, in_=T2v, compare_op=ALU.is_ge, fill=NEG, base=128,
                pattern=[[0, 8], [-1, 256]], channel_multiplier=1), t)
            pads["t", kv] = Q.op("pool", lambda e: e.affine_select(
                out=T2v, in_=T2v, compare_op=ALU.is_gt, fill=NEG, base=0,
                pattern=[[0, 8], [1, 256]], channel_multiplier=-1), t)

        for j in range(16):
            if j == 3:
                tl = [self.table_load(T2[kv], gd, 8 + 8 * kv, f"t2{kv}", [gst, pooled_done]) for kv in range(2)]
            if j in (6, 8):
                tables(j // 2 - 3)
            if j == 14:
                q0 = self.tmp.take()
                q0t = Q.load(q0.t[:, :], qd[0:128, :], "ld_" + q0.name, q0.free, qdt[0])
            if j == 10:
                zz = self.zero_pads([(KP[0], 64), (KP[1], 64), (KP[2], 0), (KP[3], 0)], xst)
                zv = self.zero_v([(VP[0], 64), (VP[1], 64), (VP[2], 0), (VP[3], 0)], xst)
                key_pads(0, [zz, xst])
            if j == 12:
                pads["v"] = self.v_pads(vt_, VP, 0, 128, vtt, [zv, xst])
            if j < 2:
                ps, t = q01[j]
            else:
                u = self.unit(self.w8(A["b_w_in_2"][0], 128 * j))
                ps, t = self.gemm(u, 8, 128, h)
            s = self.tmp.take()
            if j < 8:
                t = Q.op("act", lambda e, ps=ps, s=s: e.activation(s.t[:, :], ps.t[:, :], ACT.Copy, scale=0.125), t, s.free)
            else:
                t = Q.op("act", lambda e, ps=ps, s=s: e.activation(s.t[:, :], ps.t[:, :], ACT.Silu), t, s.free)
            ps.free = [t]
            qdt.append(Q.load(qd[j * 128:j * 128 + 128, :], s.t[:, :], "st_" + s.name, t))
            s.free = [qdt[-1]]
        qz_done = [Q.last("pe", "dve", "act"), xst, htok]
        ptb = [(self.main(f"p2h{i}", 16 + i, FR), self.main(f"p2l{i}", 18 + i, FR)) for i in range(2)]
        ptf = [qz_done, qz_done]
        qb = [(self.main(f"q2h{i}", (5, 20)[i], FR), self.main(f"q2l{i}", (6, 21)[i], FR)) for i in range(2)]
        qf = [pooled_done, qz_done]
        otile = [24, 25, 26, 27, 28, 29, 30, 4, 31, 32, 35, 22, 23, 7, 33, 34]
        oh = [self.main(f"o2h{j}", otile[j], FR) for j in range(8)]
        ol = [self.main(f"o2l{j}", otile[8 + j], FR) for j in range(8)]
        ott = [[] for _ in range(8)]
        items = [(j, hb, odd) for j in range(8) for hb in range(2) for odd in range(2)]
        st, heads = {}, {}

        zs = Slot(self.at("zs", 51, 512), "zs")
        zs.free = [kv_done, gst, Q.last("dve")]

        def zload(m):
            heads["z"] = (zs, Q.load(zs.t[:, :], qd[1024 + m // 2 * 128:1152 + m // 2 * 128, m % 2 * 512:m % 2 * 512 + 512],
                                     "zs", zs.free, qdt[8 + m // 2]))

        def fetch(n):
            j, hb, odd = items[n]
            if hb or odd:
                return
            if j == 0:
                heads["q"] = (q0, q0t)
                zload(0)
            else:
                s = self.tmp.take()
                heads["q"] = (s, Q.load(s.t[:, :], qd[j * 128:j * 128 + 128, :], "ld_" + s.name, s.free, qdt[j]))

        def begin(n):
            j, hb, odd = items[n]
            if hb or odd:
                return
            s, t = heads["q"]
            QH, QL = qb[j % 2]
            qt = self.split(s.t[:, :], QH[:, :], QL[:, :], t, free=qf[j % 2], eng="dve")
            s.free = qt
            heads[j] = (QH, QL, qt)

        def score(n):
            j, hb, odd = items[n]
            QH, QL, qt = heads[j]
            kpt = pads["k"]
            K = (KP[2], KP[3]) if odd else (KP[0], KP[1])
            ps = self.ps.take()
            for i in range(4):
                blk = 4 * hb + i
                c = slice(blk * 128, blk * 128 + 128)
                lo_ = max(blk - 1, 0)
                k_ = slice(lo_ * 128, blk * 128 + 128)
                o = i * 256 + (128 if blk == 0 else 0)
                t = self.prods(ps.t[:, o:i * 256 + 256], (QH[:, c], QL[:, c]),
                               (K[0][:, k_], K[1][:, k_]), True, True, [qt, kpt, ps.free])
            st[n] = (ps, t)
            if hb and odd:
                qf[j % 2] = [t]

        def top(n):
            j, hb, odd = items[n]
            ps, t = st[n]
            hl = (2 * j + odd) % 8
            L = self.att.take()
            c = (n % 4) * 32
            mm, nm, sm, es, rd = (self.st[:, c + 4 * i:c + 4 * i + 4] for i in range(5))
            sk = self.sk[:, 2 * j + odd:2 * j + odd + 1]
            zt = Q.op("pool", lambda e: e.memset(L.t[:, 0:128], 0.0), L.free) if hb == 0 else None
            for i in range(4):
                o = i * 256 + (128 if hb == 0 and i == 0 else 0)
                e_ = i * 256 + 256
                tt = Q.op("dve", lambda e: e.tensor_tensor_reduce(
                    L.t[:, o:e_], ps.t[:, o:e_], T2[j // 4][:, hl * 256 + o - i * 256:hl * 256 + 256], 1.0, sk,
                    ALU.add, ALU.max, mm[:, i:i + 1]), t, L.free, pads["t", j // 4])
            ps.free = [tt]
            t = Q.op("dve", lambda e: e.tensor_scalar(nm, mm, -1.0, None, ALU.mult), tt)
            st[n] = (L, t, zt, nm, sm, es, rd)

        def exps(n):
            j, hb, odd = items[n]
            L, t, zt, nm, sm, es, rd = st[n]
            sk = self.sk[:, 2 * j + odd:2 * j + odd + 1]
            for i in range(4):
                o = i * 256 + (128 if hb == 0 and i == 0 else 0)
                e_ = i * 256 + 256
                t2 = Q.op("act", lambda e: e.activation(L.t[:, o:e_], L.t[:, o:e_], ACT.Exp,
                                                        bias=nm[:, i:i + 1], accum_out=sm[:, i:i + 1]), t)
            t = Q.op("act", lambda e: e.activation(es, nm, ACT.Exp, bias=sk), t)
            st[n] = (L, [t2, t, zt], sm, es, rd)

        def norm(n):
            L, t, sm, es, rd = st[n]
            t = Q.op("dve", lambda e: e.tensor_tensor(sm, sm, es, ALU.add), t)
            t = Q.op("dve", lambda e: e.reciprocal(rd, sm), t)
            L3 = L.t[:, :].rearrange("p (b c) -> p b c", b=4)
            t = Q.op("pool", lambda e: e.tensor_tensor(
                L3, L3, rd.unsqueeze(2).to_broadcast([128, 4, 256]), ALU.mult), t)
            st[n] = (L, t)

        def turn(n):
            L, t = st[n]
            ps = self.ps.take()
            for i in range(8):
                m = Q.op("pe", lambda e: e.transpose(
                    ps.t[:, i * 128:i * 128 + 128], L.t[:, i * 128:i * 128 + 128], self.ident[:, :]), t, ps.free)
            L.free = [m]
            st[n] = (ps, m)

        def turned(n):
            odd = items[n][2]
            ps, t = st[n]
            PH, PL = ptb[odd]
            a = Q.op("act", lambda e: e.activation(PH[:, :], ps.t[:, :], ACT.Copy), t, ptf[odd])
            st[n] = (ps, PH, PL, a)

        def turned_low(n):
            ps, PH, PL, a = st[n]
            d = Q.op("dve", lambda e: e.tensor_tensor(PL[:, :], ps.t[:, :], PH[:, :].bitcast(F32), ALU.subtract),
                     a, ptf[items[n][2]])
            ps.free = [d]
            st[n] = (PH, PL, [a, d])

        def values(n):
            j, hb, odd = items[n]
            if not odd:
                st["po"] = self.po.take()
            po = st["po"]
            vpt = pads["v"]
            V = (VP[2], VP[3]) if odd else (VP[0], VP[1])
            PH, PL, pt = st[n]
            ks = (0, 2, 1, 3, -1) if hb else (0, 2, 1, 3)
            for k in ks:
                c0, c1 = max(k, 0) * 128, min(k + 2, 4) * 128
                p0 = k * 256 + 128 if k >= 0 else 0
                sv = slice((4 * hb + k) * 128, (4 * hb + k + 1) * 128)
                pc = slice(p0, p0 + c1 - c0)
                t = self.prods(po.t[:, c0:c1], (V[0][:, sv], V[1][:, sv]), (PH[:, pc], PL[:, pc]),
                               odd == 0 and k == 0, odd == 1 and k == ks[-1], [pt, po.free, vpt])
            ptf[odd] = [t]
            st[n] = (po, t)

        def stored(n):
            j, hb, odd = items[n]
            if not odd:
                return
            po, t = st[n]
            hs = slice(hb * 512, hb * 512 + 512)
            z, zt = heads["z"]
            t = Q.op("dve", lambda e: e.tensor_tensor(z.t[:, :], z.t[:, :], po.t[:, 0:512], ALU.mult), t, zt)
            po.free = [t]
            free = [qz_done, pads["k"], pads["v"]]
            heads["zh"] = Q.op("act", lambda e: e.activation(oh[j][:, hs], z.t[:, :], ACT.Copy), t, free)

        def stored_low(n):
            j, hb, odd = items[n]
            if not odd:
                return
            z, zt = heads["z"]
            hs = slice(hb * 512, hb * 512 + 512)
            t = [heads["zh"], Q.op("dve", lambda e: e.tensor_tensor(
                ol[j][:, hs], z.t[:, :], oh[j][:, hs].bitcast(F32), ALU.subtract), heads["zh"],
                qz_done, pads["k"], pads["v"])]
            ott[j] += t
            z.free = t
            if n < 31:
                zload(n // 2 + 1)

        self.att = Ring([x for x in self.tmp.slots if x is not q0])
        self.tmp = Ring([q0])
        self.part_psum()
        def other_keys(n):
            if n == 16:
                key_pads(1, Q.last("pe"))

        def other_values(n):
            if n == 16:
                pads["v"] = self.v_pads(vt_, VP, 64, 128, vtt, Q.last("pe"))

        def score_first(n):
            if n != 16:
                score(n)

        def score_last(n):
            if n == 16:
                score(n)

        self.pipeline(32, [(4, other_values), (0, other_keys), (0, score_first), (3, turn), (4, values), (0, score_last), (2, norm), (0, top), (3, turned), (5, stored), (3, turned_low),
                           (5, stored_low), (-2, begin), (-5, fetch), (0, exps)])
        self.tmp = Ring(self.att.slots + self.tmp.slots)
        self.join_psum()
        att_done = Q.last("pe", "dve", "act", "pool")
        X = [self.main(f"Y{j}", 16 + j if j < 6 else j - 6) for j in range(NT)]
        outs = Ring([Slot(self.main(f"os{i}", 8 + i), f"os{i}") for i in range(4)])
        for s in outs.slots:
            s.free = att_done
        xtok = [[Q.load(X[j][:, :], xs[j * 128:j * 128 + 128, :], f"xs{j}", att_done, xst[j])] for j in range(8)]
        self.norm_open(X)

        def product(j, hf):
            u = self.unit(self.w8(A["b_w_out_2"][0], 128 * j))
            return self.gemm(u, 8, 128, self.acts(oh, ol, ott), half=hf)

        def update(j, c, p, t, xt):
            return Q.op("dve", lambda e: e.scalar_tensor_tensor(
                out=X[j][:, c], in0=p, scalar=md(40)(j), in1=X[j][:, c], op0=ALU.mult, op1=ALU.add), t, xt)

        G = self.main("gfull", 12)
        gft = Q.load(G[:, :], A["final_g_2"].rearrange("(a n) -> a n", a=1).to_broadcast([128, S]), "gfull", att_done)
        rs, stages = {}, {}

        def total(hf):
            rs[hf] = self.sums(hf, False)

        def turn_out(i):
            ps = self.ps.take()
            for j in range(NT):
                t = Q.op("pe", lambda e: e.transpose(
                    ps.t[:, j * 128:j * 128 + 128], X[j][:, i * 128:i * 128 + 128], self.ident[:, :]),
                    self.summed[i // 4][j], ps.free)
            stages[i] = (ps, t)

        def store(i):
            ps, t = stages[i]
            s = outs.take()
            r, rt = rs[i // 4]
            r1 = r[:, i % 4:i % 4 + 1]
            if i % 4 == 1:
                t = Q.op("act", lambda e: e.activation(s.t[:, :], ps.t[:, :], ACT.Copy, scale=r1), t, rt, s.free)
                ps.free = [t]
                t = Q.op("pool", lambda e: e.tensor_tensor(s.t[:, :], s.t[:, :], G[:, :], ALU.mult), t, gft)
            else:
                t = Q.op("dve", lambda e: e.scalar_tensor_tensor(
                    out=s.t[:, :], in0=ps.t[:, :], scalar=r1, in1=G[:, :], op0=ALU.mult, op1=ALU.mult),
                    t, rt, s.free, gft)
                ps.free = [t]
            s.free = [Q.load(self.out[0, i * 128:(i + 1) * 128, :], s.t[:, :], "st_" + s.name, t)]

        def out_tile(i):
            turn_out(i)
            store(i)

        self.by_halves(product, update, xtok, {1: lambda: total(0), 2: lambda: out_tile(0), 3: lambda: out_tile(1),
                                               4: lambda: out_tile(2), 5: lambda: out_tile(3)})
        for i in (4, 5, 6):
            turn_out(i)
        total(1)
        for i in (4, 5, 6):
            store(i)
        out_tile(7)

    def part_psum(self):
        self.whole, s = self.ps, self.ps.take()
        self.kept = s
        self.ps = Ring([x for x in self.whole.slots if x is not s])
        self.po = Ring([Slot(s.t[:, 0:512], "po0"), Slot(s.t[:, 512:1024], "po1")])
        for x in self.po.slots:
            x.free = list(s.free)

    def join_psum(self):
        self.kept.free = self.po.slots[0].free + self.po.slots[1].free
        self.ps = self.whole

    def pipeline(self, n, stages, n0=0):
        for s in range(min(lag for lag, _ in stages), n + max(lag for lag, _ in stages)):
            for lag, f in stages:
                if 0 <= s - lag < n:
                    f(n0 + s - lag)

    def transposed(self, xn, X, h, hooks={}):
        c = slice(h * 512, h * 512 + 512)
        for j in range(NT):
            ps = self.ps.take()
            for i in range(4 * h, 4 * h + 4):
                t = self.Q.op("pe", lambda e: e.transpose(
                    ps.t[:, i * 128:i * 128 + 128], xn[i][0][:, j * 128:j * 128 + 128], self.ident[:, :]),
                    xn[i][1], ps.free, self.ctok)
            if j % 2:
                a = self.Q.op("act", lambda e: e.activation(X[j][:, c], ps.t[:, c], ACT.Copy), t)
            else:
                a = self.Q.op("dve", lambda e: e.tensor_copy(X[j][:, c], ps.t[:, c]), t)
            ps.free = [a]
            self.copied[j].append(a)
            self.square(j, h, a)
            if j in hooks:
                hooks[j]()

    def zero_pads(self, pads, after):
        return [self.Q.op("dve", lambda e, p=p, h=h: e.memset(p[h:h + 64, :].bitcast(F32), 0.0), after)
                for p, h in pads]

    def zero_v(self, pads, after):
        return [self.Q.op("pool", lambda e, p=p, h=h: e.memset(
            p[:, :].rearrange("p (i c) -> p i c", c=128)[:, :, h:h + 64].bitcast(F32), 0.0), after)
            for p, h in pads]

    def k_pads(self, kt, kt2, pads, after, sem, free):
        KE, LE, KO, LO = pads
        d = self.Q.load(kt2[64:128, :], kt[0:64, :], sem, after)
        a = self.split(kt[0:64, :], KE[0:64, :], LE[0:64, :], after, free=free, eng="dve")
        b = self.split(kt2[64:128, :], KO[64:128, :], LO[64:128, :], d, after, free=free, eng="dve")
        return [a, b]

    def v_pads(self, src, pads, row, n, after, free):
        VE, VLE, VO, VLO = pads
        ps = self.ps.take()
        for i in range(NT):
            t = self.Q.op("pe", lambda e, i=i, ps=ps: e.transpose(
                ps.t[:, i * 128:i * 128 + 128], src[:, i * 128:i * 128 + 128], self.ident[:, :]), after, ps.free)
        v = ps.t[:, :].rearrange("p (i c) -> p i c", c=128)[:, :, row:row + 64]
        out = []
        for H, L, c in ((VE, VLE, 0), (VO, VLO, 64)):
            h = H[:, :].rearrange("p (i c) -> p i c", c=128)[:, :, c:c + 64]
            l = L[:, :].rearrange("p (i c) -> p i c", c=128)[:, :, c:c + 64]
            t = self.Q.op("act", lambda e, h=h: e.activation(h, v, ACT.Copy), t, free)
            t = self.Q.op("dve", lambda e, h=h, l=l: e.tensor_tensor(l, v, h.bitcast(F32), ALU.subtract), t)
            out.append(t)
        ps.free = [t]
        return out

    def table_load(self, Tt, gd, h0, sem, after):
        src = bass.AP(gd.tensor, gd.offset + h0 * 384, [[1, 128], [384, 8], [1, 256]])
        return self.Q.load(Tt[:, :].rearrange("p (h c) -> p h c", h=8), src, sem, after)

    def table_flip(self, Tt, t):
        Q = self.Q
        toks = []
        for i in range(2):
            ps = self.ps.take()
            for h in range(2):
                c = i * 1024 + h * 512
                m = Q.op("pe", lambda e, ps=ps, h=h, c=c: e.matmul(
                    ps.t[:, h * 512:h * 512 + 512], self.flip[:, :], Tt[:, c:c + 512], start=True, stop=True), t, ps.free)
            a = Q.op("act", lambda e, ps=ps, i=i: e.activation(
                Tt[:, i * 1024:i * 1024 + 1024], ps.t[:, :], ACT.Copy), m)
            ps.free = [a]
            toks.append(a)
        return toks

    def logits(self, q, K, b, Wd, after):
        ps = self.ps.take()
        c = slice(b * 128, b * 128 + 128)
        for s0 in range(0, Wd, 512):
            s1 = min(s0 + 512, Wd)
            t = self.prods(ps.t[:, s0:s1], (q[0][:, c], q[1][:, c]), (K[0][:, s0:s1], K[1][:, s0:s1]),
                           True, True, [after, ps.free])
        ps.free = []
        return ps, t

    def glu(self, pg, tg, pu, tu):
        Q = self.Q
        s = self.tmp.take()
        a = Q.op("act", lambda e: e.activation(s.t[:, :], pg.t[:, :], ACT.Silu), tg, s.free)
        pg.free = [a]
        a = Q.op("dve", lambda e: e.tensor_tensor(s.t[:, :], s.t[:, :], pu.t[:, :], ALU.mult), a, tu)
        pu.free = [a]
        g = self.G.take()
        t = self.split(s.t[:, :], g.t[0][:, :], g.t[1][:, :], a, free=g.free)
        s.free = t
        return g, t

    def pooled(self, ps, t, g):
        Q, w = self.Q, 2 << g
        u, a, b = self.tmp.take(), self.tmp.take(), self.tmp.take()
        tu = Q.op("act", lambda e: e.activation(u.t[:, :], ps.t[:, :], ACT.Copy), t, u.free)
        ps.free = [tu]
        src, t = u, tu
        k = 1
        while k < w:
            dst = a if src is not a else b
            t1 = Q.op("dve", lambda e, s=src, d=dst, k=k: e.tensor_tensor(
                d.t[:, k:S], s.t[:, k:S], s.t[:, 0:S - k], ALU.add), t, dst.free)
            t2 = Q.op("dve", lambda e, s=src, d=dst, k=k: e.tensor_copy(d.t[:, 0:k], s.t[:, 0:k]), t, dst.free)
            dst.free = []
            t, src, k = [t1, t2], dst, 2 * k
        inv = self.invc[:, 16 * g:16 * g + 16]
        t = Q.op("dve", lambda e, s=src: e.tensor_tensor(s.t[:, 0:16], s.t[:, 0:16], inv, ALU.mult), t)
        t = Q.op("dve", lambda e, s=src: e.scalar_tensor_tensor(
            out=u.t[:, :], in0=s.t[:, :], scalar=1.0 / w, in1=u.t[:, :], op0=ALU.mult, op1=ALU.subtract), t)
        gs = self.G.take()
        t2 = self.split(u.t[:, :], gs.t[0][:, :], gs.t[1][:, :], t, free=gs.free)
        u.free, a.free, b.free = t2, [t], [t]
        return gs, t2

    def down(self, pend, W, X, xtok, gate=None, middle=None):
        r0, tiles = pend
        nk = len(tiles)
        n = 1024 // nk
        acts = [(g.t[0], g.t[1], t, t) for g, t in tiles]
        held = []

        def product(j, half):
            if (128 * j) % n == 0:
                held.append(self.unit(self.w8(W, 128 * j, n, k0=r0, nk=nk)))
            return self.gemm(held[-1], nk, n, acts, col0=(128 * j) % n, half=half)

        def update(j, c, p, t, xt):
            if gate is None:
                return self.Q.op("dve", lambda e: e.tensor_tensor(X[j][:, c], X[j][:, c], p, ALU.add), t, xt)
            return self.Q.op("dve", lambda e: e.scalar_tensor_tensor(
                out=X[j][:, c], in0=p, scalar=gate(j), in1=X[j][:, c], op0=ALU.mult, op1=ALU.add),
                t, xt, self.modtok)

        if middle is not None:
            self.by_halves(product, update, xtok, middle)
        else:
            for j in range(8):
                ps, t = product(j, None)
                ps.free = [update(j, slice(0, S), ps.t[:, :], t, xtok[j])]
                xtok[j] = list(ps.free)
        for g, _ in tiles:
            g.free = self.Q.last("pe")


def program(nc, A, out, consts):
    mem = {}
    draft = Net(nc, A, out, consts, None, mem)
    draft.build()
    net = Net(nc, A, out, consts, draft.units, mem)
    net.build()
    with ExitStack() as ctx:
        net.Q.emit(nc, ctx)


def constants():
    dist = np.maximum(255 - np.arange(384), 0)
    large = 16 + (np.log(np.maximum(dist, 1).astype(np.float32) / np.float32(16)) / np.float32(np.log(8.0))
                  * np.float32(16)).astype(np.int32)
    bucket = np.where(dist < 16, dist, np.minimum(large, 31))
    oneh = (np.arange(32)[:, None] == bucket[None, :]).astype(np.float32)
    t = np.arange(16)
    invc = np.stack([w / np.minimum(t + 1, w) for w in (2, 4, 8, 16)]).astype(np.float32).reshape(1, 64)
    return {"ident": np.eye(128, dtype=np.float32), "flip": np.eye(128, dtype=np.float32)[::-1].copy(), "oneh": oneh, "invc": invc}


_INS = ["x", "g_mix", "w_in", "b_gate", "conv_w", "w_branch_a", "w_branch_b", "w_out", "rel_bias", "g_ffn",
        "w_ffn_gate", "w_ffn_up", "w_ffn_down", "g_final", "c_2", "norm_g_2", "ada_w_2", "ada_b_2", "a_w_in_2",
        "a_w_group_2", "a_scale_2", "a_w_out_2", "kv_norm_g_2", "kv_ada_w_2", "kv_ada_b_2", "w_kv_2", "b_w_in_2",
        "b_sinks_2", "b_w_out_2", "rel_bias_2", "final_g_2"]


def kernel(**inputs):
    import concourse.bacc as _bacc
    from concourse.bass_utils import run_bass_kernel_spmd as _run

    nc = _bacc.Bacc("TRN2", target_bir_lowering=False, num_devices=1)
    arrays, A, C = {}, {}, {}
    for name in _INS:
        a = np.ascontiguousarray(inputs[name])
        arrays[f"in_{name}"] = a
        A[name] = nc.dram_tensor(f"in_{name}", a.shape, F32, kind="ExternalInput").ap()
    for name, a in constants().items():
        arrays[f"c_{name}"] = a
        C[name] = nc.dram_tensor(f"c_{name}", a.shape, F32, kind="ExternalInput").ap()
    out = nc.dram_tensor("out_0", (1, S, 1024), F32, kind="ExternalOutput").ap()
    program(nc, A, out, C)
    r = _run(nc, [arrays], core_ids=[0])
    return r.results[0]["out_0"]
```
